# Optimizing a Trainium2 kernel written in Bass

```python
import math
import jax, jax.numpy as jnp
from jax import lax
import numpy as np

D_MODEL = 1024
BATCH = 1
SEQ = 256
DEPTH = 1

EPS = 1e-6
GDN_HEADS = 4
GDN_DK = 128
GDN_DV = 128
CONV_K = 4
CHUNK = 64
SWA_HEADS = 8
SWA_DH = 64
DILATED_BRANCHES = ((128, 1), (512, 4), (2048, 16))
SWA_BLOCK = 128
REL_BUCKETS = 32
REL_MAX_DIST = 2048
N_EXPERTS = 32
TOP_K = 4
D_FF = D_MODEL
SWIGLU_LIMIT = 7.0
SWIGLU_ALPHA = 1.702
MOE_BLOCK = 256
IN_WIDTHS = (GDN_HEADS * GDN_DK, GDN_HEADS * GDN_DK, GDN_HEADS * GDN_DV, GDN_HEADS * GDN_DV,
             GDN_HEADS, GDN_HEADS, SWA_HEADS * SWA_DH, SWA_HEADS * SWA_DH, SWA_HEADS * SWA_DH)
IN_DIM = sum(IN_WIDTHS)
CONV_DIM = 2 * GDN_HEADS * GDN_DK + GDN_HEADS * GDN_DV
MIX_WIDTH = GDN_HEADS * GDN_DV + SWA_HEADS * SWA_DH

kernel_name = 'hymba_gdn_dilated_swa_moe'

def _rmsnorm(x, w):
    xf = x.astype(jnp.float32)
    y = xf * lax.rsqrt(jnp.mean(xf * xf, axis=-1, keepdims=True) + EPS) * w.astype(jnp.float32)
    return y.astype(x.dtype)

def _l2norm(x):
    return x * lax.rsqrt(jnp.sum(x * x, axis=-1, keepdims=True) + EPS)

def _split_columns(z):
    offsets, acc = [], 0
    for w in IN_WIDTHS[:-1]:
        acc += w
        offsets.append(acc)
    return jnp.split(z, offsets, axis=-1)

def _causal_dwconv(x, w):
    c = x.shape[-1]
    return lax.conv_general_dilated(x, w.astype(x.dtype)[:, None, :], window_strides=(1,),
                                    padding=[(CONV_K - 1, 0)],
                                    dimension_numbers=('NWC', 'WIO', 'NWC'),
                                    feature_group_count=c)

def _gated_deltanet(q, k, v, beta, g):
    b, s, h, dk = q.shape
    dv = v.shape[-1]
    n = s // CHUNK

    def chunks(t):
        return t.reshape(b, n, CHUNK, h, -1).transpose(0, 3, 1, 2, 4)

    q, k, v = chunks(q), chunks(k), chunks(v)
    beta = beta.reshape(b, n, CHUNK, h).transpose(0, 3, 1, 2)
    g = g.reshape(b, n, CHUNK, h).transpose(0, 3, 1, 2)
    gc = jnp.cumsum(g, axis=-1)
    ii = np.arange(CHUNK)[:, None]
    jj = np.arange(CHUNK)[None, :]
    decay = jnp.exp(jnp.where(ii >= jj, gc[..., :, None] - gc[..., None, :], -jnp.inf))
    kb = k * beta[..., None]
    a_kk = jnp.where(ii > jj, jnp.einsum('bhnik,bhnjk->bhnij', kb, k) * decay, 0.0)
    m = a_kk + jnp.eye(CHUNK, dtype=a_kk.dtype)
    rhs = jnp.concatenate([v * beta[..., None], kb * jnp.exp(gc)[..., None]], axis=-1)
    sol = lax.linalg.triangular_solve(m, rhs, left_side=True, lower=True, unit_diagonal=True)
    u, w = sol[..., :dv], sol[..., dv:]
    a_qk = jnp.einsum('bhnik,bhnjk->bhnij', q, k) * decay
    q_dec = q * jnp.exp(gc)[..., None]
    k_dec = k * jnp.exp(gc[..., -1:] - gc)[..., None]
    chunk_decay = jnp.exp(gc[..., -1])

    def step(state, xs):
        u_n, w_n, qd_n, kd_n, a_n, cd_n = xs
        v_new = u_n - jnp.einsum('bhck,bhkv->bhcv', w_n, state)
        o_n = jnp.einsum('bhck,bhkv->bhcv', qd_n, state) + jnp.einsum('bhij,bhjv->bhiv', a_n, v_new)
        state = state * cd_n[..., None, None] + jnp.einsum('bhck,bhcv->bhkv', kd_n, v_new)
        return state, o_n

    xs = tuple(jnp.moveaxis(t, 2, 0) for t in (u, w, q_dec, k_dec, a_qk, chunk_decay))
    state0 = jnp.zeros((b, h, dk, dv), jnp.float32)
    _, o = lax.scan(step, state0, xs)
    return o.transpose(1, 0, 3, 2, 4).reshape(b, s, h, dv)

def _t5_bucket(dist):
    max_exact = REL_BUCKETS // 2
    n = np.maximum(dist, 0)
    large = max_exact + (np.log(np.maximum(n, 1) / max_exact) / math.log(REL_MAX_DIST / max_exact)
                         * (REL_BUCKETS - max_exact)).astype(np.int32)
    large = np.minimum(large, REL_BUCKETS - 1)
    return np.where(n < max_exact, n, large).astype(np.int32)

def _dilated_branch(q, k, v, rel_bias, window, dilation):
    b, s, h, dh = q.shape
    length = s // dilation
    nb = -(-length // SWA_BLOCK)
    lp = nb * SWA_BLOCK

    def split(t):
        t = t.reshape(b, length, dilation, h, dh).transpose(0, 2, 1, 3, 4).reshape(b * dilation, length, h, dh)
        return jnp.pad(t, ((0, 0), (0, lp - length), (0, 0), (0, 0)))

    def band(t):
        tb = t.reshape(-1, nb, SWA_BLOCK, h, dh)
        prev = jnp.pad(tb, ((0, 0), (1, 0), (0, 0), (0, 0), (0, 0)))[:, :-1]
        return jnp.concatenate([prev, tb], axis=2)

    qb = split(q).reshape(-1, nb, SWA_BLOCK, h, dh)
    kb, vb = band(split(k)), band(split(v))
    qi = np.arange(SWA_BLOCK)[:, None]
    kj = np.arange(2 * SWA_BLOCK)[None, :]
    steps = qi + SWA_BLOCK - kj
    valid_local = (steps >= 0) & (steps <= window // dilation)
    valid = np.where((np.arange(nb) == 0)[:, None, None], valid_local & (kj >= SWA_BLOCK), valid_local)
    bias = rel_bias.astype(jnp.float32)[jnp.asarray(_t5_bucket(steps * dilation))].transpose(2, 0, 1)
    scores = jnp.einsum('bnqhe,bnkhe->bhnqk', qb, kb) + bias[:, None]
    scores = jnp.where(valid[None, None], scores, -jnp.inf)
    mx = jnp.max(scores, axis=-1, keepdims=True)
    p = jnp.exp(scores - mx)
    den = jnp.sum(p, axis=-1)
    o = jnp.einsum('bhnqk,bnkhe->bnqhe', p, vb) / den.transpose(0, 2, 3, 1)[..., None]
    lse = (mx[..., 0] + jnp.log(den)).transpose(0, 2, 3, 1)
    o = o.reshape(b, dilation, lp, h, dh)[:, :, :length].transpose(0, 2, 1, 3, 4).reshape(b, s, h, dh)
    lse = lse.reshape(b, dilation, lp, h)[:, :, :length].transpose(0, 2, 1, 3).reshape(b, s, h)
    return o, lse

def _dilated_attention(q, k, v, rel_bias):
    outs, lses = [], []
    for window, dilation in DILATED_BRANCHES:
        o, lse = _dilated_branch(q, k, v, rel_bias, window, dilation)
        outs.append(o)
        lses.append(lse)
    wts = jax.nn.softmax(jnp.stack(lses), axis=0)
    return jnp.sum(wts[..., None] * jnp.stack(outs), axis=0)

def _moe(hn, w_router, b_router, w_gu, b_gu, w_dn, b_dn):
    b, s, d = hn.shape
    t = b * s
    hf = hn.reshape(t, d)
    logits = hf.astype(jnp.float32) @ w_router.astype(jnp.float32) + b_router.astype(jnp.float32)
    top_v, top_e = lax.top_k(logits, TOP_K)
    gates = jax.nn.softmax(top_v, axis=-1)
    e_flat = top_e.reshape(-1)
    tok_flat = jnp.repeat(jnp.arange(t, dtype=jnp.int32), TOP_K)
    g_flat = gates.reshape(-1)
    order = jnp.argsort(e_flat)
    e_s, tok_s, g_s = e_flat[order], tok_flat[order], g_flat[order]
    counts = jnp.bincount(e_flat, length=N_EXPERTS)
    padded = (counts + MOE_BLOCK - 1) // MOE_BLOCK * MOE_BLOCK
    raw_start = jnp.cumsum(counts) - counts
    pad_end = jnp.cumsum(padded)
    pad_start = pad_end - padded
    dest = pad_start[e_s] + jnp.arange(t * TOP_K, dtype=jnp.int32) - raw_start[e_s]
    p_rows = t * TOP_K + N_EXPERTS * MOE_BLOCK
    nblk = p_rows // MOE_BLOCK
    buf_tok = jnp.full((p_rows,), t, jnp.int32).at[dest].set(tok_s)
    buf_gate = jnp.zeros((p_rows,), jnp.float32).at[dest].set(g_s)
    blk_start = jnp.arange(nblk, dtype=jnp.int32) * MOE_BLOCK
    blk_expert = jnp.minimum(jnp.sum(blk_start[:, None] >= pad_end[None, :], axis=1), N_EXPERTS - 1)
    h_pad = jnp.concatenate([hf, jnp.zeros((1, d), hf.dtype)], axis=0)
    xb = h_pad[buf_tok].reshape(nblk, MOE_BLOCK, d)

    def expert_block(args):
        xblk, e = args
        gu = xblk @ w_gu[e] + b_gu[e]
        gate = jnp.minimum(gu[:, :D_FF], SWIGLU_LIMIT)
        up = jnp.clip(gu[:, D_FF:], -SWIGLU_LIMIT, SWIGLU_LIMIT)
        act = (up + 1.0) * gate * jax.nn.sigmoid(SWIGLU_ALPHA * gate)
        return act @ w_dn[e] + b_dn[e]

    yb = lax.map(expert_block, (xb, blk_expert)).reshape(p_rows, d)
    out = jnp.zeros((t + 1, d), jnp.float32).at[buf_tok].add(yb.astype(jnp.float32) * buf_gate[:, None])
    return out[:t].reshape(b, s, d).astype(hn.dtype)

def _layer(x, norm1_w, w_in, conv_w, a_log, dt_bias, gdn_norm_w, q_norm_w, k_norm_w, rel_bias,
           w_out, norm2_w, w_router, b_router, w_gate_up, b_gate_up, w_down, b_down):
    b, s, _ = x.shape
    f32 = jnp.float32
    z = _rmsnorm(x, norm1_w) @ w_in
    qa, ka, va, gate_a, beta_l, alpha_l, qb, kb, vb = _split_columns(z)
    qkv = jax.nn.silu(_causal_dwconv(jnp.concatenate([qa, ka, va], axis=-1), conv_w)).astype(f32)
    qa, ka, va = jnp.split(qkv, [GDN_HEADS * GDN_DK, 2 * GDN_HEADS * GDN_DK], axis=-1)
    qa = _l2norm(qa.reshape(b, s, GDN_HEADS, GDN_DK)) * (GDN_DK ** -0.5)
    ka = _l2norm(ka.reshape(b, s, GDN_HEADS, GDN_DK))
    va = va.reshape(b, s, GDN_HEADS, GDN_DV)
    beta = jax.nn.sigmoid(beta_l.astype(f32))
    g = -jnp.exp(a_log.astype(f32)) * jax.nn.softplus(alpha_l.astype(f32) + dt_bias.astype(f32))
    oa = _gated_deltanet(qa, ka, va, beta, g)
    oa = (oa * lax.rsqrt(jnp.mean(oa * oa, axis=-1, keepdims=True) + EPS) * gdn_norm_w.astype(f32)
          * jax.nn.silu(gate_a.astype(f32).reshape(b, s, GDN_HEADS, GDN_DV)))
    oa = oa.reshape(b, s, GDN_HEADS * GDN_DV)
    qb = _rmsnorm(qb.astype(f32).reshape(b, s, SWA_HEADS, SWA_DH), q_norm_w) * (SWA_DH ** -0.5)
    kb = _rmsnorm(kb.astype(f32).reshape(b, s, SWA_HEADS, SWA_DH), k_norm_w)
    vb = vb.astype(f32).reshape(b, s, SWA_HEADS, SWA_DH)
    ob = _dilated_attention(qb, kb, vb, rel_bias).reshape(b, s, SWA_HEADS * SWA_DH)
    h = x + jnp.concatenate([oa, ob], axis=-1).astype(x.dtype) @ w_out
    return h + _moe(_rmsnorm(h, norm2_w), w_router, b_router, w_gate_up, b_gate_up, w_down, b_down)

def setup_inputs(seed: int = 0) -> dict:
    key = jax.random.key(seed)
    ks = jax.random.split(key, 18)
    f32 = jnp.float32
    L = DEPTH
    nrm = jax.random.normal
    dt = jnp.exp(jax.random.uniform(ks[5], (L, GDN_HEADS), f32, math.log(1e-3), math.log(1e-1)))
    return {
        'x': nrm(ks[0], (BATCH, SEQ, D_MODEL), f32),
        'norm1_w': 1.0 + 0.05 * nrm(ks[1], (L, D_MODEL), f32),
        'w_in': nrm(ks[2], (L, D_MODEL, IN_DIM), f32) * D_MODEL ** -0.5,
        'conv_w': nrm(ks[3], (L, CONV_K, CONV_DIM), f32) * CONV_K ** -0.5,
        'a_log': jnp.log(jax.random.uniform(ks[4], (L, GDN_HEADS), f32, 1.0, 16.0)),
        'dt_bias': dt + jnp.log(-jnp.expm1(-dt)),
        'gdn_norm_w': 1.0 + 0.05 * nrm(ks[6], (L, GDN_DV), f32),
        'q_norm_w': 1.0 + 0.05 * nrm(ks[7], (L, SWA_DH), f32),
        'k_norm_w': 1.0 + 0.05 * nrm(ks[8], (L, SWA_DH), f32),
        'rel_bias': 0.5 * nrm(ks[9], (REL_BUCKETS, SWA_HEADS), f32),
        'w_out': nrm(ks[10], (L, MIX_WIDTH, D_MODEL), f32) * MIX_WIDTH ** -0.5,
        'norm2_w': 1.0 + 0.05 * nrm(ks[11], (L, D_MODEL), f32),
        'w_router': nrm(ks[12], (L, D_MODEL, N_EXPERTS), f32) * D_MODEL ** -0.5,
        'b_router': 0.01 * nrm(ks[13], (L, N_EXPERTS), f32),
        'w_gate_up': nrm(ks[14], (L, N_EXPERTS, D_MODEL, 2 * D_FF), f32) * D_MODEL ** -0.5,
        'b_gate_up': 0.01 * nrm(ks[15], (L, N_EXPERTS, 2 * D_FF), f32),
        'w_down': nrm(ks[16], (L, N_EXPERTS, D_FF, D_MODEL), f32) * D_FF ** -0.5,
        'b_down': 0.01 * nrm(ks[17], (L, N_EXPERTS, D_MODEL), f32),
    }

def reference(x, norm1_w, w_in, conv_w, a_log, dt_bias, gdn_norm_w, q_norm_w, k_norm_w, rel_bias,
              w_out, norm2_w, w_router, b_router, w_gate_up, b_gate_up, w_down, b_down):
    h = x
    for l in range(DEPTH):
        h = _layer(h, norm1_w[l], w_in[l], conv_w[l], a_log[l], dt_bias[l], gdn_norm_w[l],
                   q_norm_w[l], k_norm_w[l], rel_bias, w_out[l], norm2_w[l], w_router[l],
                   b_router[l], w_gate_up[l], b_gate_up[l], w_down[l], b_down[l])
    return h


_drawn_inputs = setup_inputs


def setup_inputs(seed=0):
    import zlib

    import numpy as np

    out = dict(_drawn_inputs(seed))
    spreads = {}
    factors = {'k_norm_w': 4.171, 'b_gate_up': 8.0, 'b_down': 8.0}
    for name, (base, spread) in spreads.items():
        noise = np.random.default_rng([zlib.crc32(name.encode()), seed]).standard_normal(out[name].shape)
        drawn = base * np.exp(spread * noise) if base else spread * noise
        out[name] = __import__('jax').numpy.asarray(drawn.astype(out[name].dtype))
    for name, factor in factors.items():
        out[name] = (out[name] * factor).astype(out[name].dtype)
    return out
```

```python
import math
from contextlib import ExitStack

import concourse.bass as bass
import numpy as np
from concourse import mybir

ALU = mybir.AluOpType
ACT = mybir.ActivationFunctionType
AX_X = mybir.AxisListType.X
F32 = mybir.dt.float32
I32 = mybir.dt.int32
U32 = mybir.dt.uint32

P = 128
EPS = 1e-6
HG, DK = 4, 128
HS, DH = 8, 64
CONV_K = 4
BRANCHES = ((128, 1), (512, 4), (2048, 16))
REL_BUCKETS, REL_MAX_DIST = 32, 2048
N_EXP, TOP_K = 32, 4
LIMIT, ALPHA = 7.0, 1.702
SLOTS = 64
MASKED = -1e30
ABSENT = 1024.0


def distance_table(seq):
    dist = seq - 1 - np.arange(seq + P)
    near = REL_BUCKETS // 2
    n = np.maximum(dist, 0)
    far = near + (np.log(np.maximum(n, 1) / near) / math.log(REL_MAX_DIST / near)
                  * (REL_BUCKETS - near)).astype(np.int32)
    bucket = np.where(n < near, n, np.minimum(far, REL_BUCKETS - 1))
    held = sum(((dist % dil == 0) & (dist <= window)).astype(np.int32) for window, dil in BRANCHES)
    held = np.where(dist < 0, 0, held)
    table = np.zeros((REL_BUCKETS + 1, seq + P), np.float32)
    table[bucket, np.arange(seq + P)] = 1.0
    table[REL_BUCKETS] = np.where(held > 0, np.log(np.maximum(held, 1)), MASKED)
    return table


def attention_order():
    order = []
    swa = [("swa", g, part) for g in range(6) for part in "STO"]
    swa = [swa[0]] + [x for g in range(6) for x in
                      ([("swa", g + 1, "S")] if g < 5 else []) + [("swa", g, "T"), ("swa", g, "O")]]
    gdn = [("gdn", t, s) for s in range(1, 9) for t in (0, 1) if (t, s) != (1, 8)]
    gdn += [("gdn", 0, s) for s in (9, 10, 11, 12)] + [("gdn", 1, "K"), ("gdn", 1, 8), ("gdn", 0, 13)]
    gdn += [("gdn", 1, s) for s in (9, 10, 11, 12, 13)]
    for i, x in enumerate(gdn):
        order.append(x)
        if i < len(swa):
            order.append(swa[i])
    return order + swa[len(gdn):]


ORDER = attention_order()
DVE_STAGES = {1, 2, 3, 4, 5, 6, 7, 8, 9, 10, 11, 12, 13, "K"}
ACT_STAGES = {3, 4, 5, 7, 8, 9, 12}
SHARED_BANK_STAGES = {2, 4, 5, 8, 9, "K"}


def stage_counts(stages):
    n, out = 0, {}
    for kind, t, s in ORDER:
        if kind == "gdn":
            n += s in stages
            out[t, s] = n
    return out


DVE_DONE, ACT_DONE = stage_counts(DVE_STAGES), stage_counts(ACT_STAGES)
GDN_SEQ = [(t, s) for kind, t, s in ORDER if kind == "gdn"]


class Tally:

    def __init__(self, eng, sem):
        self.eng, self.sem, self.n = eng, sem, 0

    def mark(self, ins):
        ins.then_inc(self.sem, 1)
        self.n += 1

    def step(self, ins):
        self.mark(ins)
        self.eng.wait_ge(self.sem, self.n)


def hybrid_layer(nc, x, norm1_w, w_in, conv_w, a_log, dt_bias, gdn_norm_w, q_norm_w, k_norm_w,
                 rel_bias, w_out, norm2_w, w_router, b_router, w_gate_up, b_gate_up, w_down,
                 b_down, dist_table, out):
    S, D = x.shape[1], x.shape[2]
    T = S // P
    KT = D // P
    C_GDN = 3 * HG * DK
    C_GATE, C_BA = C_GDN, C_GDN + HG * DK
    C_SWA = C_BA + 2 * HG
    MAXB = N_EXP + (S * TOP_K - N_EXP) // SLOTS + 1
    assert T == 2 and D == 1024 and w_in.shape[2] == C_SWA + 3 * HS * DH
    NB_MAX = MAXB - 1
    TW = S + P

    with ExitStack() as ctx:
        def sb(name, shape, dt=F32):
            return ctx.enter_context(nc.sbuf_tensor(name, shape, dt))

        def sem(name):
            return ctx.enter_context(nc.semaphore(name))

        ring = sb("ring", [P, 12, 2048])
        hx = sb("hx", [P, T, D])
        arena1 = sb("arena1", [P, T, D])
        arena2 = sb("arena2", [P, KT, S])
        nw = sb("nw", [P, D])
        zswa = sb("zswa", [P, 3 * T, 512])
        qkT = sb("qkT", [P, 2, HS // 2, S])
        zpad = sb("zpad", [P, 12, S + 4])
        conv = sb("conv", [P, 12, S])
        gate = sb("gate", [P, T, HG * DK])
        bias = sb("bias", [P, HS, S])
        sc = sb("sc", [P, 2, 512])
        pt = sb("pt", [P, 2, 512])
        mats = sb("mats", [P, 6, 512])
        ident = sb("ident", [P, P])
        ones = sb("ones", [P, P])
        ucum = sb("ucum", [P, P])
        ustr = sb("ustr", [P, P])
        m_in = sb("m_in", [P, P])
        m_out = sb("m_out", [P, P])
        slot2 = sb("slot2", [P, 2, SLOTS])
        iota_e = sb("iota_e", [P, N_EXP])
        iota_b = sb("iota_b", [N_EXP, MAXB])
        col = sb("col", [P, 64])
        ba = sb("ba", [P, T, 2 * HG])
        gd = sb("gd", [P, 12, T, HG])
        wba = sb("wba", [P, KT, 2 * HG])
        cw = sb("cw", [P, CONV_K, 12])
        nrm = sb("nrm", [P, 8, 32])
        rel = sb("rel", [REL_BUCKETS + 1, HS])
        nbl = sb("nbl", [1, 64], I32)

        xn, hn = arena1, arena1
        xnT, mixT, hnT = arena2, arena2, arena2
        ug = arena1[:, 0, :].rearrange("p (t n) -> p t n", t=T)
        a1m = arena1[:].rearrange("p t d -> p (t d)").rearrange("p (m n) -> p m n", n=512)
        zpm = zpad[:].rearrange("p c s -> p (c s)")[:, 0:6 * 512].rearrange("p (m n) -> p m n", n=512)
        MAT = [dict(N=mats[:, 3 * t + 0], L=mats[:, 3 * t + 1], A=mats[:, 3 * t + 2],
                    D=zpm[:, 3 * t + 0], E=zpm[:, 3 * t + 1], F=zpm[:, 3 * t + 2],
                    G=a1m[:, 2 * t], H=a1m[:, 2 * t + 1], I=zswa[:, t], V=zswa[:, 2 + t])
               for t in range(T)]
        cw_rows = mats[0:CONV_K * 12, 5, 0:P]
        fdist = pt[0:HS, 0, 0:TW]
        dtab = pt[0:REL_BUCKETS + 1, 1, 0:TW]
        wout = ring[:, 8:12, :].rearrange("p s (j n) -> p (s j) n", n=D)
        bgu = bias[0:N_EXP].rearrange("p h s -> p (h s)")
        bdn = gate[0:N_EXP].rearrange("p t d -> p (t d)")
        wr = sc[:, 0, 0:KT * N_EXP].rearrange("p (k e) -> p k e", e=N_EXP)
        cv = conv[:].rearrange("p c s -> p (c s)").rearrange("p (m n) -> p m n", n=512)
        xg, xgT, gt, up, sg, actT = (cv[:, m] for m in range(6))
        qk = qkT[:].rearrange("p a b s -> p (a b s)").rearrange("p (m n) -> p m n", n=512)
        yb = qk[:, 0]
        SGT = qk[:, 1, 0:S]
        SEL = qk[:, 1, S:S + T * SLOTS].rearrange("p (t s) -> p t s", t=T)
        oh_cur = qk[0:N_EXP, 1, S + T * SLOTS:S + T * SLOTS + SLOTS]
        SG = qk[:, 2, 0:T * 2 * SLOTS].rearrange("p (t s) -> p t s", t=T)
        RM = qk[:, 2, 256:256 + T * MAXB].rearrange("p (t b) -> p t b", t=T)
        GB = qk[:, 2, 256 + T * MAXB:256 + 2 * T * MAXB].rearrange("p (t b) -> p t b", t=T)
        r3 = qk[:, 3]

        bank = [ctx.enter_context(nc.psum_tensor(f"bank{i}", [P, 512], F32)) for i in range(8)]
        swa_s = [bank[5], bank[6]]

        fd_dram = nc.dram_tensor("bias_by_distance", [HS, P, TW], F32, kind="Internal").ap()

        ld_x, ld_nw, ld_ba, ld_small, ld_rel = (sem(n) for n in ("ld_x", "ld_nw", "ld_ba", "ld_small", "ld_rel"))
        ld_win = [sem(f"ld_win{i}") for i in range(4)]
        ld_wout, ld_nw2, ld_moe = sem("ld_wout"), sem("ld_nw2"), sem("ld_moe")
        ld_slot = [sem(f"ld_slot{i}") for i in range(12)]
        st_dist, ld_bias, st_out = sem("st_dist"), sem("ld_bias"), sem("st_out")
        consts = sem("consts")
        dve_step, act_step, pool_step = sem("dve_step"), sem("act_step"), sem("pool_step")
        x_sq, xn_ready, xT_psum, xnT_ready = sem("x_sq"), sem("xn_ready"), sem("xT_psum"), sem("xnT_ready")
        dist_psum, dist_ready, cw_psum, cw_ready = (sem(n) for n in ("dist_psum", "dist_ready", "cw_psum", "cw_ready"))
        z_psum, z_evac = sem("z_psum"), sem("z_evac")
        dec_dve, dec_act, g_ready, ug_ready = sem("dec_dve"), sem("dec_act"), sem("g_ready"), sem("ug_ready")
        gc_psum, gcrow_psum, gap_ready, e_ready, emask_ready = (
            sem(n) for n in ("gc_psum", "gcrow_psum", "gap_ready", "e_ready", "emask_ready"))
        swa_sq, swa_ss, swa_root, swa_normed = sem("swa_sq"), sem("swa_ss"), sem("swa_root"), sem("swa_normed")
        qkT_psum, qkT_ready = sem("qkT_psum"), sem("qkT_ready")
        pad_ready, conv_ready, silu_ready, gsilu = sem("pad_ready"), sem("conv_ready"), sem("silu_ready"), sem("gsilu")
        l2_sq, l2_psum, l2_root, l2_done = sem("l2_sq"), sem("l2_psum"), sem("l2_root"), sem("l2_done")
        gdn_psum, gdn_dve, gdn_act, gdn_o, gdn_ss, gdn_root = (
            sem(n) for n in ("gdn_psum", "gdn_dve", "gdn_act", "gdn_o", "gdn_ss", "gdn_root"))
        s_psum, s_max, p_exp, p_ready, pt_psum, pt_ready, o_psum, o_ready = (
            sem(n) for n in ("s_psum", "s_max", "p_exp", "p_ready", "pt_psum", "pt_ready", "o_psum", "o_ready"))
        h_psum, h_ready, h_sq, hn_ready, hT_psum, hnT_ready = (
            sem(n) for n in ("h_psum", "h_ready", "h_sq", "hn_ready", "hT_psum", "hnT_ready"))
        lgT_psum, lgT_ready, lg_psum, lg_max, lg_exp, mask_ready = (
            sem(n) for n in ("lgT_psum", "lgT_ready", "lg_psum", "lg_max", "lg_exp", "mask_ready"))
        cnt_psum, nb_ready, end_psum, rt_psum, rt_ready, tab_psum, tab_ready = (
            sem(n) for n in ("cnt_psum", "nb_ready", "end_psum", "rt_psum", "rt_ready", "tab_psum", "tab_ready"))
        wgu_used, wdn_used = sem("wgu_used"), sem("wdn_used")
        g_min, sig_ready, act_ready, actT_psum, actT_ready = (
            sem(n) for n in ("g_min", "sig_ready", "act_ready", "actT_psum", "actT_ready"))
        S_ready, SG_ready, oh_ready, SGT_psum, SGT_ready = (
            sem(n) for n in ("S_ready", "SG_ready", "oh_ready", "SGT_psum", "SGT_ready"))
        zeroed, xg_psum, xg_ready, xgT_psum, xgT_ready, y_ready, acc_done, out_ready = (
            sem(n) for n in ("zeroed", "xg_psum", "xg_ready", "xgT_psum", "xgT_ready", "y_ready", "acc_done", "out_ready"))

        block = ctx.enter_context(nc.Block())

        win = w_in[0].rearrange("(k p) n -> p k n", p=P)
        PIECES = [C_SWA, C_SWA + 512, C_SWA + 1024, C_GATE, 0, 512, 1024]

        def piece(j):
            s = 2 * (j % 4)
            return ring[:, s:s + 2, :].rearrange("p s (j n) -> p (s j) n", n=512)

        def heads(ap, h=HG):
            return ap.rearrange("p (h n) -> p h n", h=h)

        def wide(cols, n):
            return cols.unsqueeze(2).to_broadcast([cols.shape[0], cols.shape[1], n])

        def each_head(mask):
            return mask.unsqueeze(1).to_broadcast([P, HG, P])

        def expert_tile(e_ap, slot):
            if slot < 8:
                src = w_gate_up[0][e_ap, slot * P:(slot + 1) * P, :]
                return src.rearrange("a p n -> p (a n)")
            s = slot - 8
            src = w_down[0][e_ap, 2 * s * P:2 * (s + 1) * P, :]
            return src.rearrange("a (j p) n -> p (a j) n", p=P)

        def slot_dst(slot):
            if slot < 8:
                return ring[:, slot, :]
            return ring[:, slot, :].rearrange("p (j n) -> p j n", n=D)

        @block.sync
        def _(sp):
            sp.dma_start(hx[:], x[0].rearrange("(t p) d -> p t d", p=P)).then_inc(ld_x, 16)
            sp.dma_start(nw[:], norm1_w.to_broadcast([P, D])).then_inc(ld_nw, 16)
            sp.dma_start(wba[:], win[:, :, C_BA:C_BA + 2 * HG]).then_inc(ld_ba, 16)
            for j, c0 in enumerate(PIECES):
                if j >= 4:
                    sp.wait_ge(z_psum, 2 * (j - 4) + 3)
                sp.dma_start(piece(j), win[:, :, c0:c0 + 512]).then_inc(ld_win[j % 4], 16)
                if j == 3:
                    sp.dma_start(wout, w_out[0].rearrange("(k p) n -> p k n", p=P)).then_inc(ld_wout, 16)
            for s in (6, 7, 0, 1, 2, 3, 4, 5):
                j = 3 if s >= 6 else 4 + s // 2
                sp.wait_ge(z_psum, 2 * j + 3)
                sp.dma_start(slot_dst(s), expert_tile(slice(0, 1), s)).then_inc(ld_slot[s], 16)
            sp.wait_ge(xn_ready, T)
            sp.dma_start(nw[:], norm2_w.to_broadcast([P, D])).then_inc(ld_nw2, 16)
            sp.wait_ge(s_max, 6)
            sp.dma_start(bgu, b_gate_up[0]).then_inc(ld_moe, 16)
            sp.wait_ge(pt_psum, 6)
            sp.dma_start(wr, w_router[0].rearrange("(k p) e -> p k e", p=P)).then_inc(ld_moe, 16)
            sp.wait_ge(gdn_dve, DVE_DONE[1, 12])
            sp.dma_start(bdn, b_down[0]).then_inc(ld_moe, 16)
            sp.wait_ge(h_psum, 2 * T)
            for s in range(8, 12):
                sp.dma_start(slot_dst(s), expert_tile(slice(0, 1), s)).then_inc(ld_slot[s], 16)
            sp.wait_ge(tab_ready, 4)
            n_blocks = sp.value_load(nbl[0:1, MAXB:MAXB + 1], min_val=N_EXP, max_val=NB_MAX)
            with sp.Fori(1, n_blocks) as b:
                e = sp.value_load(nbl[0:1, bass.ds(b, 1)], min_val=0, max_val=N_EXP - 1)
                for s in range(12):
                    if s < 8:
                        sp.wait_ge(wgu_used, 8 * b + (s - 7))
                    else:
                        sp.wait_ge(wdn_used, 4 * b + (s - 11))
                    sp.dma_start(slot_dst(s), expert_tile(bass.ds(e, 1), s)).then_inc(ld_slot[s], 16)
            for t in range(T):
                sp.wait_ge(out_ready, t + 1)
                sp.dma_start(out[0, t * P:(t + 1) * P, :], hx[:, t, :]).then_inc(st_out, 16)
            sp.wait_ge(st_out, 16 * T)

        @block.gpsimd
        def _(pool):
            c = Tally(pool, consts)
            c.mark(pool.memset(ones[:], 1.0))
            c.mark(pool.memset(rel[:], 1.0))
            c.mark(pool.memset(ident[:], 0.0))
            c.mark(pool.memset(zpad[:], 0.0))
            c.mark(pool.iota(slot2[:], [[0, 2], [1, SLOTS]], base=0, channel_multiplier=0,
                             allow_small_or_imprecise_dtypes=True))
            c.mark(pool.iota(iota_e[:], [[1, N_EXP]], base=0, channel_multiplier=0,
                             allow_small_or_imprecise_dtypes=True))
            c.mark(pool.iota(iota_b[:], [[1, MAXB]], base=0, channel_multiplier=0,
                             allow_small_or_imprecise_dtypes=True))
            c.mark(pool.iota(col[:, 8:9], [[0, 1]], base=0, channel_multiplier=1,
                             allow_small_or_imprecise_dtypes=True))
            c.mark(pool.memset(m_out[:], -1.0))
            c.mark(pool.memset(col[:, 0:1], EPS))
            c.mark(pool.memset(col[:, 1:2], EPS * DK))
            c.step(pool.memset(col[:, 2:3], 1.0))
            c.mark(pool.affine_select(ident[:], ident[:], [[-1, P]], ALU.not_equal, 1.0, base=0,
                                      channel_multiplier=1))
            c.mark(pool.affine_select(ucum[:], ones[:], [[1, P]], ALU.is_ge, 0.0, base=0,
                                      channel_multiplier=-1))
            c.mark(pool.affine_select(ustr[:], ones[:], [[1, P]], ALU.is_gt, 0.0, base=0,
                                      channel_multiplier=-1))
            c.step(pool.affine_select(m_out[:], m_out[:], [[-1, P]], ALU.is_gt, 0.0, base=0,
                                      channel_multiplier=1))
            c.step(pool.affine_select(m_in[:].rearrange("p (b n) -> p b n", n=16),
                                      m_out[:].rearrange("p (b n) -> p b n", n=16),
                                      [[16, P // 16], [0, 16]], ALU.is_ge, 0.0, base=15,
                                      channel_multiplier=-1))
            c.step(pool.tensor_tensor(m_out[:], m_out[:], m_in[:], ALU.subtract))
            sq = Tally(pool, swa_sq)
            for u in range(2 * T):
                pool.wait_ge(z_evac, u + 2)
                if u >= 2:
                    pool.wait_ge(swa_ss, u - 1)
                sq.mark(pool.tensor_tensor(sc[:, u % 2], zswa[:, u], zswa[:, u], ALU.mult))
            em, st = Tally(pool, emask_ready), Tally(pool, pool_step)
            for t in range(T):
                m = MAT[t]
                pool.wait_ge(e_ready, 2 * t + 2)
                pool.wait_ge(dec_act, 3)
                st.step(pool.tensor_tensor(heads(m["L"]), heads(m["N"]), wide(gd[:, 2, t], P), ALU.mult))
                st.step(pool.tensor_tensor(heads(m["N"]), heads(m["L"]), each_head(m_in[:]), ALU.mult))
                st.step(pool.tensor_tensor(heads(m["L"]), heads(m["L"]), each_head(m_out[:]), ALU.mult))
                em.mark(pool.tensor_tensor(heads(m["A"]), heads(m["A"]), each_head(ucum[:]), ALU.mult))
            l2 = Tally(pool, l2_sq)
            for u in range(4):
                pool.wait_ge(silu_ready, u + 1)
                pool.wait_ge(swa_ss, 4)
                if u >= 2:
                    pool.wait_ge(l2_psum, u - 1)
                v = conv[:, 2 * u:2 * u + 2, :].rearrange("p c s -> p (c s)")
                l2.mark(pool.tensor_tensor(sc[:, u % 2], v, v, ALU.mult))

        @block.scalar
        def _(act):
            act.wait_ge(consts, 12)
            act.dma_start(rel[0:REL_BUCKETS, :], rel_bias).then_inc(ld_rel, 16)
            act.dma_start(dtab, dist_table).then_inc(ld_rel, 16)
            small = [(gd[:, 0, 0], a_log.to_broadcast([P, HG])),
                     (gd[:, 1, 0], dt_bias.to_broadcast([P, HG])),
                     (col[:, 16:17], gdn_norm_w.rearrange("a d -> d a")),
                     (col[0:DH, 17:18], q_norm_w.rearrange("a d -> d a")),
                     (col[DH:P, 17:18], q_norm_w.rearrange("a d -> d a")),
                     (col[0:DH, 18:19], k_norm_w.rearrange("a d -> d a")),
                     (col[DH:P, 18:19], k_norm_w.rearrange("a d -> d a")),
                     (col[0:N_EXP, 19:20], b_router.rearrange("a d -> d a"))]
            for dst, src in small:
                act.dma_start(dst, src).then_inc(ld_small, 16)
            act.dma_start(cw_rows, conv_w[0].rearrange("i (c p) -> (i c) p", p=P)).then_inc(ld_rel, 16)

            st = Tally(act, act_step)
            act.wait_ge(ld_x, 16)
            act.wait_ge(consts, 12)
            xs = Tally(act, x_sq)
            for t in range(T):
                st.step(act.activation(xn[:, t, :], hx[:, t, :], ACT.Square, accum_out=nrm[:, 0, t:t + 1]))
            xs.mark(act.activation(nrm[:, 1, 0:T], nrm[:, 0, 0:T], ACT.Sqrt, bias=col[:, 0:1], scale=1.0 / D))
            xt = Tally(act, xnT_ready)
            for i in range(2 * T):
                t, q = divmod(i, 2)
                act.wait_ge(xT_psum, i + 1)
                xt.mark(act.copy(xnT[:, 4 * q:4 * q + 4, t * P:(t + 1) * P], heads(bank[4 + i][:])))
            act.wait_ge(dist_ready, 1)
            act.dma_start(fd_dram, fdist.unsqueeze(1).to_broadcast([HS, P, TW])).then_inc(st_dist, 16)
            act.wait_ge(st_dist, 16)
            act.dma_start(bias[:], bass.AP(fd_dram.tensor, S - 1 - P, [[TW - 1, P], [P * TW, HS], [1, S]])
                          ).then_inc(ld_bias, 16)

            z = Tally(act, z_evac)

            def evac(u):
                act.wait_ge(z_psum, u + 1)
                src = bank[u % 4]
                if u == 0:
                    z.mark(act.copy(ba[:], src[:, 0:T * 8].rearrange("p (t n) -> p t n", t=T)))
                elif u <= 6:
                    z.mark(act.copy(zswa[:, u - 1], src[:]))
                elif u <= 8:
                    z.mark(act.copy(gate[:, u - 7], src[:]))
                else:
                    act.wait_ge(consts, 12)
                    z.mark(act.copy(zpad[:, 2 * (u - 9):2 * (u - 9) + 2, 3:3 + S],
                                    src[:].rearrange("p (c s) -> p c s", c=2)))

            si = Tally(act, silu_ready)

            def silu(u):
                act.wait_ge(conv_ready, u - 8)
                v = conv[:, 2 * (u - 9):2 * (u - 9) + 2, :]
                si.mark(act.activation(v, v, ACT.Silu))

            da = Tally(act, dec_act)
            evac(0)
            act.wait_ge(dec_dve, 1)
            act.wait_ge(ld_small, 16 * 8)
            st.step(act.activation(gd[:, 4], gd[:, 3], ACT.Abs))
            st.step(act.activation(gd[:, 4], gd[:, 4], ACT.Exp, scale=-1.0))
            da.mark(act.activation(gd[:, 0, 0], gd[:, 0, 0], ACT.Exp))
            da.mark(act.activation(gd[:, 4], gd[:, 4], ACT.Ln, bias=1.0))
            da.mark(act.activation(gd[:, 2], ba[:, :, 0:HG], ACT.Sigmoid))
            evac(1)
            evac(2)
            evac(3)
            act.wait_ge(gap_ready, 1)
            da.mark(act.activation(gd[:, 7], gd[:, 5], ACT.Exp))
            da.mark(act.activation(gd[:, 8], gd[:, 6], ACT.Exp))
            evac(4)
            er = Tally(act, e_ready)
            for t in range(T):
                act.wait_ge(gap_ready, 2 + t)
                er.mark(act.activation(MAT[t]["N"], MAT[t]["N"], ACT.Exp, scale=-1.0))
                er.mark(act.activation(MAT[t]["A"], MAT[t]["A"], ACT.Exp))
            evac(5)
            act.wait_ge(swa_ss, 4)
            Tally(act, swa_root).mark(act.activation(nrm[:, 3], nrm[:, 2], ACT.Sqrt, bias=col[:, 0:1],
                                                     scale=1.0 / DH))
            evac(6)
            evac(7)
            evac(8)
            gs = Tally(act, gsilu)
            act.wait_ge(z_evac, 9)
            gs.mark(act.activation(gate[:], gate[:], ACT.Silu))
            evac(9)
            evac(10)
            qt = Tally(act, qkT_ready)
            for u in range(2 * T):
                a, t = divmod(u, T)
                act.wait_ge(qkT_psum, u + 1)
                act.wait_ge(dec_dve, 2)
                qt.mark(act.activation(qkT[:, a, :, t * P:(t + 1) * P], heads(bank[4 + u][:]), ACT.Copy,
                                       scale=col[:, 17 + a:18 + a]))
            silu(9)
            evac(11)
            silu(10)
            evac(12)
            silu(11)
            evac(13)
            silu(12)
            lr = Tally(act, l2_root)
            for u in range(4):
                act.wait_ge(l2_psum, u + 1)
                if u >= 2:
                    act.wait_ge(l2_done, u - 1)
                q = u < 2
                lr.mark(act.activation(pt[:, u % 2], bank[4 + u][:], ACT.Sqrt,
                                       bias=col[:, 1:2] if q else col[:, 0:1], scale=float(DK) if q else 1.0))
                if u == 2:
                    evac(14)
            silu(13)
            silu(14)

            gdn, pe_, pr = Tally(act, gdn_act), Tally(act, p_exp), Tally(act, pt_ready)
            go, gr = Tally(act, gdn_o), Tally(act, gdn_root)
            n_psum = 0
            for kind, a, s in ORDER:
                if kind == "gdn":
                    n_psum += 1
                    if s not in ACT_STAGES:
                        continue
                    m, X, Z = MAT[a], bank[2 * a], bank[4]
                    act.wait_ge(gdn_psum, n_psum)
                    if s == 12:
                        act.wait_ge(gdn_ss, 2 * a + 1)
                        go.mark(act.activation(m["E"], m["D"], ACT.Square))
                        act.wait_ge(gdn_ss, 2 * a + 2)
                        gdn.mark(act.activation(nrm[:, 6, 4 * a:4 * a + 4], nrm[:, 5, 4 * a:4 * a + 4],
                                                ACT.Sqrt, bias=col[:, 0:1], scale=1.0 / DK))
                    else:
                        dst = {3: "E", 4: "N", 5: "E", 7: "N", 8: "E", 9: "N"}[s]
                        gdn.mark(act.copy(m[dst], X[:]))
                elif s == "S":
                    g = a
                    n = 2 if g < 4 else 4
                    act.wait_ge(s_max, g + 1)
                    for h in range(n):
                        w = 512 // n
                        pe_.mark(act.activation(sc[:, g % 2, h * w:(h + 1) * w], sc[:, g % 2, h * w:(h + 1) * w],
                                                ACT.Exp, bias=nrm[:, 4, 8 * (g % 2) + h:8 * (g % 2) + h + 1],
                                                accum_out=nrm[:, 4, 16 + 8 * (g % 2) + h:17 + 8 * (g % 2) + h]))
                elif s == "T":
                    act.wait_ge(pt_psum, a + 1)
                    if a == 0:
                        act.wait_ge(l2_done, 4)
                    if a >= 2:
                        act.wait_ge(o_psum, a - 1)
                    pr.mark(act.copy(pt[:, a % 2], bank[7][:]))

            for t in range(T):
                act.wait_ge(h_ready, 2 * t + 2)
                act.wait_ge(gdn_dve, DVE_DONE[1, 13])
                st.step(act.activation(xn[:, t, :], hx[:, t, :], ACT.Square, accum_out=nrm[:, 0, t:t + 1]))
            hs = Tally(act, h_sq)
            hs.mark(act.activation(nrm[:, 1, 0:T], nrm[:, 0, 0:T], ACT.Sqrt, bias=col[:, 0:1], scale=1.0 / D))
            ht = Tally(act, hnT_ready)
            for i in range(2 * T):
                t, q = divmod(i, 2)
                act.wait_ge(hT_psum, i + 1)
                ht.mark(act.copy(hnT[:, 4 * q:4 * q + 4, t * P:(t + 1) * P], heads(bank[4 + i][:])))
            le = Tally(act, lg_exp)
            for t in range(T):
                act.wait_ge(lg_max, t + 1)
                le.mark(act.activation(r3[:, 32 * t + 8:32 * t + 12], r3[:, 32 * t:32 * t + 4], ACT.Exp,
                                       bias=nrm[:, 7, t:t + 1], accum_out=nrm[:, 7, 2 + t:3 + t]))
            act.wait_ge(xg_psum, 1)
            xr, yr, sr, gr2 = Tally(act, xg_ready), Tally(act, y_ready), Tally(act, sig_ready), Tally(act, SGT_ready)
            xr.mark(act.copy(xg, bank[6][:]))
            act.wait_ge(zeroed, 2)
            yr.mark(act.copy(yb[:, 0:1], yb[:, 0:1]))
            act.wait_ge(tab_ready, 4)
            n_blocks = act.value_load(nbl[0:1, MAXB:MAXB + 1], min_val=N_EXP, max_val=NB_MAX)
            with act.Fori(0, n_blocks) as b:
                act.wait_ge(g_min, b + 1)
                act.activation(sg, gt, ACT.Sigmoid, scale=ALPHA).then_inc(sig_ready, 1)
                act.wait_ge(SGT_psum, b + 1)
                act.copy(SGT, bank[7][:, 0:S]).then_inc(SGT_ready, 1)
                act.wait_ge(xg_psum, b + 2)
                act.copy(xg, bank[6][:]).then_inc(xg_ready, 1)
                act.wait_ge(wdn_used, 4 * b + 4)
                act.copy(yb, bank[7][:]).then_inc(y_ready, 1)

        @block.vector
        def _(dve):
            st = Tally(dve, dve_step)
            dve.wait_ge(x_sq, 1)
            dve.wait_ge(ld_nw, 16)
            st.step(dve.reciprocal(nrm[:, 1, 2:4], nrm[:, 1, 0:2]))
            xr = Tally(dve, xn_ready)
            for t in range(T):
                xr.mark(dve.scalar_tensor_tensor(out=xn[:, t, :], in0=hx[:, t, :], scalar=nrm[:, 1, 2 + t:3 + t],
                                                 in1=nw[:], op0=ALU.mult, op1=ALU.mult))
            dve.wait_ge(dist_psum, 1)
            Tally(dve, dist_ready).mark(dve.tensor_copy(fdist, bank[3][0:HS, 0:TW]))
            dve.wait_ge(cw_psum, 1)
            cwr = Tally(dve, cw_ready)
            cwr.step(dve.tensor_copy(cw[:].rearrange("p i c -> p (i c)"), bank[0][:, 0:CONV_K * 12]))

            dd = Tally(dve, dec_dve)
            dve.wait_ge(z_evac, 1)
            dve.wait_ge(ld_small, 16 * 8)
            dd.step(dve.tensor_tensor(gd[:, 3], ba[:, :, HG:2 * HG],
                                      gd[:, 1, 0].unsqueeze(1).to_broadcast([P, T, HG]), ALU.add))
            dd.step(dve.tensor_scalar(col[:, 17:18], col[:, 17:18], DH ** -0.5, None, ALU.mult))
            st.step(dve.tensor_scalar(gd[:, 9], gd[:, 3], 0.0, None, ALU.max))
            dve.wait_ge(dec_act, 2)
            st.step(dve.tensor_tensor(gd[:, 9], gd[:, 9], gd[:, 4], ALU.add))
            gr = Tally(dve, g_ready)
            for t in range(T):
                gr.step(dve.scalar_tensor_tensor(out=gd[:, 9, t], in0=gd[:, 9, t], scalar=-1.0,
                                                 in1=gd[:, 0, 0], op0=ALU.mult, op1=ALU.mult))
            ur = Tally(dve, ug_ready)
            dve.wait_ge(xT_psum, 2 * T)
            dve.wait_ge(consts, 18)
            for t in range(T):
                for h in range(HG):
                    ur.mark(dve.tensor_scalar(ug[:, t, h * P:(h + 1) * P], ucum[:], gd[:, 9, t, h:h + 1], None,
                                              ALU.mult))
            gp = Tally(dve, gap_ready)
            dve.wait_ge(gc_psum, 1)
            st.step(dve.tensor_copy(gd[:, 5], bank[4][:, 0:8].rearrange("p (t h) -> p t h", t=T)))
            gp.mark(dve.tensor_tensor(gd[:, 6], bank[4][:, 8:16].rearrange("p (t h) -> p t h", t=T), gd[:, 5],
                                      ALU.subtract))
            for t in range(T):
                dve.wait_ge(gcrow_psum, t + 1)
                for h in range(HG):
                    row, mine = bank[5 + t][:, h * P:(h + 1) * P], gd[:, 5, t, h:h + 1]
                    dve.tensor_scalar(MAT[t]["N"][:, h * P:(h + 1) * P], row, mine, 0.0, ALU.subtract, ALU.max)
                    last = dve.tensor_scalar(MAT[t]["A"][:, h * P:(h + 1) * P], row, mine, 0.0,
                                             ALU.subtract, ALU.min)
                gp.mark(last)
            ss = Tally(dve, swa_ss)
            for u in range(2 * T):
                dve.wait_ge(swa_sq, u + 1)
                ss.mark(dve.reduce_sum(nrm[:, 2, 8 * u:8 * u + 8], heads(sc[:, u % 2], HS), AX_X))
            dve.wait_ge(swa_root, 1)
            st.step(dve.reciprocal(nrm[:, 3], nrm[:, 3]))
            sn = Tally(dve, swa_normed)
            for u in range(2 * T):
                sn.mark(dve.tensor_tensor(heads(zswa[:, u], HS), heads(zswa[:, u], HS),
                                          wide(nrm[:, 3, 8 * u:8 * u + 8], DH), ALU.mult))

            cr, l2 = Tally(dve, conv_ready), Tally(dve, l2_done)

            def convolve(u):
                dve.wait_ge(z_evac, u + 1)
                for c in (2 * (u - 9), 2 * (u - 9) + 1):
                    st.step(dve.tensor_scalar(conv[:, c, :], zpad[:, c, 0:S], cw[:, 0, c:c + 1], None, ALU.mult))
                    for i in range(1, CONV_K):
                        ins = dve.scalar_tensor_tensor(out=conv[:, c, :], in0=zpad[:, c, i:i + S],
                                                       scalar=cw[:, i, c:c + 1], in1=conv[:, c, :],
                                                       op0=ALU.mult, op1=ALU.add)
                        if i < CONV_K - 1 or c % 2 == 0:
                            st.step(ins)
                cr.mark(ins)

            def l2_scale(u):
                dve.wait_ge(l2_root, u + 1)
                st.step(dve.reciprocal(pt[:, u % 2], pt[:, u % 2]))
                v = conv[:, 2 * u:2 * u + 2, :].rearrange("p c s -> p (c s)")
                l2.mark(dve.tensor_tensor(v, v, pt[:, u % 2], ALU.mult))

            for u in range(9, 14):
                convolve(u)
            l2_scale(0)
            l2_scale(1)
            l2_scale(2)
            convolve(14)
            l2_scale(3)
            dve.wait_ge(dec_act, 5)
            st.step(dve.tensor_tensor(gd[:, 10], gd[:, 2], gd[:, 7], ALU.mult))

            gdn, gss = Tally(dve, gdn_dve), Tally(dve, gdn_ss)
            sm, pr, orr = Tally(dve, s_max), Tally(dve, p_ready), Tally(dve, o_ready)
            n_psum = n_exp = 0
            for kind, a, s in ORDER:
                if kind == "gdn":
                    t, m = a, MAT[a]
                    X, Y, Z = bank[2 * t], bank[2 * t + 1], bank[4]
                    n_psum += 1
                    if s not in DVE_STAGES:
                        continue
                    dve.wait_ge(gdn_psum, n_psum)
                    if s == 1:
                        dve.wait_ge(emask_ready, t + 1)
                        st.mark(dve.tensor_tensor(m["N"], X[:], m["N"], ALU.mult))
                        st.mark(dve.tensor_tensor(m["L"], X[:], m["L"], ALU.mult))
                        gdn.mark(dve.tensor_tensor(m["A"], Y[:], m["A"], ALU.mult))
                    elif s == 2:
                        st.step(dve.tensor_copy(m["D"], X[:]))
                        st.step(dve.tensor_tensor(heads(m["G"]), heads(m["D"]), each_head(ident[:]), ALU.add))
                        if t == 0:
                            st.step(dve.tensor_tensor(heads(m["I"]), heads(Y[:]), wide(gd[:, 8, t], P), ALU.mult))
                        gdn.mark(dve.tensor_tensor(heads(m["H"]), heads(Z[:]), wide(gd[:, 2, t], P), ALU.mult))
                    elif s == 3:
                        gdn.mark(dve.tensor_copy(m["F"], Y[:]))
                    elif s == 4:
                        st.step(dve.tensor_copy(m["D"], Y[:]))
                        gdn.mark(dve.tensor_tensor(m["G"], Z[:], m["G"], ALU.add))
                    elif s == 5:
                        gdn.mark(dve.tensor_tensor(m["G"], Z[:], m["G"], ALU.add))
                    elif s == 6:
                        gdn.mark(dve.tensor_tensor(m["G"], X[:], m["G"], ALU.add))
                    elif s == 7:
                        gdn.mark(dve.tensor_copy(m["D"], Y[:]))
                    elif s == "K":
                        st.step(dve.tensor_tensor(heads(m["I"]), heads(Y[:]), wide(gd[:, 10, t], P), ALU.mult))
                        gdn.mark(dve.tensor_tensor(m["H"], m["H"], m["I"], ALU.subtract))
                    elif s == 8:
                        st.step(dve.tensor_copy(m["F"], Y[:]))
                        gdn.mark(dve.tensor_copy(m["V"], Z[:]))
                    elif s == 9:
                        gdn.mark(dve.tensor_tensor(m["V"], Z[:], m["V"], ALU.add))
                    elif s == 10:
                        gdn.mark(dve.tensor_tensor(m["V"], X[:], m["V"], ALU.add))
                    elif s == 11:
                        gdn.mark(dve.tensor_tensor(m["V"], Y[:], m["V"], ALU.add))
                    elif s == 12:
                        if t == 0:
                            st.step(dve.tensor_copy(m["F"], Y[:]))
                            gss.mark(dve.tensor_copy(m["D"], X[:]))
                        else:
                            st.step(dve.tensor_tensor(heads(m["F"]), heads(Y[:]), wide(gd[:, 7, t], P), ALU.mult))
                            gss.mark(dve.tensor_tensor(m["D"], X[:], m["F"], ALU.add))
                        dve.wait_ge(gdn_o, t + 1)
                        gss.mark(dve.reduce_sum(nrm[:, 5, 4 * t:4 * t + 4], heads(m["E"]), AX_X))
                        dve.wait_ge(gdn_act, ACT_DONE[t, 12])
                        dve.wait_ge(gsilu, 1)
                        st.step(dve.reciprocal(nrm[:, 6, 4 * t:4 * t + 4], nrm[:, 6, 4 * t:4 * t + 4]))
                        st.step(dve.tensor_tensor(heads(m["D"]), heads(m["D"]), wide(nrm[:, 6, 4 * t:4 * t + 4], P),
                                                  ALU.mult))
                        gdn.mark(dve.tensor_tensor(m["D"], m["D"], gate[:, t], ALU.mult))
                    elif s == 13:
                        gdn.mark(dve.tensor_scalar(mixT[:, 0:HG, t * P:(t + 1) * P], heads(X[:]), col[:, 16:17],
                                                   None, ALU.mult))
                    continue
                g = a
                n = 2 if g < 4 else 4
                if s == "S":
                    dve.wait_ge(s_psum, g + 1)
                    dve.wait_ge(ld_bias, 16)
                    if g == 0:
                        dve.wait_ge(l2_psum, 4)
                    if g >= 2:
                        dve.wait_ge(pt_psum, g - 1)
                    for r in range(2):
                        if g < 4:
                            o_, i_ = sc[:, g % 2, r * S:(r + 1) * S], swa_s[r][:, 0:S]
                            b_ = bias[:, 2 * g + r, :]
                        else:
                            o_ = heads(sc[:, g % 2], 4)[:, r:4:2, :]
                            i_ = swa_s[r][:, 0:S].rearrange("p (h j) -> p h j", h=2)
                            b_ = bias[:, 4 * (g - 4) + r:4 * (g - 4) + 4:2, P:2 * P]
                        st.step(dve.tensor_tensor(o_, i_, b_, ALU.add))
                    c0 = 8 * (g % 2)
                    st.step(dve.reduce_max(nrm[:, 4, c0:c0 + n], heads(sc[:, g % 2], n), AX_X))
                    sm.mark(dve.tensor_scalar(nrm[:, 4, c0:c0 + n], nrm[:, 4, c0:c0 + n], -1.0, None, ALU.mult))
                elif s == "T":
                    n_exp += n
                    c0 = 16 + 8 * (g % 2)
                    dve.wait_ge(p_exp, n_exp)
                    st.step(dve.reciprocal(nrm[:, 4, c0:c0 + n], nrm[:, 4, c0:c0 + n]))
                    v = heads(sc[:, g % 2], n)
                    pr.mark(dve.tensor_tensor(v, v, wide(nrm[:, 4, c0:c0 + n], 512 // n), ALU.mult))
                else:
                    dve.wait_ge(o_psum, g + 1)
                    if g < 4:
                        orr.mark(dve.tensor_copy(mixT[:, HG + g, P:2 * P], bank[7][:, 0:P]))
                    else:
                        orr.mark(dve.tensor_copy(mixT[:, HG + 2 * (g - 4):HG + 2 * (g - 4) + 2, 0:P],
                                                 bank[7][:, 0:S].rearrange("p (q i) -> p q i", q=2)))

            hr = Tally(dve, h_ready)
            for i in range(2 * T):
                t, hf = divmod(i, 2)
                dve.wait_ge(h_psum, i + 1)
                v = hx[:, t, hf * 512:(hf + 1) * 512]
                hr.mark(dve.tensor_tensor(v, bank[i][:], v, ALU.add))
            dve.wait_ge(h_sq, 1)
            dve.wait_ge(ld_nw2, 16)
            st.step(dve.reciprocal(nrm[:, 1, 2:4], nrm[:, 1, 0:2]))
            hr = Tally(dve, hn_ready)
            for t in range(T):
                hr.mark(dve.scalar_tensor_tensor(out=hn[:, t, :], in0=hx[:, t, :], scalar=nrm[:, 1, 2 + t:3 + t],
                                                 in1=nw[:], op0=ALU.mult, op1=ALU.mult))
            lgT = r3[0:N_EXP, 64:64 + S]
            dve.wait_ge(lgT_psum, 1)
            Tally(dve, lgT_ready).mark(dve.tensor_scalar(lgT, bank[0][0:N_EXP, 0:S], col[0:N_EXP, 19:20], None,
                                                         ALU.add))
            lm, mr = Tally(dve, lg_max), Tally(dve, mask_ready)
            idx, idf = gd[:, 0:2, :, :], gd[:, 2:4, :, :]
            lg = [r3[:, 320 + 32 * t:352 + 32 * t] for t in range(T)]
            mask = [r3[:, 384 + 32 * t:416 + 32 * t] for t in range(T)]
            rm = [r3[:, 448 + 32 * t:480 + 32 * t] for t in range(T)]
            gates = [qk[:, 2, 32 * t:32 * t + 32] for t in range(T)]
            dve.wait_ge(lg_psum, 1)
            for t in range(T):
                st.step(dve.tensor_copy(lg[t], bank[1][:, 32 * t:32 * t + 32]))
                st.step(dve.max(r3[:, 32 * t:32 * t + 8], lg[t]))
                iu = gd[:, 4 + t].rearrange("p t h -> p (t h)").bitcast(U32)
                lm.mark(dve.tensor_scalar(nrm[:, 7, t:t + 1], r3[:, 32 * t:32 * t + 1], -1.0, None, ALU.mult))
                st.step(dve.max_index(iu, r3[:, 32 * t:32 * t + 8], lg[t]))
                st.step(dve.tensor_copy(gd[:, 6 + t].rearrange("p t h -> p (t h)"), iu))
            for t in range(T):
                fi = gd[:, 6 + t].rearrange("p t h -> p (t h)")
                dve.wait_ge(lg_exp, t + 1)
                st.step(dve.reciprocal(nrm[:, 7, 4 + t:5 + t], nrm[:, 7, 2 + t:3 + t]))
                st.step(dve.tensor_scalar(r3[:, 32 * t + 8:32 * t + 12], r3[:, 32 * t + 8:32 * t + 12],
                                          nrm[:, 7, 4 + t:5 + t], None, ALU.mult))
                st.mark(dve.tensor_scalar(mask[t], iota_e[:], fi[:, 0:1], None, ALU.is_equal))
                st.step(dve.tensor_scalar(gates[t], iota_e[:], fi[:, 0:1], r3[:, 32 * t + 8:32 * t + 9],
                                          ALU.is_equal, ALU.mult))
                for j in range(1, TOP_K):
                    st.mark(dve.scalar_tensor_tensor(out=mask[t], in0=iota_e[:], scalar=fi[:, j:j + 1],
                                                     in1=mask[t], op0=ALU.is_equal, op1=ALU.add))
                    st.step(dve.tensor_scalar(lg[t], iota_e[:], fi[:, j:j + 1],
                                              r3[:, 32 * t + 8 + j:32 * t + 9 + j], ALU.is_equal, ALU.mult))
                    st.step(dve.tensor_tensor(gates[t], gates[t], lg[t], ALU.add))
                mr.mark(dve.tensor_copy(lg[t], mask[t]))
            dve.wait_ge(cnt_psum, 1)
            for t in range(T):
                st.step(dve.tensor_scalar(rm[t], bank[2][:, 32 * t:32 * t + 32], ABSENT, None, ALU.add))
                st.step(dve.tensor_tensor(rm[t], rm[t], mask[t], ALU.mult))
                st.step(dve.tensor_scalar(rm[t], rm[t], -ABSENT, None, ALU.add))
            nb = Tally(dve, nb_ready)
            more = col[0:N_EXP, 24:25]
            cnt = bank[3][0:N_EXP, 0:1]
            st.step(dve.tensor_scalar(more, cnt, float(SLOTS), None, ALU.is_gt))
            for j in range(2, S // SLOTS):
                ins = dve.scalar_tensor_tensor(out=more, in0=cnt, scalar=float(j * SLOTS), in1=more,
                                               op0=ALU.is_gt, op1=ALU.add)
                (st.step if j < S // SLOTS - 1 else nb.mark)(ins)
            dve.wait_ge(rt_psum, 1)
            rmT, gT = qk[0:N_EXP, 0, 0:S], qk[0:N_EXP, 0, S:2 * S]
            st.mark(dve.tensor_copy(rmT, bank[4][0:N_EXP, 0:S]))
            rt = Tally(dve, rt_ready)
            rt.mark(dve.tensor_copy(gT, bank[5][0:N_EXP, 0:S]))
            dve.wait_ge(end_psum, 1)
            end, beg = col[0:N_EXP, 25:26], col[0:N_EXP, 26:27]
            oh = r3[0:N_EXP, 0:MAXB]
            ohr = r3[0:N_EXP, 64:64 + MAXB]
            tmp = r3[0:N_EXP, 128:128 + MAXB]
            st.step(dve.tensor_scalar(end, bank[3][0:N_EXP, 1:2], float(N_EXP), None, ALU.add))
            st.step(dve.tensor_tensor(beg, end, more, ALU.subtract))
            st.step(dve.tensor_scalar(oh, iota_b[:], beg, None, ALU.is_ge))
            st.step(dve.scalar_tensor_tensor(out=oh, in0=iota_b[:], scalar=end, in1=oh, op0=ALU.is_lt,
                                             op1=ALU.mult))
            st.step(dve.tensor_scalar(tmp, iota_b[:], beg, 1.0, ALU.subtract, ALU.add))
            st.step(dve.scalar_tensor_tensor(out=ohr, in0=tmp, scalar=-float(SLOTS), in1=oh, op0=ALU.mult,
                                             op1=ALU.mult))
            st.step(dve.tensor_scalar(tmp, iota_b[:], col[0:N_EXP, 8:9], None, ALU.is_equal))
            rt.mark(dve.tensor_tensor(oh, oh, tmp, ALU.add))
            dve.wait_ge(tab_psum, 1)
            tr = Tally(dve, tab_ready)
            tr.mark(dve.tensor_copy(nbl[0:1, 0:MAXB], bank[6][0:1, 0:MAXB]))
            tr.mark(dve.tensor_scalar(nbl[0:1, MAXB:MAXB + 1], bank[6][0:1, 64:65], float(N_EXP), None, ALU.add))
            tr.mark(dve.tensor_copy(RM, bank[7][:, 0:T * MAXB].rearrange("p (t b) -> p t b", t=T)))
            tr.mark(dve.tensor_copy(GB, bank[7][:, 128:128 + T * MAXB].rearrange("p (t b) -> p t b", t=T)))
            dve.wait_ge(tab_ready, 4)
            for t in range(T):
                ins = dve.tensor_scalar(SEL[:, t, :], slot2[:, 0, :], RM[:, t, 0:1], None, ALU.is_equal)
            ins.then_inc(S_ready, 1)
            dve.tensor_copy(oh_cur, oh[:, 0:1].to_broadcast([N_EXP, SLOTS])).then_inc(oh_ready, 1)
            dve.wait_ge(xgT_psum, 1)
            dve.tensor_copy(xgT, bank[6][:]).then_inc(xgT_ready, 1)
            dve.memset(yb, 0.0).then_inc(zeroed, 1)
            dve.memset(SGT, 0.0).then_inc(zeroed, 1)
            n_blocks = dve.value_load(nbl[0:1, MAXB:MAXB + 1], min_val=N_EXP, max_val=NB_MAX)
            with dve.Fori(0, n_blocks) as b:
                dve.wait_ge(xg_psum, b + 1)
                for t in range(T):
                    ins = dve.tensor_scalar(SEL[:, t, :], slot2[:, 0, :], RM[:, t, bass.ds(b + 1, 1)], None,
                                            ALU.is_equal)
                ins.then_inc(S_ready, 1)
                for t in range(T):
                    ins = dve.tensor_scalar(SG[:, t, :], slot2[:].rearrange("p a s -> p (a s)"),
                                            RM[:, t, bass.ds(b, 1)], GB[:, t, bass.ds(b, 1)],
                                            ALU.is_equal, ALU.mult)
                ins.then_inc(SG_ready, 1)
                dve.wait_ge(wgu_used, 8 * b + 8)
                dve.tensor_scalar(gt, bank[4][:], LIMIT, None, ALU.min).then_inc(g_min, 1)
                dve.tensor_scalar(up, bank[5][:], LIMIT, -LIMIT, ALU.min, ALU.max).then_inc(dve_step, 1)
                dve.wait_ge(dve_step, 2 * b + (st.n + 1))
                dve.wait_ge(g_min, b + 1)
                dve.scalar_tensor_tensor(out=up, in0=up, scalar=1.0, in1=gt, op0=ALU.add,
                                         op1=ALU.mult).then_inc(dve_step, 1)
                dve.tensor_copy(oh_cur, oh[:, bass.ds(b + 1, 1)].to_broadcast([N_EXP, SLOTS])
                                ).then_inc(oh_ready, 1)
                dve.wait_ge(dve_step, 2 * b + (st.n + 2))
                dve.wait_ge(sig_ready, b + 1)
                dve.tensor_tensor(up, up, sg, ALU.mult).then_inc(act_ready, 1)
                dve.wait_ge(actT_psum, b + 1)
                dve.tensor_copy(actT, bank[4][:]).then_inc(actT_ready, 1)
                dve.wait_ge(xgT_psum, b + 2)
                dve.tensor_copy(xgT, bank[6][:]).then_inc(xgT_ready, 1)
            dve.wait_ge(acc_done, n_blocks + 1)
            for t in range(T):
                for hf in range(2):
                    v = hx[:, t, hf * 512:(hf + 1) * 512]
                    ins = dve.tensor_tensor(v, bank[2 * t + hf][:], v, ALU.add)
                ins.then_inc(out_ready, 1)

        @block.tensor
        def _(pe):
            mm, tp = pe.matmul, pe.transpose
            pe.wait_ge(ld_rel, 48)
            Tally(pe, dist_psum).mark(mm(bank[3][0:HS, 0:TW], rel[:], dtab, start=True, stop=True))
            pe.wait_ge(consts, 18)
            Tally(pe, cw_psum).mark(tp(bank[0][:, 0:CONV_K * 12], cw_rows, ident[0:CONV_K * 12, 0:CONV_K * 12]))
            xt = Tally(pe, xT_psum)
            for i in range(2 * T):
                t, q = divmod(i, 2)
                pe.wait_ge(xn_ready, t + 1)
                for k in range(4):
                    ins = tp(bank[4 + i][:, k * P:(k + 1) * P], xn[:, t, (4 * q + k) * P:(4 * q + k + 1) * P],
                             ident[:])
                xt.mark(ins)

            z = Tally(pe, z_psum)

            def unit(u):
                dst = bank[u % 4]
                if u >= 4:
                    pe.wait_ge(z_evac, u - 3)
                if u == 3:
                    pe.wait_ge(dist_ready, 1)
                if u == 0:
                    pe.wait_ge(ld_ba, 16)
                    pe.wait_ge(cw_ready, 1)
                    for t in range(T):
                        for k in range(KT):
                            ins = mm(dst[:, 8 * t:8 * t + 8], xnT[:, k, t * P:(t + 1) * P], wba[:, k, :],
                                     start=k == 0, stop=k == KT - 1)
                    z.mark(ins)
                    return
                j, half = divmod(u - 1, 2)
                pe.wait_ge(ld_win[j % 4], 16 * (j // 4 + 1))
                w = piece(j)
                if j < 4:
                    for k in range(KT):
                        ins = mm(dst[:], xnT[:, k, half * P:(half + 1) * P], w[:, k, :],
                                 start=k == 0, stop=k == KT - 1)
                else:
                    for c in range(2):
                        c0 = (2 * half + c) * P
                        for k in range(KT):
                            ins = mm(dst[:, c * S:(c + 1) * S], w[:, k, c0:c0 + P], xnT[:, k, :],
                                     start=k == 0, stop=k == KT - 1)
                z.mark(ins)

            pe.wait_ge(xnT_ready, 2 * T)
            for u in range(4):
                unit(u)
            pe.wait_ge(g_ready, T)
            for t in range(T):
                mm(bank[4][:, 4 * t:4 * t + 4], ucum[:], gd[:, 9, t], start=True, stop=True)
                ins = mm(bank[4][:, 8 + 4 * t:12 + 4 * t], ones[:], gd[:, 9, t], start=True, stop=True)
            Tally(pe, gc_psum).mark(ins)
            unit(4)
            gr = Tally(pe, gcrow_psum)
            for t in range(T):
                pe.wait_ge(ug_ready, HG * (t + 1))
                gr.mark(mm(bank[5 + t][:], ones[:], ug[:, t, :], start=True, stop=True))
            for u in range(5, 10):
                unit(u)
            qt = Tally(pe, qkT_psum)
            for u in range(2 * T):
                pe.wait_ge(swa_normed, u + 1)
                if u == 0:
                    pe.wait_ge(gap_ready, 1)
                else:
                    pe.wait_ge(gap_ready, 3)
                for c in range(4):
                    ins = tp(bank[4 + u][:, c * P:(c + 1) * P], zswa[:, u, c * P:(c + 1) * P], ident[:])
                qt.mark(ins)
            l2 = Tally(pe, l2_psum)

            def l2_sum(u):
                pe.wait_ge(l2_sq, u + 1)
                pe.wait_ge(qkT_ready, u + 1)
                l2.mark(mm(bank[4 + u][:], ones[:], sc[:, u % 2], start=True, stop=True))

            unit(10)
            unit(11)
            unit(12)
            l2_sum(0)
            unit(13)
            l2_sum(1)
            l2_sum(2)
            unit(14)
            l2_sum(3)

            gdn = Tally(pe, gdn_psum)
            sp_, pp, op = Tally(pe, s_psum), Tally(pe, pt_psum), Tally(pe, o_psum)
            kT = lambda t, h: conv[:, HG + h, t * P:(t + 1) * P]
            qT = lambda t, h: conv[:, h, t * P:(t + 1) * P]
            vT = lambda t, h: conv[:, 2 * HG + h, t * P:(t + 1) * P]
            pe.wait_ge(l2_done, 4)
            pe.wait_ge(z_evac, 15)
            for kind, a, s in ORDER:
                if kind == "gdn":
                    t, m = a, MAT[a]
                    X, Y, Z = bank[2 * t], bank[2 * t + 1], bank[4]
                    at = GDN_SEQ.index((t, s))
                    before = [q for q in GDN_SEQ[:at] if q[0] == t or s in SHARED_BANK_STAGES]
                    if before:
                        pe.wait_ge(gdn_dve, DVE_DONE[before[-1]])
                        if ACT_DONE[before[-1]]:
                            pe.wait_ge(gdn_act, ACT_DONE[before[-1]])

                    def product(dst, lhsT, rhs, start=True, stop=True):
                        for h in range(HG):
                            c = slice(h * P, (h + 1) * P)
                            last = mm(dst[:, c], lhsT(h) if callable(lhsT) else lhsT[:, c],
                                      rhs(h) if callable(rhs) else rhs[:, c], start=start, stop=stop)
                        return last

                    def flip(dst, src):
                        for h in range(HG):
                            c = slice(h * P, (h + 1) * P)
                            last = tp(dst[:, c], src(h) if callable(src) else src[:, c], ident[:])
                        return last

                    kt, qt_, vt = (lambda h, f=f: f(t, h) for f in (kT, qT, vT))
                    if s == 1:
                        product(X, kt, kt)
                        ins = product(Y, kt, qt_)
                    elif s == 2:
                        flip(X, m["N"])
                        if t == 0:
                            flip(Y, kt)
                            pe.wait_ge(l2_root, 4)
                        pe.wait_ge(silu_ready, 6)
                        ins = flip(Z, vt)
                    elif s == 3:
                        product(X, m["D"], m["N"])
                        ins = product(Y, m["N"], m["D"])
                    elif s == 4:
                        product(X, m["F"], m["E"])
                        product(Y, m["E"], m["F"])
                        ins = product(Z, m["E"], m["G"])
                    elif s == 5:
                        product(X, m["D"], m["N"])
                        ins = product(Z, m["N"], m["G"])
                    elif s == 6:
                        ins = product(X, m["E"], m["G"])
                    elif s == 7:
                        product(X, m["G"], m["L"])
                        ins = product(Y, m["L"], m["G"])
                    elif s == "K":
                        ins = product(Y, kt, MAT[0]["F"])
                    elif s == 8:
                        product(X, m["D"], m["N"])
                        product(Y, m["N"], m["D"])
                        ins = product(Z, m["G"], m["H"])
                    elif s == 9:
                        product(X, m["E"], m["F"])
                        ins = product(Z, m["D"], m["V"])
                    elif s == 10:
                        ins = product(X, m["F"], m["V"])
                    elif s == 11:
                        ins = product(Y, m["N"], m["V"])
                    elif s == 12:
                        product(X, m["A"], m["V"])
                        if t == 0:
                            ins = product(Y, m["I"], m["V"])
                        else:
                            ins = product(Y, qt_, MAT[0]["F"])
                    elif s == 13:
                        ins = flip(X, m["D"])
                    gdn.mark(ins)
                    continue
                g = a
                if s == "S":
                    pe.wait_ge(qkT_ready, 4)
                    if g == 0:
                        pe.wait_ge(l2_root, 4)
                    if g >= 1:
                        pe.wait_ge(s_max, g)
                    for i in range(2 if g < 4 else 4):
                        r = i % 2
                        pair, qt0, n = (g, 1, S) if g < 4 else (2 * (g - 4) + i // 2, 0, P)
                        c0 = 0 if g < 4 else (i // 2) * P
                        ins = mm(swa_s[r][:, c0:c0 + n], qkT[DH * r:DH * (r + 1), 0, pair, qt0 * P:(qt0 + 1) * P],
                                 qkT[DH * r:DH * (r + 1), 1, pair, 0:n], start=True, stop=True)
                    sp_.mark(ins)
                elif s == "T":
                    pe.wait_ge(p_ready, g + 1)
                    if g >= 1:
                        pe.wait_ge(o_ready, g)
                    for c in range(4):
                        ins = tp(bank[7][:, c * P:(c + 1) * P], sc[:, g % 2, c * P:(c + 1) * P], ident[:])
                    pp.mark(ins)
                else:
                    pe.wait_ge(pt_ready, g + 1)
                    pe.wait_ge(z_evac, 7)
                    if g < 4:
                        for r in range(2):
                            h = 2 * g + r
                            for j in range(2):
                                ins = mm(bank[7][DH * r:DH * (r + 1), 0:P], zswa[:, 4 + j, h * DH:(h + 1) * DH],
                                         pt[:, g % 2, (2 * r + j) * P:(2 * r + j + 1) * P],
                                         start=j == 0, stop=j == 1)
                    else:
                        for i in range(4):
                            h, r = 4 * (g - 4) + i, i % 2
                            ins = mm(bank[7][DH * r:DH * (r + 1), (i // 2) * P:(i // 2 + 1) * P],
                                     zswa[:, 4, h * DH:(h + 1) * DH], pt[:, g % 2, i * P:(i + 1) * P],
                                     start=True, stop=True)
                    op.mark(ins)

            pe.wait_ge(ld_wout, 16)
            pe.wait_ge(gdn_dve, DVE_DONE[1, 13])
            pe.wait_ge(o_ready, 6)
            hp = Tally(pe, h_psum)
            for i in range(2 * T):
                t, hf = divmod(i, 2)
                for k in range(KT):
                    ins = mm(bank[i][:], mixT[:, k, t * P:(t + 1) * P], wout[:, k, hf * 512:(hf + 1) * 512],
                             start=k == 0, stop=k == KT - 1)
                hp.mark(ins)
            ht = Tally(pe, hT_psum)
            for i in range(2 * T):
                t, q = divmod(i, 2)
                pe.wait_ge(hn_ready, t + 1)
                for k in range(4):
                    ins = tp(bank[4 + i][:, k * P:(k + 1) * P], hn[:, t, (4 * q + k) * P:(4 * q + k + 1) * P],
                             ident[:])
                ht.mark(ins)
            pe.wait_ge(hnT_ready, 2 * T)
            pe.wait_ge(ld_moe, 48)
            for k in range(KT):
                ins = mm(bank[0][0:N_EXP, 0:S], wr[:, k, :], hnT[:, k, :], start=k == 0, stop=k == KT - 1)
            Tally(pe, lgT_psum).mark(ins)
            pe.wait_ge(lgT_ready, 1)
            for t in range(T):
                ins = tp(bank[1][:, 32 * t:32 * t + 32], r3[0:N_EXP, 64 + t * P:64 + (t + 1) * P],
                         ident[0:N_EXP, 0:N_EXP])
            Tally(pe, lg_psum).mark(ins)
            pe.wait_ge(mask_ready, T)
            mask = [r3[:, 384 + 32 * t:416 + 32 * t] for t in range(T)]
            rm = [r3[:, 448 + 32 * t:480 + 32 * t] for t in range(T)]
            gates = [qk[:, 2, 32 * t:32 * t + 32] for t in range(T)]
            mm(bank[2][:, 0:32], ustr[:], mask[0], start=True, stop=True)
            mm(bank[2][:, 32:64], ustr[:], mask[1], start=True, stop=False)
            mm(bank[2][:, 32:64], ones[:], mask[0], start=False, stop=True)
            for t in range(T):
                ins = mm(bank[3][0:N_EXP, 0:1], mask[t], ones[:, 0:1], start=t == 0, stop=t == T - 1)
            Tally(pe, cnt_psum).mark(ins)
            pe.wait_ge(nb_ready, 1)
            more = col[0:N_EXP, 24:25]
            for t in range(T):
                tp(bank[4][0:N_EXP, t * P:(t + 1) * P], rm[t], ident[:])
                ins = tp(bank[5][0:N_EXP, t * P:(t + 1) * P], gates[t], ident[:])
            Tally(pe, rt_psum).mark(ins)
            mm(bank[6][0:1, 64:65], ones[0:N_EXP, 0:1], more, start=True, stop=True)
            Tally(pe, end_psum).mark(mm(bank[3][0:N_EXP, 1:2], ucum[0:N_EXP, 0:N_EXP], more, start=True, stop=True))
            pe.wait_ge(rt_ready, 2)
            oh = r3[0:N_EXP, 0:MAXB]
            ohr = r3[0:N_EXP, 64:64 + MAXB]
            rmT, gT = qk[0:N_EXP, 0, 0:S], qk[0:N_EXP, 0, S:2 * S]
            mm(bank[6][0:1, 0:MAXB], col[0:N_EXP, 8:9], oh, start=True, stop=True)
            for t in range(T):
                c = slice(t * MAXB, (t + 1) * MAXB)
                mm(bank[7][:, c], rmT[:, t * P:(t + 1) * P], oh, start=True, stop=False)
                mm(bank[7][:, c], ones[0:N_EXP, :], ohr, start=False, stop=True)
                ins = mm(bank[7][:, 128 + t * MAXB:128 + (t + 1) * MAXB], gT[:, t * P:(t + 1) * P], oh,
                         start=True, stop=True)
            Tally(pe, tab_psum).mark(ins)
            for t in range(T):
                for hf in range(2):
                    mm(bank[2 * t + hf][:], gT[:, t * P:(t + 1) * P], bdn[:, hf * 512:(hf + 1) * 512],
                       start=True, stop=False, skip_group_check=True)

            def gather():
                for t in range(T):
                    for hf in range(2):
                        last = mm(bank[6][SLOTS * hf:SLOTS * (hf + 1), :], SEL[:, t, :],
                                  hn[:, t, hf * 512:(hf + 1) * 512], start=t == 0, stop=t == T - 1)
                last.then_inc(xg_psum, 1)

            def gather_flip():
                for c in range(4):
                    last = tp(bank[6][:, c * P:(c + 1) * P], xg[:, c * P:(c + 1) * P], ident[:])
                last.then_inc(xgT_psum, 1)

            def combine():
                for t in range(T):
                    for hf in range(2):
                        last = mm(bank[2 * t + hf][:], SGT[SLOTS * hf:SLOTS * (hf + 1), t * P:(t + 1) * P],
                                  yb[SLOTS * hf:SLOTS * (hf + 1), :], start=False, stop=False,
                                  skip_group_check=True)
                last.then_inc(acc_done, 1)

            pe.wait_ge(S_ready, 1)
            gather()
            pe.wait_ge(xg_ready, 1)
            gather_flip()
            n_blocks = pe.value_load(nbl[0:1, MAXB:MAXB + 1], min_val=N_EXP, max_val=NB_MAX)

            def gate_up(b):
                pe.wait_ge(xgT_ready, b + 1)
                pe.wait_ge(oh_ready, b + 1)
                order = [(bank[4], 0, 0), (bank[4], 1, 512), (bank[5], 0, 1024), (bank[5], 1, 1536)]
                for dst, hf, c0 in order:
                    mm(dst[SLOTS * hf:SLOTS * (hf + 1), :], oh_cur, bgu[:, c0:c0 + 512], start=True, stop=False)
                for k in range(KT):
                    pe.wait_ge(ld_slot[k], 16 * (b + 1))
                    c = (k % 4) * P + (k // 4) * SLOTS
                    for dst, hf, c0 in order:
                        last = mm(dst[SLOTS * hf:SLOTS * (hf + 1), :], xgT[:, c:c + SLOTS],
                                  ring[:, k, c0:c0 + 512], start=False, stop=k == KT - 1)
                    last.then_inc(wgu_used, 1)

            def rest(b):
                pe.wait_ge(SG_ready, b + 1)
                for t in range(T):
                    last = tp(bank[7][:, t * P:(t + 1) * P], SG[:, t, :], ident[:])
                last.then_inc(SGT_psum, 1)
                pe.wait_ge(S_ready, b + 2)
                gather()
                pe.wait_ge(act_ready, b + 1)
                for c in range(4):
                    last = tp(bank[4][:, c * P:(c + 1) * P], up[:, c * P:(c + 1) * P], ident[:])
                last.then_inc(actT_psum, 1)
                pe.wait_ge(xg_ready, b + 2)
                gather_flip()
                pe.wait_ge(actT_ready, b + 1)
                pe.wait_ge(SGT_ready, b + 1)
                for f in range(KT):
                    if f % 2 == 0:
                        pe.wait_ge(ld_slot[8 + f // 2], 16 * (b + 1))
                    w = ring[:, 8 + f // 2, (f % 2) * D:(f % 2 + 1) * D]
                    c = (f % 4) * P + (f // 4) * SLOTS
                    for hf in range(2):
                        last = mm(bank[7][SLOTS * hf:SLOTS * (hf + 1), :], actT[:, c:c + SLOTS],
                                  w[:, hf * 512:(hf + 1) * 512], start=f == 0, stop=f == KT - 1)
                    if f % 2:
                        last.then_inc(wdn_used, 1)

            pe.wait_ge(zeroed, 2)
            with pe.Fori(0, n_blocks) as b:
                gate_up(b)
                pe.wait_ge(y_ready, b + 1)
                combine()
                rest(b)
            pe.wait_ge(y_ready, n_blocks + 1)
            combine()


_INS = ["x", "norm1_w", "w_in", "conv_w", "a_log", "dt_bias", "gdn_norm_w", "q_norm_w", "k_norm_w", "rel_bias",
        "w_out", "norm2_w", "w_router", "b_router", "w_gate_up", "b_gate_up", "w_down", "b_down"]


def kernel(**inputs):
    import numpy as _np
    import concourse.bacc as _bacc
    from concourse import mybir as _mybir
    from concourse.bass_utils import run_bass_kernel_spmd as _run

    nc = _bacc.Bacc("TRN2", target_bir_lowering=False, num_devices=1)
    arrays, args = {}, []
    for name in _INS + ["dist_table"]:
        a = distance_table(inputs["x"].shape[1]) if name == "dist_table" else inputs[name]
        a = _np.ascontiguousarray(a)
        arrays[f"in_{name}_dram"] = a
        args.append(nc.dram_tensor(f"in_{name}_dram", a.shape, _mybir.dt.from_np(a.dtype), kind="ExternalInput").ap())
    shape = inputs["x"].shape
    args.append(nc.dram_tensor("out_dram", shape, _mybir.dt.float32, kind="ExternalOutput").ap())
    hybrid_layer(nc, *args)
    r = _run(nc, [arrays], core_ids=[0])
    return r.results[0]["out_dram"]
```

```python
import math
from contextlib import ExitStack

import concourse.bass as bass
import numpy as np
from concourse import mybir

ALU = mybir.AluOpType
ACT = mybir.ActivationFunctionType
AX_X = mybir.AxisListType.X
F32 = mybir.dt.float32
I32 = mybir.dt.int32
U32 = mybir.dt.uint32

P = 128
EPS = 1e-6
HG, DK = 4, 128
HS, DH = 8, 64
CONV_K = 4
BRANCHES = ((128, 1), (512, 4), (2048, 16))
REL_BUCKETS, REL_MAX_DIST = 32, 2048
N_EXP, TOP_K = 32, 4
LIMIT, ALPHA = 7.0, 1.702
SLOTS = 64
MASKED = -1e30
ABSENT = 1024.0


def distance_table(seq):
    dist = seq - 1 - np.arange(seq + P)
    near = REL_BUCKETS // 2
    n = np.maximum(dist, 0)
    far = near + (np.log(np.maximum(n, 1) / near) / math.log(REL_MAX_DIST / near)
                  * (REL_BUCKETS - near)).astype(np.int32)
    bucket = np.where(n < near, n, np.minimum(far, REL_BUCKETS - 1))
    held = sum(((dist % dil == 0) & (dist <= window)).astype(np.int32) for window, dil in BRANCHES)
    held = np.where(dist < 0, 0, held)
    table = np.zeros((REL_BUCKETS + 1, seq + P), np.float32)
    table[bucket, np.arange(seq + P)] = 1.0
    table[REL_BUCKETS] = np.where(held > 0, np.log(np.maximum(held, 1)), MASKED)
    return table


RING = [1, 0, *range(2, 12), "f0", "f1", "f2", "f3"]
LATE_UNITS = [12, 13, 14]


def attention_order():
    text = ("z7 01 11 z8 02 12 z9 03 13 z10 04 14 n0 z11 f0 f1 05 15 f2 f3 06 16 S0 z12 07 17 S1 08 T0 "
            "z13 09 O0 0A T1 S2 0B O1 z14 0C 1K T2 S3 0M 18 O2 0N T3 S4 19 0D O3 1A W0 T4 S5 1B O4 1C W1 "
            "1M T5 A0 O5 1N W2 W3 R0 1D L0 X2 X3 A1 G0 R1 L1 G1")
    names = {str(i): i for i in range(10)} | {"A": 10, "B": 11, "C": 12, "D": 13, "K": "K", "M": "M", "N": "N"}
    return [("gdn", int(w[0]), names[w[1]]) if w[0] in "01" else (w[0], int(w[1:]), None)
            for w in text.split()]


ORDER = attention_order()
BANK7 = [(kind, a) for kind, a, _ in ORDER if kind in "TO" or (kind == "z" and a in LATE_UNITS)]
PE_STAGES = {1, 2, 3, 4, 5, 6, 7, "K", 8, 9, 10, 11, 12, 13}
DVE_STAGES = PE_STAGES | {"M", "N"}
ACT_STAGES = {3, 4, 5, 7, 8, 9, "M", "N"}
SHARED_BANK_STAGES = {2, 4, 5, 8, 9, "K"}


def stage_counts(stages):
    n, out = 0, {}
    for kind, t, s in ORDER:
        if kind == "gdn":
            n += s in stages
            out[t, s] = n
    return out


PE_DONE, DVE_DONE, ACT_DONE = (stage_counts(x) for x in (PE_STAGES, DVE_STAGES, ACT_STAGES))
GDN_SEQ = [(t, s) for kind, t, s in ORDER if kind == "gdn"]


def evacuated(user):
    return (RING + LATE_UNITS).index(user) + 1


def z_bank(user):
    return 7 if user in LATE_UNITS else 5 + RING.index(user) % 3


class Tally:

    def __init__(self, eng, sem):
        self.eng, self.sem, self.n = eng, sem, 0

    def mark(self, ins):
        ins.then_inc(self.sem, 1)
        self.n += 1

    def step(self, ins):
        self.mark(ins)
        self.eng.wait_ge(self.sem, self.n)


def hybrid_layer(nc, x, norm1_w, w_in, conv_w, a_log, dt_bias, gdn_norm_w, q_norm_w, k_norm_w,
                 rel_bias, w_out, norm2_w, w_router, b_router, w_gate_up, b_gate_up, w_down,
                 b_down, dist_table, out):
    S, D = x.shape[1], x.shape[2]
    T = S // P
    KT = D // P
    C_GDN = 3 * HG * DK
    C_GATE, C_BA = C_GDN, C_GDN + HG * DK
    C_SWA = C_BA + 2 * HG
    MAXB = N_EXP + (S * TOP_K - N_EXP) // SLOTS + 1
    assert T == 2 and D == 1024 and w_in.shape[2] == C_SWA + 3 * HS * DH
    NB_MAX = MAXB - 1
    TW = S + P

    with ExitStack() as ctx:
        def sb(name, shape, dt=F32):
            return ctx.enter_context(nc.sbuf_tensor(name, shape, dt))

        def sem(name):
            return ctx.enter_context(nc.semaphore(name))

        ring = sb("ring", [P, 12, 2048])
        hx = sb("hx", [P, T, D])
        arena1 = sb("arena1", [P, T, D])
        arena2 = sb("arena2", [P, KT, S])
        nw = sb("nw", [P, D])
        zswa = sb("zswa", [P, 3 * T, 512])
        qkT = sb("qkT", [P, 2, HS // 2, S])
        zpad = sb("zpad", [P, 12, S + 4])
        conv = sb("conv", [P, 12, S])
        gate = sb("gate", [P, T, HG * DK])
        bias = sb("bias", [P, HS, S])
        sc = sb("sc", [P, 2, 512])
        pt = sb("pt", [P, 2, 512])
        mats = sb("mats", [P, 6, 512])
        ident = sb("ident", [P, P])
        ones = sb("ones", [P, P])
        ucum = sb("ucum", [P, P])
        ustr = sb("ustr", [P, P])
        m_in = sb("m_in", [P, P])
        m_out = sb("m_out", [P, P])
        slot2 = sb("slot2", [P, 2, SLOTS])
        iota_e = sb("iota_e", [P, N_EXP])
        iota_b = sb("iota_b", [N_EXP, MAXB])
        col = sb("col", [P, 64])
        ba = sb("ba", [P, T, 2 * HG])
        gd = sb("gd", [P, 12, T, HG])
        wba = sb("wba", [P, KT, 2 * HG])
        brt = sb("brt", [P, N_EXP])
        own = sb("own", [N_EXP, MAXB])
        cw = sb("cw", [P, CONV_K, 12])
        nrm = sb("nrm", [P, 8, 32])
        rel = sb("rel", [REL_BUCKETS + 1, HS])
        nbl = sb("nbl", [1, 64], I32)

        xn, hn = arena1, arena1
        xnT, hnT = arena2, arena2
        mix_gdn, mix_swa = arena2[:, 0:HG], conv[:, 2 * HG:3 * HG]
        ug = arena1[:, 0, :].rearrange("p (t n) -> p t n", t=T)
        a1m = arena1[:].rearrange("p t d -> p (t d)").rearrange("p (m n) -> p m n", n=512)
        zpm = zpad[:].rearrange("p c s -> p (c s)")[:, 0:6 * 512].rearrange("p (m n) -> p m n", n=512)
        MAT = [dict(N=mats[:, 3 * t + 0], L=mats[:, 3 * t + 1], A=mats[:, 3 * t + 2],
                    D=zpm[:, 3 * t + 0], E=zpm[:, 3 * t + 1], F=zpm[:, 3 * t + 2],
                    G=a1m[:, 2 * t], H=a1m[:, 2 * t + 1], I=zswa[:, t], V=zswa[:, 2 + t])
               for t in range(T)]
        cw_rows = mats[0:CONV_K * 12, 5, 0:P]
        fdist = pt[0:HS, 0, 0:TW]
        dtab = pt[0:REL_BUCKETS + 1, 1, 0:TW]
        wout = ring[:, 8:12, :].rearrange("p s (j n) -> p (s j) n", n=D)
        bgu = bias[0:N_EXP].rearrange("p h s -> p (h s)")
        bdn = gate[0:N_EXP].rearrange("p t d -> p (t d)")
        wr = sc[:, 0, 0:KT * N_EXP].rearrange("p (k e) -> p k e", e=N_EXP)
        cv = conv[:].rearrange("p c s -> p (c s)").rearrange("p (m n) -> p m n", n=512)
        xg, xgT, gt, up, sg, actT = (cv[:, m] for m in range(6))
        qk = qkT[:].rearrange("p a b s -> p (a b s)").rearrange("p (m n) -> p m n", n=512)
        yb = qk[:, 0]
        SGT = qk[:, 1, 0:S]
        SEL = qk[:, 1, S:S + T * SLOTS].rearrange("p (t s) -> p t s", t=T)
        oh_cur = qk[0:N_EXP, 1, S + T * SLOTS:S + T * SLOTS + SLOTS]
        SG = qk[:, 2, 0:T * 2 * SLOTS].rearrange("p (t s) -> p t s", t=T)
        RM = qk[:, 2, 256:256 + T * MAXB].rearrange("p (t b) -> p t b", t=T)
        GB = qk[:, 2, 256 + T * MAXB:256 + 2 * T * MAXB].rearrange("p (t b) -> p t b", t=T)
        r3 = qk[:, 3]
        top = [r3[:, 16 * t:16 * t + 8] for t in range(T)]
        ex = [r3[:, 16 * t + 8:16 * t + 8 + TOP_K] for t in range(T)]
        picks = [r3[:, 64 + 128 * t:192 + 128 * t].rearrange("p (j e) -> p j e", j=TOP_K) for t in range(T)]
        shares = [qk[:, 0, 128 * t:128 * t + 128].rearrange("p (j e) -> p j e", j=TOP_K) for t in range(T)]
        lg = [r3[:, 320 + 32 * t:352 + 32 * t] for t in range(T)]
        mask = [r3[:, 384 + 32 * t:416 + 32 * t] for t in range(T)]
        rm = [r3[:, 448 + 32 * t:480 + 32 * t] for t in range(T)]
        masks, rms = r3[:, 384:448], r3[:, 448:512]
        gates = [qk[:, 2, 32 * t:32 * t + 32] for t in range(T)]
        oh, ohr, since = r3[0:N_EXP, 0:MAXB], r3[0:N_EXP, 64:64 + MAXB], r3[0:N_EXP, 128:128 + MAXB]
        rmT, gT = qk[0:N_EXP, 0, 0:S], qk[0:N_EXP, 0, S:2 * S]
        more, end, beg = (col[0:N_EXP, c:c + 1] for c in (24, 25, 26))

        bank = [ctx.enter_context(nc.psum_tensor(f"bank{i}", [P, 512], F32)) for i in range(8)]
        swa_s = [bank[5], bank[6]]

        fd_dram = nc.dram_tensor("bias_by_distance", [HS, P, TW], F32, kind="Internal").ap()

        ld_x, ld_nw, ld_ba, ld_small, ld_rel = (sem(n) for n in ("ld_x", "ld_nw", "ld_ba", "ld_small", "ld_rel"))
        ld_win = [sem(f"ld_win{i}") for i in range(4)]
        ld_wout, ld_nw2, ld_wr, ld_moe = sem("ld_wout"), sem("ld_nw2"), sem("ld_wr"), sem("ld_moe")
        ld_slot = [sem(f"ld_slot{i}") for i in range(12)]
        st_dist, ld_bias, st_out = sem("st_dist"), sem("ld_bias"), sem("st_out")
        consts, rel_one = sem("consts"), sem("rel_one")
        dve_step, act_step, pool_step = sem("dve_step"), sem("act_step"), sem("pool_step")
        x_sq, xn_ready, xT_psum, xnT_ready = sem("x_sq"), sem("xn_ready"), sem("xT_psum"), sem("xnT_ready")
        dist_psum, dist_ready, cw_ready = (sem(n) for n in ("dist_psum", "dist_ready", "cw_ready"))
        z_psum, z_evac = sem("z_psum"), sem("z_evac")
        dec_dve, dec_act, g_ready, ug_ready = sem("dec_dve"), sem("dec_act"), sem("g_ready"), sem("ug_ready")
        gc_psum, gcrow_psum, gap_ready, e_ready, emask_ready = (
            sem(n) for n in ("gc_psum", "gcrow_psum", "gap_ready", "e_ready", "emask_ready"))
        swa_sq, swa_ss, swa_root, swa_normed = sem("swa_sq"), sem("swa_ss"), sem("swa_root"), sem("swa_normed")
        qkT_psum = sem("qkT_psum")
        pad_ready, conv_ready, silu_ready, gsilu = sem("pad_ready"), sem("conv_ready"), sem("silu_ready"), sem("gsilu")
        l2_sq, l2_psum, l2_root, l2_done = sem("l2_sq"), sem("l2_psum"), sem("l2_root"), sem("l2_done")
        gdn_psum, gdn_dve, gdn_act = sem("gdn_psum"), sem("gdn_dve"), sem("gdn_act")
        s_psum, s_max, p_exp, p_ready, pt_psum, pt_ready, o_psum, o_ready = (
            sem(n) for n in ("s_psum", "s_max", "p_exp", "p_ready", "pt_psum", "pt_ready", "o_psum", "o_ready"))
        h_psum, h_ready, h_sq, hn_ready, hT_psum, hnT_ready = (
            sem(n) for n in ("h_psum", "h_ready", "h_sq", "hn_ready", "hT_psum", "hnT_ready"))
        lg_psum, lg_max, lg_exp, mask_ready = (sem(n) for n in ("lg_psum", "lg_max", "lg_exp", "mask_ready"))
        cnt_psum, nb_ready, end_psum, rm_ready, rt_psum, rt_ready, tab_psum, tab_ready = (
            sem(n) for n in ("cnt_psum", "nb_ready", "end_psum", "rm_ready", "rt_psum", "rt_ready", "tab_psum",
                             "tab_ready"))
        wgu_used, wdn_used = sem("wgu_used"), sem("wdn_used")
        g_min, sig_ready, act_ready, actT_psum, actT_ready = (
            sem(n) for n in ("g_min", "sig_ready", "act_ready", "actT_psum", "actT_ready"))
        S_ready, SG_ready, oh_ready, SGT_psum, SGT_ready = (
            sem(n) for n in ("S_ready", "SG_ready", "oh_ready", "SGT_psum", "SGT_ready"))
        zeroed, xg_psum, xg_ready, xgT_psum, xgT_ready, y_ready, acc_done, out_ready = (
            sem(n) for n in ("zeroed", "xg_psum", "xg_ready", "xgT_psum", "xgT_ready", "y_ready", "acc_done", "out_ready"))

        block = ctx.enter_context(nc.Block())

        win = w_in[0].rearrange("(k p) n -> p k n", p=P)
        PIECES = [512, 0, 1024, C_SWA, C_SWA + 512, C_SWA + 1024, C_GATE]
        CONV_AT = {1: 4, 2: 6, 3: 0, 4: 2, 5: 8, 6: 10}
        H_BANK = [0, 1, 5, 6]

        def piece(j):
            s = 2 * (j % 4)
            return ring[:, s:s + 2, :].rearrange("p s (j n) -> p (s j) n", n=512)

        def heads(ap, h=HG):
            return ap.rearrange("p (h n) -> p h n", h=h)

        def wide(cols, n):
            return cols.unsqueeze(2).to_broadcast([cols.shape[0], cols.shape[1], n])

        def each_head(mask):
            return mask.unsqueeze(1).to_broadcast([P, HG, P])

        def expert_tile(e_ap, slot):
            if slot < 8:
                src = w_gate_up[0][e_ap, slot * P:(slot + 1) * P, :]
                return src.rearrange("a p n -> p (a n)")
            s = slot - 8
            src = w_down[0][e_ap, 2 * s * P:2 * (s + 1) * P, :]
            return src.rearrange("a (j p) n -> p (a j) n", p=P)

        def slot_dst(slot):
            if slot < 8:
                return ring[:, slot, :]
            return ring[:, slot, :].rearrange("p (j n) -> p j n", n=D)

        @block.sync
        def _(sp):
            sp.dma_start(hx[:], x[0].rearrange("(t p) d -> p t d", p=P)).then_inc(ld_x, 16)
            sp.dma_start(nw[:], norm1_w.to_broadcast([P, D])).then_inc(ld_nw, 16)
            sp.dma_start(dtab, dist_table).then_inc(ld_rel, 16)
            sp.dma_start(cw_rows, conv_w[0].rearrange("i (c p) -> (i c) p", p=P)).then_inc(ld_rel, 16)
            for j, c0 in enumerate(PIECES):
                if j >= 4:
                    sp.wait_ge(z_psum, 2 * (j - 4) + 3)
                sp.dma_start(piece(j), win[:, :, c0:c0 + 512]).then_inc(ld_win[j % 4], 16)
                if j == 3:
                    sp.wait_ge(dist_ready, 1)
                    sp.dma_start(fd_dram, fdist.unsqueeze(1).to_broadcast([HS, P, TW])).then_inc(st_dist, 16)
                if j == 4:
                    sp.wait_ge(st_dist, 16)
                    sp.dma_start(bias[:], bass.AP(fd_dram.tensor, S - 1 - P, [[TW - 1, P], [P * TW, HS], [1, S]])
                                 ).then_inc(ld_bias, 16)
                    sp.dma_start(wout, w_out[0].rearrange("(k p) n -> p k n", p=P)).then_inc(ld_wout, 16)
            for s in (6, 7, 0, 1, 2, 3, 4, 5):
                j = 3 if s >= 6 else 4 + s // 2
                sp.wait_ge(z_psum, 2 * j + 3)
                sp.dma_start(slot_dst(s), expert_tile(slice(0, 1), s)).then_inc(ld_slot[s], 16)
            sp.wait_ge(xn_ready, T)
            sp.dma_start(nw[:], norm2_w.to_broadcast([P, D])).then_inc(ld_nw2, 16)
            sp.wait_ge(pt_psum, 5)
            sp.dma_start(wr, w_router[0].rearrange("(k p) e -> p k e", p=P)).then_inc(ld_wr, 16)
            sp.wait_ge(s_max, 6)
            sp.dma_start(bgu, b_gate_up[0]).then_inc(ld_moe, 16)
            sp.wait_ge(gdn_dve, DVE_DONE[1, "N"])
            sp.dma_start(bdn, b_down[0]).then_inc(ld_moe, 16)
            sp.wait_ge(h_psum, 2 * T)
            for s in range(8, 12):
                sp.dma_start(slot_dst(s), expert_tile(slice(0, 1), s)).then_inc(ld_slot[s], 16)
            sp.wait_ge(tab_ready, 4)
            n_blocks = sp.value_load(nbl[0:1, MAXB:MAXB + 1], min_val=N_EXP, max_val=NB_MAX)
            with sp.Fori(1, n_blocks) as b:
                e = sp.value_load(nbl[0:1, bass.ds(b, 1)], min_val=0, max_val=N_EXP - 1)
                for s in range(12):
                    if s < 8:
                        sp.wait_ge(wgu_used, 8 * b + (s - 7))
                    else:
                        sp.wait_ge(wdn_used, 4 * b + (s - 11))
                    sp.dma_start(slot_dst(s), expert_tile(bass.ds(e, 1), s)).then_inc(ld_slot[s], 16)
            for t in range(T):
                sp.wait_ge(out_ready, t + 1)
                sp.dma_start(out[0, t * P:(t + 1) * P, :], hx[:, t, :]).then_inc(st_out, 16)
            sp.wait_ge(st_out, 16 * T)

        @block.gpsimd
        def _(pool):
            c = Tally(pool, consts)
            c.mark(pool.memset(ones[:], 1.0))
            c.mark(pool.memset(ident[:], 0.0))
            c.mark(pool.memset(zpad[:], 0.0))
            c.mark(pool.iota(slot2[:], [[0, 2], [1, SLOTS]], base=0, channel_multiplier=0,
                             allow_small_or_imprecise_dtypes=True))
            c.mark(pool.iota(iota_e[:], [[1, N_EXP]], base=0, channel_multiplier=0,
                             allow_small_or_imprecise_dtypes=True))
            c.mark(pool.iota(iota_b[:], [[1, MAXB]], base=0, channel_multiplier=0,
                             allow_small_or_imprecise_dtypes=True))
            c.mark(pool.iota(col[:, 8:9], [[0, 1]], base=0, channel_multiplier=1,
                             allow_small_or_imprecise_dtypes=True))
            c.mark(pool.memset(m_out[:], -1.0))
            c.mark(pool.memset(col[:, 0:1], EPS))
            c.mark(pool.memset(col[:, 1:2], EPS * DK))
            c.step(pool.memset(col[:, 2:3], 1.0))
            c.mark(pool.affine_select(ident[:], ident[:], [[-1, P]], ALU.not_equal, 1.0, base=0,
                                      channel_multiplier=1))
            c.mark(pool.affine_select(ucum[:], ones[:], [[1, P]], ALU.is_ge, 0.0, base=0,
                                      channel_multiplier=-1))
            c.mark(pool.affine_select(ustr[:], ones[:], [[1, P]], ALU.is_gt, 0.0, base=0,
                                      channel_multiplier=-1))
            c.step(pool.affine_select(m_out[:], m_out[:], [[-1, P]], ALU.is_gt, 0.0, base=0,
                                      channel_multiplier=1))
            c.step(pool.affine_select(m_in[:].rearrange("p (b n) -> p b n", n=16),
                                      m_out[:].rearrange("p (b n) -> p b n", n=16),
                                      [[16, P // 16], [0, 16]], ALU.is_ge, 0.0, base=15,
                                      channel_multiplier=-1))
            c.step(pool.tensor_tensor(m_out[:], m_out[:], m_in[:], ALU.subtract))
            em, st = Tally(pool, emask_ready), Tally(pool, pool_step)
            for t in range(T):
                m = MAT[t]
                pool.wait_ge(e_ready, 2 * t + 2)
                pool.wait_ge(dec_act, 3)
                st.step(pool.tensor_tensor(heads(m["L"]), heads(m["N"]), wide(gd[:, 2, t], P), ALU.mult))
                st.step(pool.tensor_tensor(heads(m["N"]), heads(m["L"]), each_head(m_in[:]), ALU.mult))
                st.step(pool.tensor_tensor(heads(m["L"]), heads(m["L"]), each_head(m_out[:]), ALU.mult))
                em.mark(pool.tensor_tensor(heads(m["A"]), heads(m["A"]), each_head(ucum[:]), ALU.mult))
            l2, sq = Tally(pool, l2_sq), Tally(pool, swa_sq)
            for u in range(4):
                pool.wait_ge(silu_ready, u + 1)
                if u >= 2:
                    pool.wait_ge(l2_psum, u - 1)
                c0 = CONV_AT[u + 1]
                v = conv[:, c0:c0 + 2, :].rearrange("p c s -> p (c s)")
                l2.mark(pool.tensor_tensor(sc[:, u % 2], v, v, ALU.mult))
            for u in range(2 * T):
                pool.wait_ge(z_evac, evacuated(u + 7))
                if u < 2:
                    pool.wait_ge(l2_psum, u + 3)
                else:
                    pool.wait_ge(swa_ss, u - 1)
                sq.mark(pool.tensor_tensor(sc[:, u % 2], zswa[:, u], zswa[:, u], ALU.mult))

        @block.scalar
        def _(act):
            act.dma_start(wba[:], win[:, :, C_BA:C_BA + 2 * HG]).then_inc(ld_ba, 16)
            act.dma_start(rel[0:REL_BUCKETS, :], rel_bias).then_inc(ld_rel, 16)
            small = [(gd[:, 0, 0], a_log.to_broadcast([P, HG])),
                     (gd[:, 1, 0], dt_bias.to_broadcast([P, HG])),
                     (col[:, 16:17], gdn_norm_w.rearrange("a d -> d a")),
                     (col[0:DH, 17:18], q_norm_w.rearrange("a d -> d a")),
                     (col[DH:P, 17:18], q_norm_w.rearrange("a d -> d a")),
                     (col[0:DH, 18:19], k_norm_w.rearrange("a d -> d a")),
                     (col[DH:P, 18:19], k_norm_w.rearrange("a d -> d a")),
                     (brt[:], b_router.to_broadcast([P, N_EXP]))]
            for dst, src in small:
                act.dma_start(dst, src).then_inc(ld_small, 16)

            st = Tally(act, act_step)
            act.wait_ge(ld_x, 16)
            act.wait_ge(consts, 11)
            xs = Tally(act, x_sq)
            for t in range(T):
                st.step(act.activation(xn[:, t, :], hx[:, t, :], ACT.Square, accum_out=nrm[:, 0, t:t + 1]))
            xs.mark(act.activation(nrm[:, 1, 0:T], nrm[:, 0, 0:T], ACT.Sqrt, bias=col[:, 0:1], scale=1.0 / D))
            xt = Tally(act, xnT_ready)
            for i in range(2 * T):
                t, q = divmod(i, 2)
                act.wait_ge(xT_psum, i + 1)
                xt.mark(act.copy(xnT[:, 4 * q:4 * q + 4, t * P:(t + 1) * P], heads(bank[i][:])))
            z = Tally(act, z_evac)

            def evac(u):
                act.wait_ge(z_psum, {1: 1, 0: 2}.get(u, u + 1))
                src = bank[z_bank(u)]
                if u == 0:
                    z.mark(act.copy(ba[:], src[:, 0:T * 8].rearrange("p (t n) -> p t n", t=T)))
                elif u <= 6:
                    act.wait_ge(consts, 11)
                    z.mark(act.copy(zpad[:, CONV_AT[u]:CONV_AT[u] + 2, 3:3 + S],
                                    src[:].rearrange("p (c s) -> p c s", c=2)))
                elif u <= 12:
                    z.mark(act.copy(zswa[:, u - 7], src[:]))
                else:
                    z.mark(act.copy(gate[:, u - 13], src[:]))

            def flip(u):
                a, t = divmod(u, T)
                act.wait_ge(qkT_psum, u + 1)
                act.wait_ge(dec_dve, 2)
                z.mark(act.activation(qkT[:, a, :, t * P:(t + 1) * P],
                                      heads(bank[z_bank(f"f{u}")][:]), ACT.Copy,
                                      scale=col[:, 17 + a:18 + a]))

            si = Tally(act, silu_ready)

            def silu(u):
                act.wait_ge(conv_ready, u)
                v = conv[:, CONV_AT[u]:CONV_AT[u] + 2, :]
                si.mark(act.activation(v, v, ACT.Silu))

            da = Tally(act, dec_act)
            evac(1)
            evac(0)
            act.wait_ge(dec_dve, 1)
            act.wait_ge(ld_small, 16 * 8)
            st.step(act.activation(gd[:, 4], gd[:, 3], ACT.Abs))
            st.step(act.activation(gd[:, 4], gd[:, 4], ACT.Exp, scale=-1.0))
            da.mark(act.activation(gd[:, 0, 0], gd[:, 0, 0], ACT.Exp))
            da.mark(act.activation(gd[:, 4], gd[:, 4], ACT.Ln, bias=1.0))
            da.mark(act.activation(gd[:, 2], ba[:, :, 0:HG], ACT.Sigmoid))
            act.wait_ge(gap_ready, 1)
            da.mark(act.activation(gd[:, 7], gd[:, 5], ACT.Exp))
            da.mark(act.activation(gd[:, 8], gd[:, 6], ACT.Exp))
            evac(2)
            er = Tally(act, e_ready)
            for t in range(T):
                act.wait_ge(gap_ready, 2 + t)
                er.mark(act.activation(MAT[t]["N"], MAT[t]["N"], ACT.Exp, scale=-1.0))
                er.mark(act.activation(MAT[t]["A"], MAT[t]["A"], ACT.Exp))
            evac(3)
            silu(1)
            silu(2)
            evac(4)
            silu(3)
            evac(5)
            silu(4)
            evac(6)
            lr = Tally(act, l2_root)
            for u in range(4):
                act.wait_ge(l2_psum, u + 1)
                q = u >= 2
                st.mark(act.activation(a1m[:, u], bank[u][:], ACT.Ln, bias=col[:, 1:2] if q else col[:, 0:1],
                                       scale=float(DK) if q else 1.0))
            act.wait_ge(act_step, st.n)
            for u in range(4):
                lr.mark(act.activation(a1m[:, u], a1m[:, u], ACT.Exp, scale=-0.5))
            silu(5)
            silu(6)

            gdn, pe_, pr = Tally(act, gdn_act), Tally(act, p_exp), Tally(act, pt_ready)
            gs, hs, ht, le = (Tally(act, q) for q in (gsilu, h_sq, hnT_ready, lg_exp))
            for kind, a, s in ORDER:
                if kind == "z":
                    evac(a)
                    if a == 14:
                        act.wait_ge(z_evac, z.n)
                        gs.mark(act.activation(gate[:], gate[:], ACT.Silu))
                elif kind == "n":
                    act.wait_ge(swa_ss, 4)
                    Tally(act, swa_root).mark(act.activation(nrm[:, 3], nrm[:, 2], ACT.Sqrt,
                                                                 bias=col[:, 0:1], scale=1.0 / DH))
                elif kind == "f":
                    flip(a)
                elif kind == "gdn":
                    m, X = MAT[a], bank[2 * a]
                    if s == "M":
                        act.wait_ge(gdn_dve, DVE_DONE[a, 12])
                        gdn.mark(act.activation(m["E"], m["D"], ACT.Square))
                    elif s == "N":
                        act.wait_ge(gdn_dve, DVE_DONE[a, "M"])
                        gdn.mark(act.activation(nrm[:, 6, 4 * a:4 * a + 4], nrm[:, 5, 4 * a:4 * a + 4],
                                                ACT.Sqrt, bias=col[:, 0:1], scale=1.0 / DK))
                    elif s in ACT_STAGES:
                        act.wait_ge(gdn_psum, PE_DONE[a, s])
                        dst = {3: "E", 4: "N", 5: "E", 7: "N", 8: "E", 9: "N"}[s]
                        gdn.mark(act.copy(m[dst], X[:]))
                elif kind == "S":
                    g = a
                    n = 4 if g < 2 else 2
                    act.wait_ge(s_max, g + 1)
                    for h in range(n):
                        w = 512 // n
                        pe_.mark(act.activation(sc[:, g % 2, h * w:(h + 1) * w], sc[:, g % 2, h * w:(h + 1) * w],
                                                ACT.Exp, bias=nrm[:, 4, 8 * (g % 2) + h:8 * (g % 2) + h + 1],
                                                accum_out=nrm[:, 4, 16 + 8 * (g % 2) + h:17 + 8 * (g % 2) + h]))
                elif kind == "T":
                    act.wait_ge(pt_psum, a + 1)
                    if a >= 2:
                        act.wait_ge(o_psum, a - 1)
                    pr.mark(act.copy(pt[:, a % 2], bank[7][:]))
                elif kind == "A":
                    act.wait_ge(h_ready, 2 * a + 2)
                    st.step(act.activation(hn[:, a, :], hx[:, a, :], ACT.Square, accum_out=nrm[:, 0, a:a + 1]))
                    hs.mark(act.activation(nrm[:, 1, a:a + 1], nrm[:, 0, a:a + 1], ACT.Sqrt, bias=col[:, 0:1],
                                           scale=1.0 / D))
                elif kind == "L":
                    for q in range(2):
                        act.wait_ge(hT_psum, 2 * a + q + 1)
                        ht.mark(act.copy(hnT[:, 4 * q:4 * q + 4, a * P:(a + 1) * P], heads(bank[2 * a + q][:])))
                elif kind == "G":
                    act.wait_ge(lg_max, a + 1)
                    le.mark(act.activation(ex[a], top[a][:, 0:TOP_K], ACT.Exp, bias=nrm[:, 7, a:a + 1],
                                           accum_out=nrm[:, 7, 2 + a:3 + a]))

            act.wait_ge(xg_psum, 1)
            xr, yr, sr, gr2 = Tally(act, xg_ready), Tally(act, y_ready), Tally(act, sig_ready), Tally(act, SGT_ready)
            xr.mark(act.copy(xg, bank[6][:]))
            act.wait_ge(zeroed, 2)
            yr.mark(act.copy(yb[:, 0:1], yb[:, 0:1]))
            act.wait_ge(tab_ready, 4)
            n_blocks = act.value_load(nbl[0:1, MAXB:MAXB + 1], min_val=N_EXP, max_val=NB_MAX)
            with act.Fori(0, n_blocks) as b:
                act.wait_ge(g_min, b + 1)
                act.activation(sg, gt, ACT.Sigmoid, scale=ALPHA).then_inc(sig_ready, 1)
                act.wait_ge(SGT_psum, b + 1)
                act.copy(SGT, bank[7][:, 0:S]).then_inc(SGT_ready, 1)
                act.wait_ge(xg_psum, b + 2)
                act.copy(xg, bank[6][:]).then_inc(xg_ready, 1)
                act.wait_ge(wdn_used, 4 * b + 4)
                act.copy(yb, bank[7][:]).then_inc(y_ready, 1)

        @block.vector
        def _(dve):
            st = Tally(dve, dve_step)
            Tally(dve, rel_one).mark(dve.memset(rel[REL_BUCKETS:REL_BUCKETS + 1, :], 1.0))
            dve.wait_ge(x_sq, 1)
            dve.wait_ge(ld_nw, 16)
            st.step(dve.reciprocal(nrm[:, 1, 2:4], nrm[:, 1, 0:2]))
            xr = Tally(dve, xn_ready)
            for t in range(T):
                xr.mark(dve.scalar_tensor_tensor(out=xn[:, t, :], in0=hx[:, t, :], scalar=nrm[:, 1, 2 + t:3 + t],
                                                 in1=nw[:], op0=ALU.mult, op1=ALU.mult))
            dve.wait_ge(dist_psum, 1)
            Tally(dve, dist_ready).mark(dve.tensor_copy(fdist, bank[4][0:HS, 0:TW]))
            cwr = Tally(dve, cw_ready)
            cwr.step(dve.tensor_copy(cw[:].rearrange("p i c -> p (i c)"), bank[4][:, TW:TW + CONV_K * 12]))
            dve.wait_ge(consts, 17)
            st.mark(dve.tensor_scalar(own[:], iota_b[:], col[0:N_EXP, 8:9], None, ALU.is_equal))

            dd = Tally(dve, dec_dve)
            dve.wait_ge(z_evac, evacuated(0))
            dve.wait_ge(ld_small, 16 * 8)
            dd.step(dve.tensor_tensor(gd[:, 3], ba[:, :, HG:2 * HG],
                                      gd[:, 1, 0].unsqueeze(1).to_broadcast([P, T, HG]), ALU.add))
            dd.step(dve.tensor_scalar(col[:, 17:18], col[:, 17:18], DH ** -0.5, None, ALU.mult))
            st.step(dve.tensor_scalar(gd[:, 9], gd[:, 3], 0.0, None, ALU.max))
            dve.wait_ge(dec_act, 2)
            st.step(dve.tensor_tensor(gd[:, 9], gd[:, 9], gd[:, 4], ALU.add))
            gr = Tally(dve, g_ready)
            for t in range(T):
                gr.step(dve.scalar_tensor_tensor(out=gd[:, 9, t], in0=gd[:, 9, t], scalar=-1.0,
                                                 in1=gd[:, 0, 0], op0=ALU.mult, op1=ALU.mult))
            ur = Tally(dve, ug_ready)
            dve.wait_ge(xT_psum, 2 * T)
            dve.wait_ge(consts, 17)
            for t in range(T):
                for h in range(HG):
                    ur.mark(dve.tensor_scalar(ug[:, t, h * P:(h + 1) * P], ucum[:], gd[:, 9, t, h:h + 1], None,
                                              ALU.mult))
            gp = Tally(dve, gap_ready)
            dve.wait_ge(gc_psum, 1)
            st.step(dve.tensor_copy(gd[:, 5], bank[4][:, 0:8].rearrange("p (t h) -> p t h", t=T)))
            gp.mark(dve.tensor_tensor(gd[:, 6], bank[4][:, 8:16].rearrange("p (t h) -> p t h", t=T), gd[:, 5],
                                      ALU.subtract))
            for t in range(T):
                dve.wait_ge(gcrow_psum, t + 1)
                for h in range(HG):
                    row, mine = bank[t][:, h * P:(h + 1) * P], gd[:, 5, t, h:h + 1]
                    dve.tensor_scalar(MAT[t]["N"][:, h * P:(h + 1) * P], row, mine, 0.0, ALU.subtract, ALU.max)
                    last = dve.tensor_scalar(MAT[t]["A"][:, h * P:(h + 1) * P], row, mine, 0.0,
                                             ALU.subtract, ALU.min)
                gp.mark(last)
            cr, l2 = Tally(dve, conv_ready), Tally(dve, l2_done)
            for u in range(1, 7):
                dve.wait_ge(z_evac, evacuated(u))
                pair = (CONV_AT[u], CONV_AT[u] + 1)
                for c in pair:
                    st.mark(dve.tensor_scalar(conv[:, c, :], zpad[:, c, 0:S], cw[:, 0, c:c + 1], None, ALU.mult))
                for i in range(1, CONV_K):
                    for c in pair:
                        dve.wait_ge(dve_step, st.n - 1)
                        ins = dve.scalar_tensor_tensor(out=conv[:, c, :], in0=zpad[:, c, i:i + S],
                                                       scalar=cw[:, i, c:c + 1], in1=conv[:, c, :],
                                                       op0=ALU.mult, op1=ALU.add)
                        if c == pair[1] and i == CONV_K - 1:
                            cr.mark(ins)
                        else:
                            st.mark(ins)
            for u in range(4):
                dve.wait_ge(l2_root, u + 1)
                c0 = CONV_AT[u + 1]
                v = conv[:, c0:c0 + 2, :].rearrange("p c s -> p (c s)")
                l2.mark(dve.tensor_tensor(v, v, a1m[:, u], ALU.mult))
            dve.wait_ge(dec_act, 5)
            st.step(dve.tensor_tensor(gd[:, 10], gd[:, 2], gd[:, 7], ALU.mult))

            gdn, ss, sn = Tally(dve, gdn_dve), Tally(dve, swa_ss), Tally(dve, swa_normed)
            sm, pr, orr = Tally(dve, s_max), Tally(dve, p_ready), Tally(dve, o_ready)
            hr, hnr, lm, mr = (Tally(dve, q) for q in (h_ready, hn_ready, lg_max, mask_ready))
            n_exp = 0
            for kind, a, s in ORDER:
                if kind == "z":
                    if 8 <= a <= 10:
                        u = a - 8
                        dve.wait_ge(swa_sq, u + 1)
                        ss.mark(dve.reduce_sum(nrm[:, 2, 8 * u:8 * u + 8], heads(sc[:, u % 2], HS), AX_X))
                    continue
                if kind == "n":
                    dve.wait_ge(swa_sq, 4)
                    ss.mark(dve.reduce_sum(nrm[:, 2, 24:32], heads(sc[:, 1], HS), AX_X))
                    dve.wait_ge(swa_root, 1)
                    st.step(dve.reciprocal(nrm[:, 3], nrm[:, 3]))
                    for u in range(2 * T):
                        sn.mark(dve.tensor_tensor(heads(zswa[:, u], HS), heads(zswa[:, u], HS),
                                                  wide(nrm[:, 3, 8 * u:8 * u + 8], DH), ALU.mult))
                    continue
                if kind in "fWXL":
                    continue
                if kind == "A":
                    for hf in range(2):
                        dve.wait_ge(h_psum, 2 * a + hf + 1)
                        v = hx[:, a, hf * 512:(hf + 1) * 512]
                        hr.mark(dve.tensor_tensor(v, bank[H_BANK[2 * a + hf]][:], v, ALU.add))
                    continue
                if kind == "R":
                    dve.wait_ge(h_sq, a + 1)
                    dve.wait_ge(ld_nw2, 16)
                    st.step(dve.reciprocal(nrm[:, 1, 2 + a:3 + a], nrm[:, 1, a:a + 1]))
                    for hf in range(2):
                        c = slice(hf * 512, (hf + 1) * 512)
                        hnr.mark(dve.scalar_tensor_tensor(out=hn[:, a, c], in0=hx[:, a, c],
                                                          scalar=nrm[:, 1, 2 + a:3 + a], in1=nw[:, c],
                                                          op0=ALU.mult, op1=ALU.mult))
                    continue
                if kind == "G":
                    dve.wait_ge(lg_psum, a + 1)
                    st.step(dve.tensor_tensor(lg[a], bank[2 * a][:, 0:N_EXP], brt[:], ALU.add))
                    st.step(dve.max(top[a], lg[a]))
                    iu = gd[:, 4 + a].rearrange("p t h -> p (t h)").bitcast(U32)
                    fi = gd[:, 6 + a].rearrange("p t h -> p (t h)")
                    lm.mark(dve.tensor_scalar(nrm[:, 7, a:a + 1], top[a][:, 0:1], -1.0, None, ALU.mult))
                    st.step(dve.max_index(iu, top[a], lg[a]))
                    st.step(dve.tensor_copy(fi, iu))
                    st.step(dve.tensor_tensor(picks[a], iota_e[:].unsqueeze(1).to_broadcast([P, TOP_K, N_EXP]),
                                              wide(fi[:, 0:TOP_K], N_EXP), ALU.is_equal))
                    mr.mark(dve.reduce_sum(mask[a], picks[a].rearrange("p j e -> p e j"), AX_X))
                    dve.wait_ge(lg_exp, a + 1)
                    st.mark(dve.reciprocal(nrm[:, 7, 4 + a:5 + a], nrm[:, 7, 2 + a:3 + a]))
                    st.step(dve.tensor_tensor(shares[a], picks[a], wide(ex[a], N_EXP), ALU.mult))
                    st.step(dve.reduce_sum(gates[a], shares[a].rearrange("p j e -> p e j"), AX_X))
                    st.step(dve.tensor_scalar(gates[a], gates[a], nrm[:, 7, 4 + a:5 + a], None, ALU.mult))
                    continue
                if kind == "gdn":
                    t, m = a, MAT[a]
                    X, Y, Z = bank[2 * t], bank[2 * t + 1], bank[4]
                    if s in PE_STAGES:
                        dve.wait_ge(gdn_psum, PE_DONE[t, s])
                    if s == 1:
                        dve.wait_ge(emask_ready, t + 1)
                        st.mark(dve.tensor_tensor(m["N"], X[:], m["N"], ALU.mult))
                        st.mark(dve.tensor_tensor(m["L"], X[:], m["L"], ALU.mult))
                        gdn.mark(dve.tensor_tensor(m["A"], Y[:], m["A"], ALU.mult))
                    elif s == 2:
                        st.step(dve.tensor_copy(m["D"], X[:]))
                        st.step(dve.tensor_tensor(heads(m["G"]), heads(m["D"]), each_head(ident[:]), ALU.add))
                        gdn.mark(dve.tensor_tensor(heads(m["H"]), heads(Z[:]), wide(gd[:, 2, t], P), ALU.mult))
                    elif s == 3:
                        gdn.mark(dve.tensor_copy(m["F"], Y[:]))
                    elif s == 4:
                        st.step(dve.tensor_copy(m["D"], Y[:]))
                        gdn.mark(dve.tensor_tensor(m["G"], Z[:], m["G"], ALU.add))
                    elif s == 5:
                        gdn.mark(dve.tensor_tensor(m["G"], Z[:], m["G"], ALU.add))
                    elif s == 6:
                        gdn.mark(dve.tensor_tensor(m["G"], X[:], m["G"], ALU.add))
                    elif s == 7:
                        gdn.mark(dve.tensor_copy(m["D"], Y[:]))
                    elif s == "K":
                        st.step(dve.tensor_tensor(heads(m["I"]), heads(Y[:]), wide(gd[:, 10, t], P), ALU.mult))
                        gdn.mark(dve.tensor_tensor(m["H"], m["H"], m["I"], ALU.subtract))
                    elif s == 8:
                        st.step(dve.tensor_copy(m["F"], Y[:]))
                        gdn.mark(dve.tensor_copy(m["V"], Z[:]))
                    elif s == 9:
                        gdn.mark(dve.tensor_tensor(m["V"], Z[:], m["V"], ALU.add))
                    elif s == 10:
                        if t == 0:
                            st.mark(dve.tensor_tensor(heads(m["I"]), heads(Y[:]), wide(gd[:, 8, t], P), ALU.mult))
                        gdn.mark(dve.tensor_tensor(m["V"], X[:], m["V"], ALU.add))
                    elif s == 11:
                        gdn.mark(dve.tensor_tensor(m["V"], Y[:], m["V"], ALU.add))
                    elif s == 12:
                        if t == 0:
                            st.step(dve.tensor_copy(m["F"], Y[:]))
                            gdn.mark(dve.tensor_copy(m["D"], X[:]))
                        else:
                            st.step(dve.tensor_tensor(heads(m["F"]), heads(Y[:]), wide(gd[:, 7, t], P), ALU.mult))
                            gdn.mark(dve.tensor_tensor(m["D"], X[:], m["F"], ALU.add))
                    elif s == "M":
                        dve.wait_ge(gdn_act, ACT_DONE[t, "M"])
                        gdn.mark(dve.reduce_sum(nrm[:, 5, 4 * t:4 * t + 4], heads(m["E"]), AX_X))
                    elif s == "N":
                        dve.wait_ge(gdn_act, ACT_DONE[t, "N"])
                        dve.wait_ge(gsilu, 1)
                        st.step(dve.reciprocal(nrm[:, 6, 4 * t:4 * t + 4], nrm[:, 6, 4 * t:4 * t + 4]))
                        st.step(dve.tensor_tensor(heads(m["D"]), heads(m["D"]), wide(nrm[:, 6, 4 * t:4 * t + 4], P),
                                                  ALU.mult))
                        gdn.mark(dve.tensor_tensor(m["D"], m["D"], gate[:, t], ALU.mult))
                    elif s == 13:
                        gdn.mark(dve.tensor_scalar(mix_gdn[:, :, t * P:(t + 1) * P], heads(X[:]), col[:, 16:17],
                                                   None, ALU.mult))
                    continue
                g = a
                n = 4 if g < 2 else 2
                if kind == "S":
                    dve.wait_ge(s_psum, g + 1)
                    dve.wait_ge(ld_bias, 16)
                    if g >= 2:
                        dve.wait_ge(pt_psum, g - 1)
                    for r in range(2):
                        if g >= 2:
                            o_, i_ = sc[:, g % 2, r * S:(r + 1) * S], swa_s[r][:, 0:S]
                            b_ = bias[:, 2 * (g - 2) + r, :]
                        else:
                            o_ = heads(sc[:, g % 2], 4)[:, r:4:2, :]
                            i_ = swa_s[r][:, 0:S].rearrange("p (h j) -> p h j", h=2)
                            b_ = bias[:, 4 * g + r:4 * g + 4:2, P:2 * P]
                        st.step(dve.tensor_tensor(o_, i_, b_, ALU.add))
                    c0 = 8 * (g % 2)
                    st.step(dve.reduce_max(nrm[:, 4, c0:c0 + n], heads(sc[:, g % 2], n), AX_X))
                    sm.mark(dve.tensor_scalar(nrm[:, 4, c0:c0 + n], nrm[:, 4, c0:c0 + n], -1.0, None, ALU.mult))
                elif kind == "T":
                    n_exp += n
                    c0 = 16 + 8 * (g % 2)
                    dve.wait_ge(p_exp, n_exp)
                    st.step(dve.reciprocal(nrm[:, 4, c0:c0 + n], nrm[:, 4, c0:c0 + n]))
                    v = heads(sc[:, g % 2], n)
                    pr.mark(dve.tensor_tensor(v, v, wide(nrm[:, 4, c0:c0 + n], 512 // n), ALU.mult))
                else:
                    dve.wait_ge(o_psum, g + 1)
                    if g >= 2:
                        orr.mark(dve.tensor_copy(mix_swa[:, g - 2, P:2 * P], bank[7][:, 0:P]))
                    else:
                        orr.mark(dve.tensor_copy(mix_swa[:, 2 * g:2 * g + 2, 0:P],
                                                 bank[7][:, 0:S].rearrange("p (q i) -> p q i", q=2)))

            dve.wait_ge(cnt_psum, 1)
            nb = Tally(dve, nb_ready)
            cnt = bank[3][0:N_EXP, 0:1]
            st.step(dve.tensor_scalar(more, cnt, float(SLOTS), None, ALU.is_gt))
            for j in range(2, S // SLOTS):
                ins = dve.scalar_tensor_tensor(out=more, in0=cnt, scalar=float(j * SLOTS), in1=more,
                                               op0=ALU.is_gt, op1=ALU.add)
                (st.step if j < S // SLOTS - 1 else nb.mark)(ins)
            st.step(dve.scalar_tensor_tensor(out=rms, in0=bank[2][:, 0:T * N_EXP], scalar=ABSENT, in1=masks,
                                             op0=ALU.add, op1=ALU.mult))
            rmr = Tally(dve, rm_ready)
            rmr.step(dve.tensor_scalar(rms, rms, -ABSENT, None, ALU.add))
            for t in range(T):
                ins = dve.tensor_scalar(SEL[:, t, :], slot2[:, 0, :], rm[t][:, 0:1], None, ALU.is_equal)
            ins.then_inc(S_ready, 1)
            dve.tensor_copy(oh_cur, own[:, 0:1].to_broadcast([N_EXP, SLOTS])).then_inc(oh_ready, 1)
            dve.wait_ge(end_psum, 1)
            tr = Tally(dve, tab_ready)
            st.step(dve.tensor_scalar(col[0:N_EXP, 25:27], bank[3][0:N_EXP, 1:3], float(N_EXP), None, ALU.add))
            tr.mark(dve.tensor_scalar(nbl[0:1, MAXB:MAXB + 1], bank[3][0:1, 4:5], float(N_EXP), None, ALU.add))
            st.mark(dve.tensor_scalar(since, iota_b[:], beg, 1.0, ALU.subtract, ALU.add))
            st.step(dve.tensor_scalar(oh, iota_b[:], beg, None, ALU.is_ge))
            st.step(dve.scalar_tensor_tensor(out=oh, in0=iota_b[:], scalar=end, in1=oh, op0=ALU.is_lt,
                                             op1=ALU.mult))
            rt = Tally(dve, rt_ready)
            rt.step(dve.scalar_tensor_tensor(out=ohr, in0=since, scalar=-float(SLOTS), in1=oh, op0=ALU.mult,
                                             op1=ALU.mult))
            rt.mark(dve.tensor_tensor(oh, oh, own[:], ALU.add))
            dve.wait_ge(rt_psum, 1)
            rt.mark(dve.tensor_copy(rmT, bank[4][0:N_EXP, 0:S]))
            rt.mark(dve.tensor_copy(gT, bank[5][0:N_EXP, 0:S]))
            dve.wait_ge(tab_psum, 1)
            tr.mark(dve.tensor_copy(nbl[0:1, 0:MAXB], bank[4][0:1, 0:MAXB]))
            tr.mark(dve.tensor_copy(RM, bank[7][:, 0:T * MAXB].rearrange("p (t b) -> p t b", t=T)))
            tr.step(dve.tensor_copy(GB, bank[7][:, 128:128 + T * MAXB].rearrange("p (t b) -> p t b", t=T)))
            dve.wait_ge(xgT_psum, 1)
            dve.tensor_copy(xgT, bank[6][:]).then_inc(xgT_ready, 1)
            dve.memset(yb, 0.0).then_inc(zeroed, 1)
            dve.memset(SGT, 0.0).then_inc(zeroed, 1)
            n_blocks = dve.value_load(nbl[0:1, MAXB:MAXB + 1], min_val=N_EXP, max_val=NB_MAX)
            with dve.Fori(0, n_blocks) as b:
                dve.wait_ge(xg_psum, b + 1)
                for t in range(T):
                    ins = dve.tensor_scalar(SEL[:, t, :], slot2[:, 0, :], RM[:, t, bass.ds(b + 1, 1)], None,
                                            ALU.is_equal)
                ins.then_inc(S_ready, 1)
                for t in range(T):
                    ins = dve.tensor_scalar(SG[:, t, :], slot2[:].rearrange("p a s -> p (a s)"),
                                            RM[:, t, bass.ds(b, 1)], GB[:, t, bass.ds(b, 1)],
                                            ALU.is_equal, ALU.mult)
                ins.then_inc(SG_ready, 1)
                dve.wait_ge(wgu_used, 8 * b + 8)
                dve.tensor_scalar(gt, bank[4][:], LIMIT, None, ALU.min).then_inc(g_min, 1)
                dve.tensor_scalar(up, bank[5][:], LIMIT, -LIMIT, ALU.min, ALU.max).then_inc(dve_step, 1)
                dve.wait_ge(dve_step, 2 * b + (st.n + 1))
                dve.wait_ge(g_min, b + 1)
                dve.scalar_tensor_tensor(out=up, in0=up, scalar=1.0, in1=gt, op0=ALU.add,
                                         op1=ALU.mult).then_inc(dve_step, 1)
                dve.tensor_copy(oh_cur, oh[:, bass.ds(b + 1, 1)].to_broadcast([N_EXP, SLOTS])
                                ).then_inc(oh_ready, 1)
                dve.wait_ge(dve_step, 2 * b + (st.n + 2))
                dve.wait_ge(sig_ready, b + 1)
                dve.tensor_tensor(up, up, sg, ALU.mult).then_inc(act_ready, 1)
                dve.wait_ge(actT_psum, b + 1)
                dve.tensor_copy(actT, bank[4][:]).then_inc(actT_ready, 1)
                dve.wait_ge(xgT_psum, b + 2)
                dve.tensor_copy(xgT, bank[6][:]).then_inc(xgT_ready, 1)
            dve.wait_ge(acc_done, n_blocks + 1)
            for t in range(T):
                for hf in range(2):
                    v = hx[:, t, hf * 512:(hf + 1) * 512]
                    ins = dve.tensor_tensor(v, bank[2 * t + hf][:], v, ALU.add)
                ins.then_inc(out_ready, 1)

        @block.tensor
        def _(pe):
            mm, tp = pe.matmul, pe.transpose
            pe.wait_ge(consts, 17)
            xt = Tally(pe, xT_psum)
            for i in range(2 * T):
                t, q = divmod(i, 2)
                pe.wait_ge(xn_ready, t + 1)
                for k in range(4):
                    ins = tp(bank[i][:, k * P:(k + 1) * P], xn[:, t, (4 * q + k) * P:(4 * q + k + 1) * P],
                             ident[:])
                xt.mark(ins)
            z = Tally(pe, z_psum)

            def ring_bank(user):
                i = RING.index(user)
                if i >= 3:
                    pe.wait_ge(z_evac, i - 2)
                return bank[z_bank(user)]

            def take_bank7(user):
                i = BANK7.index(user)
                kind, a = BANK7[i - 1] if i else ("z", "f2")
                if kind == "z":
                    pe.wait_ge(z_evac, evacuated(a))
                else:
                    pe.wait_ge(pt_ready if kind == "T" else o_ready, a + 1)
                return bank[7]

            def unit(u):
                dst = take_bank7(("z", u)) if u in LATE_UNITS else ring_bank(u)
                if u == 0:
                    pe.wait_ge(ld_ba, 16)
                    for t in range(T):
                        for k in range(KT):
                            ins = mm(dst[:, 8 * t:8 * t + 8], xnT[:, k, t * P:(t + 1) * P], wba[:, k, :],
                                     start=k == 0, stop=k == KT - 1)
                    z.mark(ins)
                    return
                j, half = divmod(u - 1, 2)
                pe.wait_ge(ld_win[j % 4], 16 * (j // 4 + 1))
                w = piece(j)
                if j >= 3:
                    for k in range(KT):
                        ins = mm(dst[:], xnT[:, k, half * P:(half + 1) * P], w[:, k, :],
                                 start=k == 0, stop=k == KT - 1)
                else:
                    for c in range(2):
                        c0 = (2 * half + c) * P
                        for k in range(KT):
                            ins = mm(dst[:, c * S:(c + 1) * S], w[:, k, c0:c0 + P], xnT[:, k, :],
                                     start=k == 0, stop=k == KT - 1)
                z.mark(ins)

            pe.wait_ge(xnT_ready, 2 * T)
            unit(1)
            pe.wait_ge(ld_rel, 48)
            pe.wait_ge(rel_one, 1)
            mm(bank[4][0:HS, 0:TW], rel[:], dtab, start=True, stop=True)
            Tally(pe, dist_psum).mark(tp(bank[4][:, TW:TW + CONV_K * 12], cw_rows, ident[0:CONV_K * 12, 0:CONV_K * 12]))
            unit(0)
            unit(2)
            pe.wait_ge(g_ready, T)
            pe.wait_ge(cw_ready, 1)
            for t in range(T):
                mm(bank[4][:, 4 * t:4 * t + 4], ucum[:], gd[:, 9, t], start=True, stop=True)
                ins = mm(bank[4][:, 8 + 4 * t:12 + 4 * t], ones[:], gd[:, 9, t], start=True, stop=True)
            Tally(pe, gc_psum).mark(ins)
            unit(3)
            gr = Tally(pe, gcrow_psum)
            for t in range(T):
                pe.wait_ge(ug_ready, HG * (t + 1))
                gr.mark(mm(bank[t][:], ones[:], ug[:, t, :], start=True, stop=True))
            l2 = Tally(pe, l2_psum)

            def l2_sum(u):
                pe.wait_ge(gap_ready, 3)
                pe.wait_ge(l2_sq, u + 1)
                l2.mark(mm(bank[u][:], ones[:], sc[:, u % 2], start=True, stop=True))

            for u in (4, 5):
                unit(u)
            l2_sum(0)
            l2_sum(1)
            unit(6)
            l2_sum(2)
            l2_sum(3)

            qt = Tally(pe, qkT_psum)
            gdn = Tally(pe, gdn_psum)
            sp_, pp, op = Tally(pe, s_psum), Tally(pe, pt_psum), Tally(pe, o_psum)
            kT = lambda t, h: conv[:, HG + h, t * P:(t + 1) * P]
            qT = lambda t, h: conv[:, h, t * P:(t + 1) * P]
            vT = lambda t, h: conv[:, 2 * HG + h, t * P:(t + 1) * P]
            hp = Tally(pe, h_psum)

            def project(i, ks):
                t, hf = divmod(i, 2)
                for k in ks:
                    lhsT = mix_gdn[:, k] if k < HG else mix_swa[:, k - HG]
                    last = mm(bank[H_BANK[i]][:], lhsT[:, t * P:(t + 1) * P],
                              wout[:, k, hf * 512:(hf + 1) * 512], start=k == HG, stop=k == HG - 1)
                return last

            ht, lp = Tally(pe, hT_psum), Tally(pe, lg_psum)
            for kind, a, s in ORDER:
                if kind == "z":
                    unit(a)
                    if a == 7:
                        pe.wait_ge(l2_done, 4)
                    continue
                if kind in "nARG":
                    continue
                if kind == "f":
                    pe.wait_ge(swa_normed, a + 1)
                    dst = ring_bank(f"f{a}")
                    for c in range(4):
                        ins = tp(dst[:, c * P:(c + 1) * P], zswa[:, a, c * P:(c + 1) * P], ident[:])
                    qt.mark(ins)
                    continue
                if kind == "W":
                    if a == 0:
                        pe.wait_ge(ld_wout, 16)
                        pe.wait_ge(o_ready, 2)
                        pe.wait_ge(gdn_dve, DVE_DONE[0, 13])
                    if a == 2:
                        pe.wait_ge(o_ready, 6)
                        pe.wait_ge(s_max, 6)
                    ins = project(a, range(HG, KT))
                    if a < 2:
                        hp.mark(project(a, range(HG)))
                    continue
                if kind == "X":
                    pe.wait_ge(gdn_dve, DVE_DONE[1, 13])
                    hp.mark(project(a, range(HG)))
                    continue
                if kind == "L":
                    for q in range(2):
                        pe.wait_ge(hn_ready, 2 * a + q + 1)
                        for k in range(4):
                            c = (4 * q + k) * P
                            ins = tp(bank[2 * a + q][:, k * P:(k + 1) * P], hn[:, a, c:c + P], ident[:])
                        ht.mark(ins)
                    pe.wait_ge(ld_wr, 16)
                    for k in range(KT):
                        if k % 4 == 0:
                            pe.wait_ge(hnT_ready, 2 * a + 1 + (k == 4))
                        ins = mm(bank[2 * a][:, 0:N_EXP], hnT[:, k, a * P:(a + 1) * P], wr[:, k, :],
                                 start=k == 0, stop=k == KT - 1)
                    lp.mark(ins)
                    continue
                if kind == "gdn" and s not in PE_STAGES:
                    continue
                if kind == "gdn":
                    t, m = a, MAT[a]
                    X, Y, Z = bank[2 * t], bank[2 * t + 1], bank[4]
                    at = GDN_SEQ.index((t, s))
                    before = [q for q in GDN_SEQ[:at] if q[0] == t or s in SHARED_BANK_STAGES]
                    if before:
                        pe.wait_ge(gdn_dve, DVE_DONE[before[-1]])
                        if ACT_DONE[before[-1]]:
                            pe.wait_ge(gdn_act, ACT_DONE[before[-1]])

                    def product(dst, lhsT, rhs, start=True, stop=True):
                        for h in range(HG):
                            c = slice(h * P, (h + 1) * P)
                            last = mm(dst[:, c], lhsT(h) if callable(lhsT) else lhsT[:, c],
                                      rhs(h) if callable(rhs) else rhs[:, c], start=start, stop=stop)
                        return last

                    def flip(dst, src):
                        for h in range(HG):
                            c = slice(h * P, (h + 1) * P)
                            last = tp(dst[:, c], src(h) if callable(src) else src[:, c], ident[:])
                        return last

                    kt, qt_, vt = (lambda h, f=f: f(t, h) for f in (kT, qT, vT))
                    if s == 1:
                        product(X, kt, kt)
                        ins = product(Y, kt, qt_)
                    elif s == 2:
                        flip(X, m["N"])
                        pe.wait_ge(silu_ready, 6)
                        ins = flip(Z, vt)
                    elif s == 3:
                        product(X, m["D"], m["N"])
                        ins = product(Y, m["N"], m["D"])
                    elif s == 4:
                        product(X, m["F"], m["E"])
                        product(Y, m["E"], m["F"])
                        ins = product(Z, m["E"], m["G"])
                    elif s == 5:
                        product(X, m["D"], m["N"])
                        ins = product(Z, m["N"], m["G"])
                    elif s == 6:
                        ins = product(X, m["E"], m["G"])
                    elif s == 7:
                        product(X, m["G"], m["L"])
                        ins = product(Y, m["L"], m["G"])
                    elif s == "K":
                        ins = product(Y, kt, MAT[0]["F"])
                    elif s == 8:
                        product(X, m["D"], m["N"])
                        product(Y, m["N"], m["D"])
                        ins = product(Z, m["G"], m["H"])
                    elif s == 9:
                        product(X, m["E"], m["F"])
                        ins = product(Z, m["D"], m["V"])
                    elif s == 10:
                        if t == 0:
                            flip(Y, kt)
                        ins = product(X, m["F"], m["V"])
                    elif s == 11:
                        ins = product(Y, m["N"], m["V"])
                    elif s == 12:
                        product(X, m["A"], m["V"])
                        if t == 0:
                            ins = product(Y, m["I"], m["V"])
                        else:
                            ins = product(Y, qt_, MAT[0]["F"])
                    elif s == 13:
                        ins = flip(X, m["D"])
                    gdn.mark(ins)
                    continue
                g = a
                if kind == "S":
                    pe.wait_ge(z_evac, len(RING))
                    if g >= 1:
                        pe.wait_ge(s_max, g)
                    for i in range(2 if g >= 2 else 4):
                        r = i % 2
                        pair, qt0, n = (g - 2, 1, S) if g >= 2 else (2 * g + i // 2, 0, P)
                        c0 = 0 if g >= 2 else (i // 2) * P
                        ins = mm(swa_s[r][:, c0:c0 + n], qkT[DH * r:DH * (r + 1), 0, pair, qt0 * P:(qt0 + 1) * P],
                                 qkT[DH * r:DH * (r + 1), 1, pair, 0:n], start=True, stop=True)
                    sp_.mark(ins)
                elif kind == "T":
                    pe.wait_ge(p_ready, g + 1)
                    take_bank7((kind, g))
                    for c in range(4):
                        ins = tp(bank[7][:, c * P:(c + 1) * P], sc[:, g % 2, c * P:(c + 1) * P], ident[:])
                    pp.mark(ins)
                else:
                    pe.wait_ge(pt_ready, g + 1)
                    take_bank7((kind, g))
                    if g >= 2:
                        for r in range(2):
                            h = 2 * (g - 2) + r
                            for j in range(2):
                                ins = mm(bank[7][DH * r:DH * (r + 1), 0:P], zswa[:, 4 + j, h * DH:(h + 1) * DH],
                                         pt[:, g % 2, (2 * r + j) * P:(2 * r + j + 1) * P],
                                         start=j == 0, stop=j == 1)
                    else:
                        for i in range(4):
                            h, r = 4 * g + i, i % 2
                            ins = mm(bank[7][DH * r:DH * (r + 1), (i // 2) * P:(i // 2 + 1) * P],
                                     zswa[:, 4, h * DH:(h + 1) * DH], pt[:, g % 2, i * P:(i + 1) * P],
                                     start=True, stop=True)
                    op.mark(ins)

            pe.wait_ge(mask_ready, T)
            mm(bank[2][:, 0:32], ustr[:], mask[0], start=True, stop=True)
            mm(bank[2][:, 32:64], ustr[:], mask[1], start=True, stop=False)
            mm(bank[2][:, 32:64], ones[:], mask[0], start=False, stop=True)
            for t in range(T):
                ins = mm(bank[3][0:N_EXP, 0:1], mask[t], ones[:, 0:1], start=t == 0, stop=t == T - 1)
            Tally(pe, cnt_psum).mark(ins)

            def gather():
                for t in range(T):
                    for hf in range(2):
                        last = mm(bank[6][SLOTS * hf:SLOTS * (hf + 1), :], SEL[:, t, :],
                                  hn[:, t, hf * 512:(hf + 1) * 512], start=t == 0, stop=t == T - 1)
                last.then_inc(xg_psum, 1)

            def gather_flip():
                for c in range(4):
                    last = tp(bank[6][:, c * P:(c + 1) * P], xg[:, c * P:(c + 1) * P], ident[:])
                last.then_inc(xgT_psum, 1)

            pe.wait_ge(nb_ready, 1)
            pe.wait_ge(rm_ready, 1)
            mm(bank[3][0:N_EXP, 1:2], ucum[0:N_EXP, 0:N_EXP], more, start=True, stop=True)
            mm(bank[3][0:N_EXP, 2:3], ustr[0:N_EXP, 0:N_EXP], more, start=True, stop=True)
            Tally(pe, end_psum).mark(mm(bank[3][0:1, 4:5], ones[0:N_EXP, 0:1], more, start=True, stop=True))
            for t in range(T):
                tp(bank[4][0:N_EXP, t * P:(t + 1) * P], rm[t], ident[:])
            pe.wait_ge(S_ready, 1)
            for t in range(T):
                ins = tp(bank[5][0:N_EXP, t * P:(t + 1) * P], gates[t], ident[:])
            Tally(pe, rt_psum).mark(ins)
            gather()
            pe.wait_ge(rt_ready, 4)
            mm(bank[4][0:1, 0:MAXB], col[0:N_EXP, 8:9], oh, start=True, stop=True)
            for t in range(T):
                c = slice(t * MAXB, (t + 1) * MAXB)
                mm(bank[7][:, c], rmT[:, t * P:(t + 1) * P], oh, start=True, stop=False)
                mm(bank[7][:, c], ones[0:N_EXP, :], ohr, start=False, stop=True)
                ins = mm(bank[7][:, 128 + t * MAXB:128 + (t + 1) * MAXB], gT[:, t * P:(t + 1) * P], oh,
                         start=True, stop=True)
            Tally(pe, tab_psum).mark(ins)
            pe.wait_ge(ld_moe, 32)
            for t in range(T):
                for hf in range(2):
                    mm(bank[2 * t + hf][:], gT[:, t * P:(t + 1) * P], bdn[:, hf * 512:(hf + 1) * 512],
                       start=True, stop=False, skip_group_check=True)
            pe.wait_ge(xg_ready, 1)
            gather_flip()

            def combine():
                for t in range(T):
                    for hf in range(2):
                        last = mm(bank[2 * t + hf][:], SGT[SLOTS * hf:SLOTS * (hf + 1), t * P:(t + 1) * P],
                                  yb[SLOTS * hf:SLOTS * (hf + 1), :], start=False, stop=False,
                                  skip_group_check=True)
                last.then_inc(acc_done, 1)

            n_blocks = pe.value_load(nbl[0:1, MAXB:MAXB + 1], min_val=N_EXP, max_val=NB_MAX)

            def gate_up(b):
                pe.wait_ge(xgT_ready, b + 1)
                pe.wait_ge(oh_ready, b + 1)
                order = [(bank[4], 0, 0), (bank[4], 1, 512), (bank[5], 0, 1024), (bank[5], 1, 1536)]
                for dst, hf, c0 in order:
                    mm(dst[SLOTS * hf:SLOTS * (hf + 1), :], oh_cur, bgu[:, c0:c0 + 512], start=True, stop=False)
                for k in range(KT):
                    pe.wait_ge(ld_slot[k], 16 * (b + 1))
                    c = (k % 4) * P + (k // 4) * SLOTS
                    for dst, hf, c0 in order:
                        last = mm(dst[SLOTS * hf:SLOTS * (hf + 1), :], xgT[:, c:c + SLOTS],
                                  ring[:, k, c0:c0 + 512], start=False, stop=k == KT - 1)
                    last.then_inc(wgu_used, 1)

            def rest(b):
                pe.wait_ge(SG_ready, b + 1)
                for t in range(T):
                    last = tp(bank[7][:, t * P:(t + 1) * P], SG[:, t, :], ident[:])
                last.then_inc(SGT_psum, 1)
                pe.wait_ge(S_ready, b + 2)
                gather()
                pe.wait_ge(act_ready, b + 1)
                for c in range(4):
                    last = tp(bank[4][:, c * P:(c + 1) * P], up[:, c * P:(c + 1) * P], ident[:])
                last.then_inc(actT_psum, 1)
                pe.wait_ge(xg_ready, b + 2)
                gather_flip()
                pe.wait_ge(actT_ready, b + 1)
                pe.wait_ge(SGT_ready, b + 1)
                for f in range(KT):
                    if f % 2 == 0:
                        pe.wait_ge(ld_slot[8 + f // 2], 16 * (b + 1))
                    w = ring[:, 8 + f // 2, (f % 2) * D:(f % 2 + 1) * D]
                    c = (f % 4) * P + (f // 4) * SLOTS
                    for hf in range(2):
                        last = mm(bank[7][SLOTS * hf:SLOTS * (hf + 1), :], actT[:, c:c + SLOTS],
                                  w[:, hf * 512:(hf + 1) * 512], start=f == 0, stop=f == KT - 1)
                    if f % 2:
                        last.then_inc(wdn_used, 1)

            pe.wait_ge(zeroed, 2)
            with pe.Fori(0, n_blocks) as b:
                gate_up(b)
                pe.wait_ge(y_ready, b + 1)
                combine()
                rest(b)
            pe.wait_ge(y_ready, n_blocks + 1)
            combine()


_INS = ["x", "norm1_w", "w_in", "conv_w", "a_log", "dt_bias", "gdn_norm_w", "q_norm_w", "k_norm_w", "rel_bias",
        "w_out", "norm2_w", "w_router", "b_router", "w_gate_up", "b_gate_up", "w_down", "b_down"]


def kernel(**inputs):
    import numpy as _np
    import concourse.bacc as _bacc
    from concourse import mybir as _mybir
    from concourse.bass_utils import run_bass_kernel_spmd as _run

    nc = _bacc.Bacc("TRN2", target_bir_lowering=False, num_devices=1)
    arrays, args = {}, []
    for name in _INS + ["dist_table"]:
        a = distance_table(inputs["x"].shape[1]) if name == "dist_table" else inputs[name]
        a = _np.ascontiguousarray(a)
        arrays[f"in_{name}_dram"] = a
        args.append(nc.dram_tensor(f"in_{name}_dram", a.shape, _mybir.dt.from_np(a.dtype), kind="ExternalInput").ap())
    shape = inputs["x"].shape
    args.append(nc.dram_tensor("out_dram", shape, _mybir.dt.float32, kind="ExternalOutput").ap())
    hybrid_layer(nc, *args)
    r = _run(nc, [arrays], core_ids=[0])
    return r.results[0]["out_dram"]
```

```python
import math
from contextlib import ExitStack

import concourse.bass as bass
import numpy as np
from concourse import mybir

ALU = mybir.AluOpType
ACT = mybir.ActivationFunctionType
AX_X = mybir.AxisListType.X
F32 = mybir.dt.float32
I32 = mybir.dt.int32
U32 = mybir.dt.uint32

P = 128
EPS = 1e-6
HG, DK = 4, 128
HS, DH = 8, 64
CONV_K = 4
BRANCHES = ((128, 1), (512, 4), (2048, 16))
REL_BUCKETS, REL_MAX_DIST = 32, 2048
N_EXP, TOP_K = 32, 4
LIMIT, ALPHA = 7.0, 1.702
EARLY_BLOCKS = 8
SLOTS = 64
MASKED = -1e30
ABSENT = 1024.0


def distance_table(seq):
    dist = seq - 1 - np.arange(seq + P)
    near = REL_BUCKETS // 2
    n = np.maximum(dist, 0)
    far = near + (np.log(np.maximum(n, 1) / near) / math.log(REL_MAX_DIST / near)
                  * (REL_BUCKETS - near)).astype(np.int32)
    bucket = np.where(n < near, n, np.minimum(far, REL_BUCKETS - 1))
    held = sum(((dist % dil == 0) & (dist <= window)).astype(np.int32) for window, dil in BRANCHES)
    held = np.where(dist < 0, 0, held)
    table = np.zeros((REL_BUCKETS + 1, seq + P), np.float32)
    table[bucket, np.arange(seq + P)] = 1.0
    table[REL_BUCKETS] = np.where(held > 0, np.log(np.maximum(held, 1)), MASKED)
    return table


RING = [1, 0, *range(2, 12), "f0", "f1", "f2", "f3"]
LATE_UNITS = {12: 4, 13: 7, 14: 4}


def attention_order():
    text = ("z7 01 11 z8 02 12 z9 03 13 z10 04 14 n0 z11 05 f0 f1 15 f2 f3 06 z12 16 07 S0 17 S1 08 "
            "y13 09 0A z13 y14 T0 0B O0 T1 S2 0C z14 1K S3 O1 18 T2 0M s0 O2 T3 0N 19 S4 0D 1A O3 S5 "
            "W0 T4 X0 O4 1B W1 T5 1C X1 1M A0 O5 W2 1N R0 1D L0 W3 G0 X2 B0 X3 C0 A1 R1 L1 G1")
    names = {str(i): i for i in range(10)} | {"A": 10, "B": 11, "C": 12, "D": 13, "K": "K", "M": "M", "N": "N"}
    return [("gdn", int(w[0]), names[w[1]]) if w[0] in "01" else (w[0], int(w[1:]), None)
            for w in text.split()]


ORDER = attention_order()
PE_STAGES = {1, 2, 3, 4, 5, 6, 7, "K", 8, 9, 10, 11, 12, 13}
DVE_STAGES = PE_STAGES | {"M", "N"}
ACT_STAGES = {3, 4, 5, 7, 8, 9, "M", "N"}
BANK4_STAGES = {2, 4, 5, 8, 9}
BANK4 = [step for step in ORDER if (step[0] == "gdn" and step[2] in BANK4_STAGES)
         or (step[0] == "z" and LATE_UNITS.get(step[1]) == 4)]
BANK7 = [step for step in ORDER if step[0] in "TO" or (step[0] == "z" and LATE_UNITS.get(step[1]) == 7)]


def stage_counts(stages):
    n, out = 0, {}
    for kind, t, s in ORDER:
        if kind == "gdn":
            n += s in stages
            out[t, s] = n
    return out


PE_DONE, DVE_DONE, ACT_DONE = (stage_counts(x) for x in (PE_STAGES, DVE_STAGES, ACT_STAGES))
GDN_SEQ = [(t, s) for kind, t, s in ORDER if kind == "gdn"]


def evacuated(user):
    return (RING + list(LATE_UNITS)).index(user) + 1


def z_bank(user):
    return LATE_UNITS[user] if user in LATE_UNITS else 5 + RING.index(user) % 3


class Tally:

    def __init__(self, eng, sem):
        self.eng, self.sem, self.n = eng, sem, 0

    def mark(self, ins):
        ins.then_inc(self.sem, 1)
        self.n += 1

    def step(self, ins):
        self.mark(ins)
        self.eng.wait_ge(self.sem, self.n)


def hybrid_layer(nc, x, norm1_w, w_in, conv_w, a_log, dt_bias, gdn_norm_w, q_norm_w, k_norm_w,
                 rel_bias, w_out, norm2_w, w_router, b_router, w_gate_up, b_gate_up, w_down,
                 b_down, dist_table, out):
    S, D = x.shape[1], x.shape[2]
    T = S // P
    KT = D // P
    C_GDN = 3 * HG * DK
    C_GATE, C_BA = C_GDN, C_GDN + HG * DK
    C_SWA = C_BA + 2 * HG
    MAXB = N_EXP + (S * TOP_K - N_EXP) // SLOTS + 1
    assert T == 2 and D == 1024 and w_in.shape[2] == C_SWA + 3 * HS * DH
    NB_MAX = MAXB - 1
    TW = S + P

    with ExitStack() as ctx:
        def sb(name, shape, dt=F32):
            return ctx.enter_context(nc.sbuf_tensor(name, shape, dt))

        def sem(name):
            return ctx.enter_context(nc.semaphore(name))

        SLOT = 2048
        ZPAD, ZSWA, MATS = 12 * (S + 4), 3 * T * 512, 6 * 512
        store = sb("store", [P, 4 * SLOT + ZPAD + ZSWA + MATS + 10 * SLOT])
        REST = 4 * SLOT + ZPAD + ZSWA + MATS
        END = REST + 8 * SLOT
        assert ZPAD + ZSWA + MATS >= 4 * SLOT + 3 * S
        hx = sb("hx", [P, T, D])
        arena1 = sb("arena1", [P, T, D])
        arena2 = store[:, END:END + KT * S].rearrange("p (k s) -> p k s", k=KT)
        nw = store[:, END + SLOT:END + SLOT + D]
        zswa = store[:, 4 * SLOT + ZPAD:4 * SLOT + ZPAD + ZSWA].rearrange("p (u n) -> p u n", n=512)
        qkT = sb("qkT", [P, 2, HS // 2, S])
        zpad = store[:, 4 * SLOT:4 * SLOT + ZPAD].rearrange("p (c s) -> p c s", c=12)
        conv = sb("conv", [P, 12, S])
        gate = sb("gate", [P, T, HG * DK])
        bias = sb("bias", [P, HS, S])
        sc = sb("sc", [P, 2, 512])
        pt = store[:, END + SLOT + D:END + 2 * SLOT].rearrange("p (g n) -> p g n", g=2)
        mats = store[:, REST - MATS:REST].rearrange("p (m n) -> p m n", n=512)
        ident = sb("ident", [P, P])
        ones = sb("ones", [P, P])
        ucum = sb("ucum", [P, P])
        ustr = sb("ustr", [P, P])
        m_in = sb("m_in", [P, P])
        m_out = sb("m_out", [P, P])
        slot2 = sb("slot2", [P, 2, SLOTS])
        iota_e = sb("iota_e", [P, N_EXP])
        iota_b = sb("iota_b", [N_EXP, MAXB])
        col = sb("col", [P, 64])
        ba = sb("ba", [P, T, 2 * HG])
        gd = sb("gd", [P, 12, T, HG])
        wba = sb("wba", [P, KT, 2 * HG])
        brt = sb("brt", [P, N_EXP])
        own = sb("own", [N_EXP, MAXB])
        cw = sb("cw", [P, CONV_K, 12])
        nrm = sb("nrm", [P, 8, 32])
        rel = sb("rel", [REL_BUCKETS + 1, HS])
        parity = sb("parity", [1, MAXB], I32)
        nbl = sb("nbl", [1, 64], I32)

        xn, hn = arena1, arena1
        xnT, hnT = arena2, arena2
        mix_gdn, mix_swa = arena2[:, 0:HG], conv[:, 2 * HG:3 * HG]
        ug = arena1[:, 0, :].rearrange("p (t n) -> p t n", t=T)
        a1m = arena1[:].rearrange("p t d -> p (t d)").rearrange("p (m n) -> p m n", n=512)
        zpm = store[:, 4 * SLOT:4 * SLOT + 6 * 512].rearrange("p (m n) -> p m n", n=512)
        MAT = [dict(N=mats[:, 3 * t + 0], L=mats[:, 3 * t + 1], A=mats[:, 3 * t + 2],
                    D=zpm[:, 3 * t + 0], E=zpm[:, 3 * t + 1], F=zpm[:, 3 * t + 2],
                    G=a1m[:, 2 * t], H=a1m[:, 2 * t + 1], I=zswa[:, t], V=zswa[:, 2 + t])
               for t in range(T)]
        cw_rows = mats[0:CONV_K * 12, 5, 0:P]
        fdist = pt[0:HS, 0, 0:TW]
        dtab = pt[0:REL_BUCKETS + 1, 1, 0:TW]
        wout = store[:, REST + 4 * SLOT:REST + 8 * SLOT].rearrange("p (k n) -> p k n", n=D)
        bgu = bias[0:N_EXP].rearrange("p h s -> p (h s)")
        bdn = gate[0:N_EXP].rearrange("p t d -> p (t d)")
        wr = sc[:, 0, 0:KT * N_EXP].rearrange("p (k e) -> p k e", e=N_EXP)
        cv = conv[:].rearrange("p c s -> p (c s)").rearrange("p (m n) -> p m n", n=512)
        xg, xgT, gt, up, sg, actT = (cv[:, m] for m in range(6))
        qk = qkT[:].rearrange("p a b s -> p (a b s)").rearrange("p (m n) -> p m n", n=512)
        yb = qk[:, 0]
        SGT = qk[:, 1, 0:S]
        SEL = qk[:, 1, S:S + T * SLOTS].rearrange("p (t s) -> p t s", t=T)
        oh_cur = qk[0:N_EXP, 1, S + T * SLOTS:S + T * SLOTS + SLOTS]
        SG = qk[:, 2, 0:T * 2 * SLOTS].rearrange("p (t s) -> p t s", t=T)
        RM = qk[:, 2, 256:256 + T * MAXB].rearrange("p (t b) -> p t b", t=T)
        GB = qk[:, 2, 256 + T * MAXB:256 + 2 * T * MAXB].rearrange("p (t b) -> p t b", t=T)
        r3 = qk[:, 3]
        late = store[:, REST - 3 * S:REST]
        top = [r3[:, 16 * t:16 * t + 8] for t in range(T)]
        ex = [r3[:, 16 * t + 8:16 * t + 8 + TOP_K] for t in range(T)]
        picks = [r3[:, 64 + 128 * t:192 + 128 * t].rearrange("p (j e) -> p j e", j=TOP_K) for t in range(T)]
        shares = [late[:, 128 * t:128 * t + 128].rearrange("p (j e) -> p j e", j=TOP_K) for t in range(T)]
        lg = [r3[:, 320 + 32 * t:352 + 32 * t] for t in range(T)]
        mask = [r3[:, 384 + 32 * t:416 + 32 * t] for t in range(T)]
        rm = [r3[:, 448 + 32 * t:480 + 32 * t] for t in range(T)]
        masks, rms = r3[:, 384:448], r3[:, 448:512]
        gates = [qk[:, 2, 32 * t:32 * t + 32] for t in range(T)]
        oh, ohr, since = r3[0:N_EXP, 0:MAXB], r3[0:N_EXP, 64:64 + MAXB], r3[0:N_EXP, 128:128 + MAXB]
        rmT, gT = late[0:N_EXP, S:2 * S], late[0:N_EXP, 2 * S:3 * S]
        more, end, beg = (col[0:N_EXP, c:c + 1] for c in (24, 25, 26))

        bank = [ctx.enter_context(nc.psum_tensor(f"bank{i}", [P, 512], F32)) for i in range(8)]
        swa_s = [bank[5], bank[6]]

        fd_dram = nc.dram_tensor("bias_by_distance", [HS, P, TW], F32, kind="Internal").ap()

        ld_x = [sem(f"ld_x{t}") for t in range(T)]
        ld_nw, ld_ba, ld_small, ld_rel = (sem(n) for n in ("ld_nw", "ld_ba", "ld_small", "ld_rel"))
        ld_win = [sem(f"ld_win{i}") for i in range(4)]
        ld_wout, ld_nw2, ld_wr, ld_moe = sem("ld_wout"), sem("ld_nw2"), sem("ld_wr"), sem("ld_moe")
        ld_slot = [sem(f"ld_slot{i}") for i in range(12)]
        st_dist, ld_bias, st_out = sem("st_dist"), sem("ld_bias"), sem("st_out")
        consts, rel_one = sem("consts"), sem("rel_one")
        dve_step, act_step, pool_step = sem("dve_step"), sem("act_step"), sem("pool_step")
        x_sq, xn_ready, xT_psum, xnT_ready = sem("x_sq"), sem("xn_ready"), sem("xT_psum"), sem("xnT_ready")
        dist_psum, dist_ready, cw_ready = (sem(n) for n in ("dist_psum", "dist_ready", "cw_ready"))
        z_psum, z_evac = sem("z_psum"), sem("z_evac")
        dec_dve, dec_act, g_ready, ug_ready = sem("dec_dve"), sem("dec_act"), sem("g_ready"), sem("ug_ready")
        gc_psum, gcrow_psum, gap_ready, e_ready, emask_ready = (
            sem(n) for n in ("gc_psum", "gcrow_psum", "gap_ready", "e_ready", "emask_ready"))
        swa_sq, swa_ss, swa_root, swa_normed = sem("swa_sq"), sem("swa_ss"), sem("swa_root"), sem("swa_normed")
        qkT_psum = sem("qkT_psum")
        conv_ready, silu_ready, gsilu = sem("conv_ready"), sem("silu_ready"), sem("gsilu")
        l2_sq, l2_psum, l2_root, l2_done = sem("l2_sq"), sem("l2_psum"), sem("l2_root"), sem("l2_done")
        gdn_psum, gdn_dve, gdn_act = sem("gdn_psum"), sem("gdn_dve"), sem("gdn_act")
        s_psum, s_max, p_exp, p_ready, pt_psum, pt_ready, o_psum, o_ready = (
            sem(n) for n in ("s_psum", "s_max", "p_exp", "p_ready", "pt_psum", "pt_ready", "o_psum", "o_ready"))
        h_psum, h_ready, h_sq, hn_ready, hT_psum, hnT_ready = (
            sem(n) for n in ("h_psum", "h_ready", "h_sq", "hn_ready", "hT_psum", "hnT_ready"))
        lg_psum, lg_max, lg_exp, mask_ready, gates_ready, gT_psum, gT_ready = (
            sem(n) for n in ("lg_psum", "lg_max", "lg_exp", "mask_ready", "gates_ready", "gT_psum", "gT_ready"))
        cnt_psum, nb_ready, end_psum, rm_ready, rt_psum, rt_ready, tab_psum, tab_ready = (
            sem(n) for n in ("cnt_psum", "nb_ready", "end_psum", "rm_ready", "rt_psum", "rt_ready", "tab_psum",
                             "tab_ready"))
        w_used = sem("w_used")
        wgu_used, wdn_used = sem("wgu_used"), sem("wdn_used")
        g_min, sig_ready, act_ready, actT_psum, actT_ready = (
            sem(n) for n in ("g_min", "sig_ready", "act_ready", "actT_psum", "actT_ready"))
        S_ready, SG_ready, oh_ready, SGT_psum, SGT_ready = (
            sem(n) for n in ("S_ready", "SG_ready", "oh_ready", "SGT_psum", "SGT_ready"))
        zeroed, xg_psum, xg_ready, xgT_psum, xgT_ready, y_ready, acc_done, out_ready = (
            sem(n) for n in ("zeroed", "xg_psum", "xg_ready", "xgT_psum", "xgT_ready", "y_ready", "acc_done",
                             "out_ready"))

        block = ctx.enter_context(nc.Block())

        win = w_in[0].rearrange("(k p) n -> p k n", p=P)
        PIECES = [512, 0, 1024, C_SWA, C_SWA + 512, C_SWA + 1024, C_GATE]
        CONV_AT = {1: 4, 2: 6, 3: 0, 4: 2, 5: 8, 6: 10}
        H_BANK = [0, 1, 5, 6]

        def slot_at(slot, odd=0):
            if slot < 4:
                return slot * SLOT + odd * 4 * SLOT
            if slot < 6:
                return REST + (slot - 4) * SLOT + odd * 8 * SLOT
            return REST + (slot - 4) * SLOT

        def piece(j):
            at = slot_at(2 * (j % 4))
            return store[:, at:at + 2 * SLOT].rearrange("p (k n) -> p k n", n=512)

        def heads(ap, h=HG):
            return ap.rearrange("p (h n) -> p h n", h=h)

        def wide(cols, n):
            return cols.unsqueeze(2).to_broadcast([cols.shape[0], cols.shape[1], n])

        def each_head(mask):
            return mask.unsqueeze(1).to_broadcast([P, HG, P])

        def expert_tile(e_ap, slot):
            if slot < 8:
                src = w_gate_up[0][e_ap, slot * P:(slot + 1) * P, :]
                return src.rearrange("a p n -> p (a n)")
            s = slot - 8
            src = w_down[0][e_ap, 2 * s * P:2 * (s + 1) * P, :]
            return src.rearrange("a (j p) n -> p (a j) n", p=P)

        def slot_dst(slot, odd=0):
            dst = store[:, bass.ds(slot_at(slot, odd), SLOT)]
            return dst if slot < 8 else dst.rearrange("p (j n) -> p j n", n=D)

        @block.sync
        def _(sp):
            sp.dma_start(hx[:, 0, :], x[0, 0:P, :]).then_inc(ld_x[0], 16)
            sp.dma_start(nw[:], norm1_w.to_broadcast([P, D])).then_inc(ld_nw, 16)
            sp.dma_start(hx[:, 1, :], x[0, P:2 * P, :]).then_inc(ld_x[1], 16)
            sp.dma_start(dtab, dist_table).then_inc(ld_rel, 16)
            sp.dma_start(cw_rows, conv_w[0].rearrange("i (c p) -> (i c) p", p=P)).then_inc(ld_rel, 16)
            for j, c0 in enumerate(PIECES):
                if j >= 4:
                    sp.wait_ge(z_psum, 2 * (j - 4) + 3)
                sp.dma_start(piece(j), win[:, :, c0:c0 + 512]).then_inc(ld_win[j % 4], 16)
                if j == 3:
                    sp.wait_ge(dist_ready, 1)
                    sp.dma_start(fd_dram, fdist.unsqueeze(1).to_broadcast([HS, P, TW])).then_inc(st_dist, 16)
                if j == 4:
                    sp.wait_ge(st_dist, 16)
                    sp.dma_start(bias[:], bass.AP(fd_dram.tensor, S - 1 - P, [[TW - 1, P], [P * TW, HS], [1, S]])
                                 ).then_inc(ld_bias, 16)
                    sp.dma_start(wout, w_out[0].rearrange("(k p) n -> p k n", p=P)).then_inc(ld_wout, 16)
            for s in (6, 7, 0, 1, 2, 3, 4, 5):
                j = 3 if s >= 6 else 4 + s // 2
                sp.wait_ge(z_psum, 2 * j + 3)
                sp.dma_start(slot_dst(s), expert_tile(slice(0, 1), s)).then_inc(ld_slot[s], 16)
            sp.wait_ge(xn_ready, T)
            sp.dma_start(nw[:], norm2_w.to_broadcast([P, D])).then_inc(ld_nw2, 16)
            sp.wait_ge(pt_psum, 5)
            sp.dma_start(wr, w_router[0].rearrange("(k p) e -> p k e", p=P)).then_inc(ld_wr, 16)
            sp.wait_ge(s_max, 6)
            sp.dma_start(bgu, b_gate_up[0]).then_inc(ld_moe, 16)
            sp.wait_ge(o_psum, 6)
            sp.wait_ge(gdn_dve, DVE_DONE[1, 12])
            for s in (2, 3):
                sp.dma_start(slot_dst(s, 1), expert_tile(slice(1, 2), s)).then_inc(ld_slot[s], 16)
            sp.wait_ge(gdn_dve, DVE_DONE[1, "N"])
            sp.dma_start(bdn, b_down[0]).then_inc(ld_moe, 16)
            sp.wait_ge(w_used, 1)
            for s in (10, 11):
                sp.dma_start(slot_dst(s), expert_tile(slice(0, 1), s)).then_inc(ld_slot[s], 16)
            sp.wait_ge(h_psum, 2 * T)
            for s in (8, 9):
                sp.dma_start(slot_dst(s), expert_tile(slice(0, 1), s)).then_inc(ld_slot[s], 16)
            for s in (0, 1):
                sp.dma_start(slot_dst(s, 1), expert_tile(slice(1, 2), s)).then_inc(ld_slot[s], 16)
            sp.wait_ge(hn_ready, 2 * T)
            sp.dma_start(slot_dst(5, 1), expert_tile(slice(1, 2), 5)).then_inc(ld_slot[5], 16)
            sp.wait_ge(lg_psum, T)
            sp.dma_start(slot_dst(4, 1), expert_tile(slice(1, 2), 4)).then_inc(ld_slot[4], 16)
            sp.wait_ge(tab_ready, 5)
            sp.wait_ge(consts, 18)
            n_blocks = sp.value_load(nbl[0:1, MAXB:MAXB + 1], min_val=N_EXP, max_val=NB_MAX)

            def expert_of(b):
                return sp.value_load(nbl[0:1, bass.ds(b, 1)], min_val=0, max_val=N_EXP - 1)

            def load_sets(m, lag):
                e = expert_of(m + (2 - lag))
                odd = sp.value_load(parity[0:1, bass.ds(m + (2 - lag), 1)], min_val=0, max_val=1)
                loads = sp.snap(16 * m + (32 - 16 * lag))
                for s in range(6):
                    sp.wait_ge(wgu_used, 8 * m + (s + 1 - 8 * lag))
                    sp.wait_ge(ld_slot[s], loads)
                    sp.dma_start(slot_dst(s, odd), expert_tile(bass.ds(e, 1), s)).then_inc(ld_slot[s], 16)

            def load_rest(m, lag):
                e = expert_of(m + (1 - lag))
                for s in range(6, 12):
                    if s < 8:
                        sp.wait_ge(wgu_used, 8 * m + (s + 1 - 8 * lag))
                    else:
                        sp.wait_ge(wdn_used, 4 * m + (s - 7 - 4 * lag))
                    sp.dma_start(slot_dst(s), expert_tile(bass.ds(e, 1), s)).then_inc(ld_slot[s], 16)

            with sp.Fori(1, EARLY_BLOCKS + 1) as b:
                load_sets(b, 1)
                load_rest(b, 1)
            with sp.Fori(EARLY_BLOCKS + 1, n_blocks - 1) as b:
                load_rest(b, 1)
                load_sets(b, 1)
            two_less = sp.value_load(nbl[0:1, MAXB + 1:MAXB + 2], min_val=N_EXP - 2, max_val=NB_MAX - 2)
            load_rest(two_less, 0)
            for i in range(2 * T):
                t, c = i // 2, slice((i % 2) * 512, (i % 2 + 1) * 512)
                sp.wait_ge(out_ready, i + 1)
                sp.dma_start(out[0, t * P:(t + 1) * P, c], hx[:, t, c]).then_inc(st_out, 16)
            sp.wait_ge(st_out, 16 * 2 * T)

        @block.gpsimd
        def _(pool):
            c = Tally(pool, consts)
            c.mark(pool.memset(ones[:], 1.0))
            c.mark(pool.memset(ident[:], 0.0))
            c.mark(pool.memset(zpad, 0.0))
            c.mark(pool.iota(slot2[:], [[0, 2], [1, SLOTS]], base=0, channel_multiplier=0,
                             allow_small_or_imprecise_dtypes=True))
            c.mark(pool.iota(iota_e[:], [[1, N_EXP]], base=0, channel_multiplier=0,
                             allow_small_or_imprecise_dtypes=True))
            c.mark(pool.iota(iota_b[:], [[1, MAXB]], base=0, channel_multiplier=0,
                             allow_small_or_imprecise_dtypes=True))
            c.mark(pool.iota(col[:, 8:9], [[0, 1]], base=0, channel_multiplier=1,
                             allow_small_or_imprecise_dtypes=True))
            c.mark(pool.memset(m_out[:], -1.0))
            c.mark(pool.iota(parity[:].rearrange("p (h o) -> p h o", o=2), [[0, MAXB // 2], [1, 2]], base=0,
                             channel_multiplier=0))
            c.mark(pool.memset(col[:, 0:1], EPS))
            c.mark(pool.memset(col[:, 1:2], EPS * DK))
            c.step(pool.memset(col[:, 2:3], 1.0))
            c.mark(pool.affine_select(ident[:], ident[:], [[-1, P]], ALU.not_equal, 1.0, base=0,
                                      channel_multiplier=1))
            c.mark(pool.affine_select(ucum[:], ones[:], [[1, P]], ALU.is_ge, 0.0, base=0,
                                      channel_multiplier=-1))
            c.mark(pool.affine_select(ustr[:], ones[:], [[1, P]], ALU.is_gt, 0.0, base=0,
                                      channel_multiplier=-1))
            c.step(pool.affine_select(m_out[:], m_out[:], [[-1, P]], ALU.is_gt, 0.0, base=0,
                                      channel_multiplier=1))
            c.step(pool.affine_select(m_in[:].rearrange("p (b n) -> p b n", n=16),
                                      m_out[:].rearrange("p (b n) -> p b n", n=16),
                                      [[16, P // 16], [0, 16]], ALU.is_ge, 0.0, base=15,
                                      channel_multiplier=-1))
            c.step(pool.tensor_tensor(m_out[:], m_out[:], m_in[:], ALU.subtract))
            em, st = Tally(pool, emask_ready), Tally(pool, pool_step)
            for t in range(T):
                m = MAT[t]
                pool.wait_ge(e_ready, 2 * t + 2)
                pool.wait_ge(dec_act, 3)
                st.step(pool.tensor_tensor(heads(m["L"]), heads(m["N"]), wide(gd[:, 2, t], P), ALU.mult))
                st.step(pool.tensor_tensor(heads(m["N"]), heads(m["L"]), each_head(m_in[:]), ALU.mult))
                st.step(pool.tensor_tensor(heads(m["L"]), heads(m["L"]), each_head(m_out[:]), ALU.mult))
                em.mark(pool.tensor_tensor(heads(m["A"]), heads(m["A"]), each_head(ucum[:]), ALU.mult))
            l2, sq = Tally(pool, l2_sq), Tally(pool, swa_sq)
            for u in range(4):
                pool.wait_ge(silu_ready, u + 1)
                if u >= 2:
                    pool.wait_ge(l2_psum, u - 1)
                c0 = CONV_AT[u + 1]
                v = conv[:, c0:c0 + 2, :].rearrange("p c s -> p (c s)")
                l2.mark(pool.tensor_tensor(sc[:, u % 2], v, v, ALU.mult))
            for u in range(2 * T):
                pool.wait_ge(z_evac, evacuated(u + 7))
                if u < 2:
                    pool.wait_ge(l2_psum, u + 3)
                else:
                    pool.wait_ge(swa_ss, u - 1)
                sq.mark(pool.tensor_tensor(sc[:, u % 2], zswa[:, u], zswa[:, u], ALU.mult))
            pool.wait_ge(s_psum, 6)
            pool.memset(yb, 0.0).then_inc(zeroed, 1)
            pool.memset(SGT, 0.0).then_inc(zeroed, 1)

        @block.scalar
        def _(act):
            act.dma_start(wba[:], win[:, :, C_BA:C_BA + 2 * HG]).then_inc(ld_ba, 16)
            act.dma_start(rel[0:REL_BUCKETS, :], rel_bias).then_inc(ld_rel, 16)
            st = Tally(act, act_step)
            act.wait_ge(consts, 12)
            xs = Tally(act, x_sq)
            for t in range(T):
                act.wait_ge(ld_x[t], 16)
                st.step(act.activation(xn[:, t, :], hx[:, t, :], ACT.Square, accum_out=nrm[:, 0, t:t + 1]))
                xs.mark(act.activation(nrm[:, 1, t:t + 1], nrm[:, 0, t:t + 1], ACT.Sqrt, bias=col[:, 0:1],
                                       scale=1.0 / D))
            xt = Tally(act, xnT_ready)
            for i in range(2 * T):
                t, q = divmod(i, 2)
                act.wait_ge(xT_psum, i + 1)
                xt.mark(act.copy(xnT[:, 4 * q:4 * q + 4, t * P:(t + 1) * P], heads(bank[i][:])))
            small = [(gd[:, 0, 0], a_log.to_broadcast([P, HG])),
                     (gd[:, 1, 0], dt_bias.to_broadcast([P, HG])),
                     (col[:, 16:17], gdn_norm_w.rearrange("a d -> d a")),
                     (col[0:DH, 17:18], q_norm_w.rearrange("a d -> d a")),
                     (col[DH:P, 17:18], q_norm_w.rearrange("a d -> d a")),
                     (col[0:DH, 18:19], k_norm_w.rearrange("a d -> d a")),
                     (col[DH:P, 18:19], k_norm_w.rearrange("a d -> d a")),
                     (brt[:], b_router.to_broadcast([P, N_EXP]))]
            for dst, src in small:
                act.dma_start(dst, src).then_inc(ld_small, 16)
            z = Tally(act, z_evac)

            def evac(u):
                act.wait_ge(z_psum, {1: 1, 0: 2}.get(u, u + 1))
                src = bank[z_bank(u)]
                if u == 0:
                    z.mark(act.copy(ba[:], src[:, 0:T * 8].rearrange("p (t n) -> p t n", t=T)))
                elif u <= 6:
                    act.wait_ge(consts, 12)
                    z.mark(act.copy(zpad[:, CONV_AT[u]:CONV_AT[u] + 2, 3:3 + S],
                                    src[:].rearrange("p (c s) -> p c s", c=2)))
                elif u <= 12:
                    z.mark(act.copy(zswa[:, u - 7], src[:]))
                else:
                    z.mark(act.copy(gate[:, u - 13], src[:]))

            def flip(u):
                a, t = divmod(u, T)
                act.wait_ge(qkT_psum, u + 1)
                act.wait_ge(dec_dve, 2)
                z.mark(act.activation(qkT[:, a, :, t * P:(t + 1) * P],
                                      heads(bank[z_bank(f"f{u}")][:]), ACT.Copy,
                                      scale=col[:, 17 + a:18 + a]))

            si = Tally(act, silu_ready)

            def silu(u):
                act.wait_ge(conv_ready, u)
                v = conv[:, CONV_AT[u]:CONV_AT[u] + 2, :]
                si.mark(act.activation(v, v, ACT.Silu))

            da = Tally(act, dec_act)
            evac(1)
            evac(0)
            act.wait_ge(dec_dve, 1)
            act.wait_ge(ld_small, 16 * 8)
            st.step(act.activation(gd[:, 4], gd[:, 3], ACT.Abs))
            st.step(act.activation(gd[:, 4], gd[:, 4], ACT.Exp, scale=-1.0))
            da.mark(act.activation(gd[:, 0, 0], gd[:, 0, 0], ACT.Exp))
            da.mark(act.activation(gd[:, 4], gd[:, 4], ACT.Ln, bias=1.0))
            da.mark(act.activation(gd[:, 2], ba[:, :, 0:HG], ACT.Sigmoid))
            act.wait_ge(gap_ready, 1)
            da.mark(act.activation(gd[:, 7], gd[:, 5], ACT.Exp))
            da.mark(act.activation(gd[:, 8], gd[:, 6], ACT.Exp))
            evac(2)
            er = Tally(act, e_ready)
            for t in range(T):
                act.wait_ge(gap_ready, 2 + t)
                er.mark(act.activation(MAT[t]["N"], MAT[t]["N"], ACT.Exp, scale=-1.0))
                er.mark(act.activation(MAT[t]["A"], MAT[t]["A"], ACT.Exp))
            evac(3)
            silu(1)
            silu(2)
            evac(4)
            silu(3)
            evac(5)
            silu(4)
            evac(6)
            lr = Tally(act, l2_root)
            for u in range(4):
                act.wait_ge(l2_psum, u + 1)
                q = u >= 2
                st.mark(act.activation(a1m[:, u], bank[u][:], ACT.Ln, bias=col[:, 1:2] if q else col[:, 0:1],
                                       scale=float(DK) if q else 1.0))
            act.wait_ge(act_step, st.n)
            for u in range(4):
                lr.mark(act.activation(a1m[:, u], a1m[:, u], ACT.Exp, scale=-0.5))
            silu(5)
            silu(6)

            gdn, pe_, pr = Tally(act, gdn_act), Tally(act, p_exp), Tally(act, pt_ready)
            gs, hs, ht, le = (Tally(act, q) for q in (gsilu, h_sq, hnT_ready, lg_exp))
            for kind, a, s in ORDER:
                if kind == "z":
                    evac(a)
                elif kind == "s":
                    act.wait_ge(z_evac, evacuated(14))
                    gs.mark(act.activation(gate[:], gate[:], ACT.Silu))
                elif kind == "n":
                    act.wait_ge(swa_ss, 4)
                    Tally(act, swa_root).mark(act.activation(nrm[:, 3], nrm[:, 2], ACT.Sqrt,
                                                                 bias=col[:, 0:1], scale=1.0 / DH))
                elif kind == "f":
                    flip(a)
                elif kind == "gdn":
                    m, X = MAT[a], bank[2 * a]
                    if s == "M":
                        act.wait_ge(gdn_dve, DVE_DONE[a, 12])
                        gdn.mark(act.activation(m["E"], m["D"], ACT.Square))
                    elif s == "N":
                        act.wait_ge(gdn_dve, DVE_DONE[a, "M"])
                        gdn.mark(act.activation(nrm[:, 6, 4 * a:4 * a + 4], nrm[:, 5, 4 * a:4 * a + 4],
                                                ACT.Sqrt, bias=col[:, 0:1], scale=1.0 / DK))
                    elif s in ACT_STAGES:
                        act.wait_ge(gdn_psum, PE_DONE[a, s])
                        dst = {3: "E", 4: "N", 5: "E", 7: "N", 8: "E", 9: "N"}[s]
                        gdn.mark(act.copy(m[dst], X[:]))
                elif kind == "S":
                    g = a
                    n = 4 if g < 2 else 2
                    act.wait_ge(s_max, g + 1)
                    for h in range(n):
                        w = 512 // n
                        pe_.mark(act.activation(sc[:, g % 2, h * w:(h + 1) * w], sc[:, g % 2, h * w:(h + 1) * w],
                                                ACT.Exp, bias=nrm[:, 4, 8 * (g % 2) + h:8 * (g % 2) + h + 1],
                                                accum_out=nrm[:, 4, 16 + 8 * (g % 2) + h:17 + 8 * (g % 2) + h]))
                elif kind == "T":
                    act.wait_ge(pt_psum, a + 1)
                    if a >= 2:
                        act.wait_ge(o_psum, a - 1)
                    pr.mark(act.copy(pt[:, a % 2], bank[7][:]))
                elif kind == "A":
                    act.wait_ge(h_ready, 2 * a + 2)
                    st.step(act.activation(hn[:, a, :], hx[:, a, :], ACT.Square, accum_out=nrm[:, 0, a:a + 1]))
                    hs.mark(act.activation(nrm[:, 1, a:a + 1], nrm[:, 0, a:a + 1], ACT.Sqrt, bias=col[:, 0:1],
                                           scale=1.0 / D))
                elif kind == "L":
                    for q in range(2):
                        act.wait_ge(hT_psum, 2 * a + q + 1)
                        ht.mark(act.copy(hnT[:, 4 * q:4 * q + 4, a * P:(a + 1) * P], heads(bank[2 * a + q][:])))
                elif kind == "G":
                    act.wait_ge(lg_max, a + 1)
                    le.mark(act.activation(ex[a], top[a][:, 0:TOP_K], ACT.Exp, bias=nrm[:, 7, a:a + 1],
                                           accum_out=nrm[:, 7, 2 + a:3 + a]))
                elif kind == "B":
                    act.wait_ge(gT_psum, a + 1)
                    Tally(act, gT_ready).mark(act.copy(gT[:, a * P:(a + 1) * P], bank[7][0:N_EXP, a * P:(a + 1) * P]))

            act.wait_ge(gT_psum, T)
            Tally(act, gT_ready).mark(act.copy(gT[:, P:2 * P], bank[7][0:N_EXP, P:2 * P]))
            act.wait_ge(xg_psum, 1)
            xr, yr, sr, gr2 = Tally(act, xg_ready), Tally(act, y_ready), Tally(act, sig_ready), Tally(act, SGT_ready)
            xr.mark(act.copy(xg, bank[6][:]))
            act.wait_ge(zeroed, 2)
            yr.mark(act.copy(yb[:, 0:1], yb[:, 0:1]))
            act.wait_ge(tab_ready, 5)
            n_blocks = act.value_load(nbl[0:1, MAXB:MAXB + 1], min_val=N_EXP, max_val=NB_MAX)
            with act.Fori(0, n_blocks) as b:
                act.wait_ge(g_min, b + 1)
                act.activation(sg, gt, ACT.Sigmoid, scale=ALPHA).then_inc(sig_ready, 1)
                act.wait_ge(SGT_psum, b + 1)
                act.copy(SGT, bank[7][:, 0:S]).then_inc(SGT_ready, 1)
                act.wait_ge(xg_psum, b + 2)
                act.copy(xg, bank[6][:]).then_inc(xg_ready, 1)
                act.wait_ge(wdn_used, 4 * b + 4)
                act.copy(yb, bank[7][:]).then_inc(y_ready, 1)

        @block.vector
        def _(dve):
            st = Tally(dve, dve_step)
            Tally(dve, rel_one).mark(dve.memset(rel[REL_BUCKETS:REL_BUCKETS + 1, :], 1.0))
            dve.wait_ge(ld_nw, 16)
            xr = Tally(dve, xn_ready)
            for t in range(T):
                dve.wait_ge(x_sq, t + 1)
                st.step(dve.reciprocal(nrm[:, 1, 2 + t:3 + t], nrm[:, 1, t:t + 1]))
                xr.mark(dve.scalar_tensor_tensor(out=xn[:, t, :], in0=hx[:, t, :], scalar=nrm[:, 1, 2 + t:3 + t],
                                                 in1=nw[:], op0=ALU.mult, op1=ALU.mult))
            dve.wait_ge(dist_psum, 1)
            Tally(dve, dist_ready).mark(dve.tensor_copy(fdist, bank[4][0:HS, 0:TW]))
            cwr = Tally(dve, cw_ready)
            cwr.step(dve.tensor_copy(cw[:].rearrange("p i c -> p (i c)"), bank[4][:, TW:TW + CONV_K * 12]))
            dve.wait_ge(consts, 18)
            st.mark(dve.tensor_scalar(own[:], iota_b[:], col[0:N_EXP, 8:9], None, ALU.is_equal))

            dd = Tally(dve, dec_dve)
            dve.wait_ge(z_evac, evacuated(0))
            dve.wait_ge(ld_small, 16 * 8)
            dd.step(dve.tensor_tensor(gd[:, 3], ba[:, :, HG:2 * HG],
                                      gd[:, 1, 0].unsqueeze(1).to_broadcast([P, T, HG]), ALU.add))
            dd.step(dve.tensor_scalar(col[:, 17:18], col[:, 17:18], DH ** -0.5, None, ALU.mult))
            st.step(dve.tensor_scalar(gd[:, 9], gd[:, 3], 0.0, None, ALU.max))
            dve.wait_ge(dec_act, 2)
            st.step(dve.tensor_tensor(gd[:, 9], gd[:, 9], gd[:, 4], ALU.add))
            gr = Tally(dve, g_ready)
            for t in range(T):
                gr.step(dve.scalar_tensor_tensor(out=gd[:, 9, t], in0=gd[:, 9, t], scalar=-1.0,
                                                 in1=gd[:, 0, 0], op0=ALU.mult, op1=ALU.mult))
            ur = Tally(dve, ug_ready)
            dve.wait_ge(xT_psum, 2 * T)
            dve.wait_ge(consts, 18)
            for t in range(T):
                for h in range(HG):
                    ur.mark(dve.tensor_scalar(ug[:, t, h * P:(h + 1) * P], ucum[:], gd[:, 9, t, h:h + 1], None,
                                              ALU.mult))
            gp = Tally(dve, gap_ready)
            dve.wait_ge(gc_psum, 1)
            st.step(dve.tensor_copy(gd[:, 5], bank[4][:, 0:8].rearrange("p (t h) -> p t h", t=T)))
            gp.mark(dve.tensor_tensor(gd[:, 6], bank[4][:, 8:16].rearrange("p (t h) -> p t h", t=T), gd[:, 5],
                                      ALU.subtract))
            for t in range(T):
                dve.wait_ge(gcrow_psum, t + 1)
                for h in range(HG):
                    row, mine = bank[t][:, h * P:(h + 1) * P], gd[:, 5, t, h:h + 1]
                    dve.tensor_scalar(MAT[t]["N"][:, h * P:(h + 1) * P], row, mine, 0.0, ALU.subtract, ALU.max)
                    last = dve.tensor_scalar(MAT[t]["A"][:, h * P:(h + 1) * P], row, mine, 0.0,
                                             ALU.subtract, ALU.min)
                gp.mark(last)
            cr, l2 = Tally(dve, conv_ready), Tally(dve, l2_done)
            for u in range(1, 7):
                dve.wait_ge(z_evac, evacuated(u))
                pair = (CONV_AT[u], CONV_AT[u] + 1)
                for c in pair:
                    st.mark(dve.tensor_scalar(conv[:, c, :], zpad[:, c, 0:S], cw[:, 0, c:c + 1], None, ALU.mult))
                for i in range(1, CONV_K):
                    for c in pair:
                        dve.wait_ge(dve_step, st.n - 1)
                        ins = dve.scalar_tensor_tensor(out=conv[:, c, :], in0=zpad[:, c, i:i + S],
                                                       scalar=cw[:, i, c:c + 1], in1=conv[:, c, :],
                                                       op0=ALU.mult, op1=ALU.add)
                        if c == pair[1] and i == CONV_K - 1:
                            cr.mark(ins)
                        else:
                            st.mark(ins)
            for u in range(4):
                dve.wait_ge(l2_root, u + 1)
                c0 = CONV_AT[u + 1]
                v = conv[:, c0:c0 + 2, :].rearrange("p c s -> p (c s)")
                l2.mark(dve.tensor_tensor(v, v, a1m[:, u], ALU.mult))
            dve.wait_ge(dec_act, 5)
            st.step(dve.tensor_tensor(gd[:, 10], gd[:, 2], gd[:, 7], ALU.mult))

            gdn, ss, sn = Tally(dve, gdn_dve), Tally(dve, swa_ss), Tally(dve, swa_normed)
            sm, pr, orr = Tally(dve, s_max), Tally(dve, p_ready), Tally(dve, o_ready)
            hr, hnr, lm, mr = (Tally(dve, q) for q in (h_ready, hn_ready, lg_max, mask_ready))
            gr2 = Tally(dve, gates_ready)
            n_exp = 0
            for kind, a, s in ORDER:
                if kind == "z":
                    if 8 <= a <= 10:
                        u = a - 8
                        dve.wait_ge(swa_sq, u + 1)
                        ss.mark(dve.reduce_sum(nrm[:, 2, 8 * u:8 * u + 8], heads(sc[:, u % 2], HS), AX_X))
                    continue
                if kind == "n":
                    dve.wait_ge(swa_sq, 4)
                    ss.mark(dve.reduce_sum(nrm[:, 2, 24:32], heads(sc[:, 1], HS), AX_X))
                    dve.wait_ge(swa_root, 1)
                    st.step(dve.reciprocal(nrm[:, 3], nrm[:, 3]))
                    for u in range(2 * T):
                        sn.mark(dve.tensor_tensor(heads(zswa[:, u], HS), heads(zswa[:, u], HS),
                                                  wide(nrm[:, 3, 8 * u:8 * u + 8], DH), ALU.mult))
                    continue
                if kind in "syfWXLBC":
                    continue
                if kind == "A":
                    for hf in range(2):
                        dve.wait_ge(h_psum, 2 * a + hf + 1)
                        v = hx[:, a, hf * 512:(hf + 1) * 512]
                        hr.mark(dve.tensor_tensor(v, bank[H_BANK[2 * a + hf]][:], v, ALU.add))
                    continue
                if kind == "R":
                    dve.wait_ge(h_sq, a + 1)
                    dve.wait_ge(ld_nw2, 16)
                    st.step(dve.reciprocal(nrm[:, 1, 2 + a:3 + a], nrm[:, 1, a:a + 1]))
                    for hf in range(2):
                        c = slice(hf * 512, (hf + 1) * 512)
                        hnr.mark(dve.scalar_tensor_tensor(out=hn[:, a, c], in0=hx[:, a, c],
                                                          scalar=nrm[:, 1, 2 + a:3 + a], in1=nw[:, c],
                                                          op0=ALU.mult, op1=ALU.mult))
                    continue
                if kind == "G":
                    dve.wait_ge(lg_psum, a + 1)
                    st.step(dve.tensor_tensor(lg[a], bank[2 * a][:, 0:N_EXP], brt[:], ALU.add))
                    st.step(dve.max(top[a], lg[a]))
                    iu = gd[:, 4 + a].rearrange("p t h -> p (t h)").bitcast(U32)
                    fi = gd[:, 6 + a].rearrange("p t h -> p (t h)")
                    lm.mark(dve.tensor_scalar(nrm[:, 7, a:a + 1], top[a][:, 0:1], -1.0, None, ALU.mult))
                    st.step(dve.max_index(iu, top[a], lg[a]))
                    st.step(dve.tensor_copy(fi, iu))
                    st.step(dve.tensor_tensor(picks[a], iota_e[:].unsqueeze(1).to_broadcast([P, TOP_K, N_EXP]),
                                              wide(fi[:, 0:TOP_K], N_EXP), ALU.is_equal))
                    mr.mark(dve.reduce_sum(mask[a], picks[a].rearrange("p j e -> p e j"), AX_X))
                    dve.wait_ge(lg_exp, a + 1)
                    st.mark(dve.reciprocal(nrm[:, 7, 4 + a:5 + a], nrm[:, 7, 2 + a:3 + a]))
                    st.step(dve.tensor_tensor(shares[a], picks[a], wide(ex[a], N_EXP), ALU.mult))
                    st.step(dve.reduce_sum(gates[a], shares[a].rearrange("p j e -> p e j"), AX_X))
                    gr2.mark(dve.tensor_scalar(gates[a], gates[a], nrm[:, 7, 4 + a:5 + a], None, ALU.mult))
                    continue
                if kind == "gdn":
                    t, m = a, MAT[a]
                    X, Y, Z = bank[2 * t], bank[2 * t + 1], bank[4]
                    if s in PE_STAGES:
                        dve.wait_ge(gdn_psum, PE_DONE[t, s])
                    if s == 1:
                        dve.wait_ge(emask_ready, t + 1)
                        st.mark(dve.tensor_tensor(m["N"], X[:], m["N"], ALU.mult))
                        st.mark(dve.tensor_tensor(m["L"], X[:], m["L"], ALU.mult))
                        gdn.mark(dve.tensor_tensor(m["A"], Y[:], m["A"], ALU.mult))
                    elif s == 2:
                        st.step(dve.tensor_copy(m["D"], X[:]))
                        st.step(dve.tensor_tensor(heads(m["G"]), heads(m["D"]), each_head(ident[:]), ALU.add))
                        gdn.mark(dve.tensor_tensor(heads(m["H"]), heads(Z[:]), wide(gd[:, 2, t], P), ALU.mult))
                    elif s == 3:
                        gdn.mark(dve.tensor_copy(m["F"], Y[:]))
                    elif s == 4:
                        st.step(dve.tensor_copy(m["D"], Y[:]))
                        gdn.mark(dve.tensor_tensor(m["G"], Z[:], m["G"], ALU.add))
                    elif s == 5:
                        gdn.mark(dve.tensor_tensor(m["G"], Z[:], m["G"], ALU.add))
                    elif s == 6:
                        gdn.mark(dve.tensor_tensor(m["G"], X[:], m["G"], ALU.add))
                    elif s == 7:
                        gdn.mark(dve.tensor_copy(m["D"], Y[:]))
                    elif s == "K":
                        st.step(dve.tensor_tensor(heads(m["I"]), heads(Y[:]), wide(gd[:, 10, t], P), ALU.mult))
                        gdn.mark(dve.tensor_tensor(m["H"], m["H"], m["I"], ALU.subtract))
                    elif s == 8:
                        st.step(dve.tensor_copy(m["F"], Y[:]))
                        gdn.mark(dve.tensor_copy(m["V"], Z[:]))
                    elif s == 9:
                        gdn.mark(dve.tensor_tensor(m["V"], Z[:], m["V"], ALU.add))
                    elif s == 10:
                        if t == 0:
                            st.mark(dve.tensor_tensor(heads(m["I"]), heads(Y[:]), wide(gd[:, 8, t], P), ALU.mult))
                        gdn.mark(dve.tensor_tensor(m["V"], X[:], m["V"], ALU.add))
                    elif s == 11:
                        gdn.mark(dve.tensor_tensor(m["V"], Y[:], m["V"], ALU.add))
                    elif s == 12:
                        if t == 0:
                            st.step(dve.tensor_copy(m["F"], Y[:]))
                            gdn.mark(dve.tensor_copy(m["D"], X[:]))
                        else:
                            st.step(dve.tensor_tensor(heads(m["F"]), heads(Y[:]), wide(gd[:, 7, t], P), ALU.mult))
                            gdn.mark(dve.tensor_tensor(m["D"], X[:], m["F"], ALU.add))
                    elif s == "M":
                        dve.wait_ge(gdn_act, ACT_DONE[t, "M"])
                        gdn.mark(dve.reduce_sum(nrm[:, 5, 4 * t:4 * t + 4], heads(m["E"]), AX_X))
                    elif s == "N":
                        dve.wait_ge(gdn_act, ACT_DONE[t, "N"])
                        dve.wait_ge(gsilu, 1)
                        st.step(dve.reciprocal(nrm[:, 6, 4 * t:4 * t + 4], nrm[:, 6, 4 * t:4 * t + 4]))
                        st.step(dve.tensor_tensor(heads(m["D"]), heads(m["D"]), wide(nrm[:, 6, 4 * t:4 * t + 4], P),
                                                  ALU.mult))
                        gdn.mark(dve.tensor_tensor(m["D"], m["D"], gate[:, t], ALU.mult))
                    elif s == 13:
                        gdn.mark(dve.tensor_scalar(mix_gdn[:, :, t * P:(t + 1) * P], heads(X[:]), col[:, 16:17],
                                                   None, ALU.mult))
                    continue
                g = a
                n = 4 if g < 2 else 2
                if kind == "S":
                    dve.wait_ge(s_psum, g + 1)
                    dve.wait_ge(ld_bias, 16)
                    if g >= 2:
                        dve.wait_ge(pt_psum, g - 1)
                    for r in range(2):
                        if g >= 2:
                            o_, i_ = sc[:, g % 2, r * S:(r + 1) * S], swa_s[r][:, 0:S]
                            b_ = bias[:, 2 * (g - 2) + r, :]
                        else:
                            o_ = heads(sc[:, g % 2], 4)[:, r:4:2, :]
                            i_ = swa_s[r][:, 0:S].rearrange("p (h j) -> p h j", h=2)
                            b_ = bias[:, 4 * g + r:4 * g + 4:2, P:2 * P]
                        st.step(dve.tensor_tensor(o_, i_, b_, ALU.add))
                    c0 = 8 * (g % 2)
                    st.step(dve.reduce_max(nrm[:, 4, c0:c0 + n], heads(sc[:, g % 2], n), AX_X))
                    sm.mark(dve.tensor_scalar(nrm[:, 4, c0:c0 + n], nrm[:, 4, c0:c0 + n], -1.0, None, ALU.mult))
                elif kind == "T":
                    n_exp += n
                    c0 = 16 + 8 * (g % 2)
                    dve.wait_ge(p_exp, n_exp)
                    st.step(dve.reciprocal(nrm[:, 4, c0:c0 + n], nrm[:, 4, c0:c0 + n]))
                    v = heads(sc[:, g % 2], n)
                    pr.mark(dve.tensor_tensor(v, v, wide(nrm[:, 4, c0:c0 + n], 512 // n), ALU.mult))
                else:
                    dve.wait_ge(o_psum, g + 1)
                    if g >= 2:
                        orr.mark(dve.tensor_copy(mix_swa[:, g - 2, P:2 * P], bank[7][:, 0:P]))
                    else:
                        orr.mark(dve.tensor_copy(mix_swa[:, 2 * g:2 * g + 2, 0:P],
                                                 bank[7][:, 0:S].rearrange("p (q i) -> p q i", q=2)))

            dve.wait_ge(cnt_psum, 1)
            nb = Tally(dve, nb_ready)
            cnt = bank[5][0:N_EXP, 0:1]
            st.step(dve.tensor_scalar(more, cnt, float(SLOTS), None, ALU.is_gt))
            for j in range(2, S // SLOTS):
                ins = dve.scalar_tensor_tensor(out=more, in0=cnt, scalar=float(j * SLOTS), in1=more,
                                               op0=ALU.is_gt, op1=ALU.add)
                (st.step if j < S // SLOTS - 1 else nb.mark)(ins)
            st.step(dve.scalar_tensor_tensor(out=rms, in0=bank[4][:, 0:T * N_EXP], scalar=ABSENT, in1=masks,
                                             op0=ALU.add, op1=ALU.mult))
            rmr = Tally(dve, rm_ready)
            rmr.step(dve.tensor_scalar(rms, rms, -ABSENT, None, ALU.add))
            for t in range(T):
                ins = dve.tensor_scalar(SEL[:, t, :], slot2[:, 0, :], rm[t][:, 0:1], None, ALU.is_equal)
            ins.then_inc(S_ready, 1)
            dve.tensor_copy(oh_cur, own[:, 0:1].to_broadcast([N_EXP, SLOTS])).then_inc(oh_ready, 1)
            dve.wait_ge(end_psum, 1)
            tr = Tally(dve, tab_ready)
            st.step(dve.tensor_scalar(col[0:N_EXP, 25:27], bank[5][0:N_EXP, 1:3], float(N_EXP), None, ALU.add))
            tr.mark(dve.tensor_scalar(nbl[0:1, MAXB:MAXB + 1], bank[5][0:1, 4:5], float(N_EXP), None, ALU.add))
            tr.mark(dve.tensor_scalar(nbl[0:1, MAXB + 1:MAXB + 2], bank[5][0:1, 4:5], float(N_EXP - 2), None,
                                      ALU.add))
            st.mark(dve.tensor_scalar(since, iota_b[:], beg, 1.0, ALU.subtract, ALU.add))
            st.step(dve.tensor_scalar(oh, iota_b[:], beg, None, ALU.is_ge))
            st.step(dve.scalar_tensor_tensor(out=oh, in0=iota_b[:], scalar=end, in1=oh, op0=ALU.is_lt,
                                             op1=ALU.mult))
            rt = Tally(dve, rt_ready)
            rt.step(dve.scalar_tensor_tensor(out=ohr, in0=since, scalar=-float(SLOTS), in1=oh, op0=ALU.mult,
                                             op1=ALU.mult))
            rt.mark(dve.tensor_tensor(oh, oh, own[:], ALU.add))
            dve.wait_ge(rt_psum, 1)
            rt.mark(dve.tensor_copy(rmT, bank[4][0:N_EXP, P:P + S]))
            dve.wait_ge(tab_psum, 1)
            tr.mark(dve.tensor_copy(nbl[0:1, 0:MAXB], bank[4][0:1, 0:MAXB]))
            tr.mark(dve.tensor_copy(RM, bank[7][:, 0:T * MAXB].rearrange("p (t b) -> p t b", t=T)))
            tr.step(dve.tensor_copy(GB, bank[7][:, 128:128 + T * MAXB].rearrange("p (t b) -> p t b", t=T)))
            dve.wait_ge(xgT_psum, 1)
            dve.tensor_copy(xgT, bank[6][:]).then_inc(xgT_ready, 1)
            n_blocks = dve.value_load(nbl[0:1, MAXB:MAXB + 1], min_val=N_EXP, max_val=NB_MAX)
            with dve.Fori(0, n_blocks) as b:
                dve.wait_ge(xg_psum, b + 1)
                for t in range(T):
                    ins = dve.tensor_scalar(SEL[:, t, :], slot2[:, 0, :], RM[:, t, bass.ds(b + 1, 1)], None,
                                            ALU.is_equal)
                ins.then_inc(S_ready, 1)
                for t in range(T):
                    ins = dve.tensor_scalar(SG[:, t, :], slot2[:].rearrange("p a s -> p (a s)"),
                                            RM[:, t, bass.ds(b, 1)], GB[:, t, bass.ds(b, 1)],
                                            ALU.is_equal, ALU.mult)
                ins.then_inc(SG_ready, 1)
                dve.wait_ge(wgu_used, 8 * b + 8)
                dve.tensor_scalar(gt, bank[4][:], LIMIT, None, ALU.min).then_inc(g_min, 1)
                dve.tensor_scalar(up, bank[5][:], LIMIT, -LIMIT, ALU.min, ALU.max).then_inc(dve_step, 1)
                dve.wait_ge(dve_step, 2 * b + (st.n + 1))
                dve.wait_ge(g_min, b + 1)
                dve.scalar_tensor_tensor(out=up, in0=up, scalar=1.0, in1=gt, op0=ALU.add,
                                         op1=ALU.mult).then_inc(dve_step, 1)
                dve.tensor_copy(oh_cur, oh[:, bass.ds(b + 1, 1)].to_broadcast([N_EXP, SLOTS])
                                ).then_inc(oh_ready, 1)
                dve.wait_ge(dve_step, 2 * b + (st.n + 2))
                dve.wait_ge(sig_ready, b + 1)
                dve.tensor_tensor(up, up, sg, ALU.mult).then_inc(act_ready, 1)
                dve.wait_ge(actT_psum, b + 1)
                dve.tensor_copy(actT, bank[4][:]).then_inc(actT_ready, 1)
                dve.wait_ge(xgT_psum, b + 2)
                dve.tensor_copy(xgT, bank[6][:]).then_inc(xgT_ready, 1)
            for i in range(2 * T):
                t, hf = divmod(i, 2)
                dve.wait_ge(acc_done, i + 1)
                v = hx[:, t, hf * 512:(hf + 1) * 512]
                dve.tensor_tensor(v, bank[i][:], v, ALU.add).then_inc(out_ready, 1)

        @block.tensor
        def _(pe):
            mm, tp = pe.matmul, pe.transpose
            pe.wait_ge(consts, 18)
            xt = Tally(pe, xT_psum)
            for i in range(2 * T):
                t, q = divmod(i, 2)
                pe.wait_ge(xn_ready, t + 1)
                for k in range(4):
                    ins = tp(bank[i][:, k * P:(k + 1) * P], xn[:, t, (4 * q + k) * P:(4 * q + k + 1) * P],
                             ident[:])
                xt.mark(ins)
            z = Tally(pe, z_psum)

            def ring_bank(user):
                i = RING.index(user)
                if i >= 3:
                    pe.wait_ge(z_evac, i - 2)
                return bank[z_bank(user)]

            def take_shared(step):
                for users, first in ((BANK4, None), (BANK7, ("z", "f2", None))):
                    if step not in users:
                        continue
                    i = users.index(step)
                    kind, a, s = (users[i - 1] if i else first) or ("", 0, None)
                    if kind == "z":
                        pe.wait_ge(z_evac, evacuated(a))
                    elif kind == "gdn":
                        pe.wait_ge(gdn_dve, DVE_DONE[a, s])
                    elif kind:
                        pe.wait_ge(pt_ready if kind == "T" else o_ready, a + 1)

            def unit(u, ks=range(KT)):
                if ks[0]:
                    dst = bank[z_bank(u)]
                elif u in LATE_UNITS:
                    take_shared(("z", u, None))
                    dst = bank[z_bank(u)]
                else:
                    dst = ring_bank(u)
                if u == 0:
                    pe.wait_ge(ld_ba, 16)
                    for t in range(T):
                        for k in range(KT):
                            ins = mm(dst[:, 8 * t:8 * t + 8], xnT[:, k, t * P:(t + 1) * P], wba[:, k, :],
                                     start=k == 0, stop=k == KT - 1)
                    z.mark(ins)
                    return
                j, half = divmod(u - 1, 2)
                pe.wait_ge(ld_win[j % 4], 16 * (j // 4 + 1))
                w = piece(j)
                if j >= 3:
                    for k in ks:
                        ins = mm(dst[:], xnT[:, k, half * P:(half + 1) * P], w[:, k, :],
                                 start=k == 0, stop=k == KT - 1)
                else:
                    for c in range(2):
                        c0 = (2 * half + c) * P
                        for k in range(KT):
                            ins = mm(dst[:, c * S:(c + 1) * S], w[:, k, c0:c0 + P], xnT[:, k, :],
                                     start=k == 0, stop=k == KT - 1)
                if ks[-1] == KT - 1:
                    z.mark(ins)

            pe.wait_ge(xnT_ready, 2 * T)
            unit(1)
            pe.wait_ge(ld_rel, 48)
            pe.wait_ge(rel_one, 1)
            mm(bank[4][0:HS, 0:TW], rel[:], dtab, start=True, stop=True)
            Tally(pe, dist_psum).mark(tp(bank[4][:, TW:TW + CONV_K * 12], cw_rows, ident[0:CONV_K * 12, 0:CONV_K * 12]))
            unit(0)
            unit(2)
            pe.wait_ge(g_ready, T)
            pe.wait_ge(cw_ready, 1)
            for t in range(T):
                mm(bank[4][:, 4 * t:4 * t + 4], ucum[:], gd[:, 9, t], start=True, stop=True)
                ins = mm(bank[4][:, 8 + 4 * t:12 + 4 * t], ones[:], gd[:, 9, t], start=True, stop=True)
            Tally(pe, gc_psum).mark(ins)
            unit(3)
            gr = Tally(pe, gcrow_psum)
            for t in range(T):
                pe.wait_ge(ug_ready, HG * (t + 1))
                gr.mark(mm(bank[t][:], ones[:], ug[:, t, :], start=True, stop=True))
            l2 = Tally(pe, l2_psum)

            def l2_sum(u):
                pe.wait_ge(gap_ready, 3)
                pe.wait_ge(l2_sq, u + 1)
                l2.mark(mm(bank[u][:], ones[:], sc[:, u % 2], start=True, stop=True))

            for u in (4, 5):
                unit(u)
            l2_sum(0)
            l2_sum(1)
            unit(6)
            l2_sum(2)
            l2_sum(3)

            qt = Tally(pe, qkT_psum)
            gdn = Tally(pe, gdn_psum)
            sp_, pp, op = Tally(pe, s_psum), Tally(pe, pt_psum), Tally(pe, o_psum)
            kT = lambda t, h: conv[:, HG + h, t * P:(t + 1) * P]
            qT = lambda t, h: conv[:, h, t * P:(t + 1) * P]
            vT = lambda t, h: conv[:, 2 * HG + h, t * P:(t + 1) * P]
            hp = Tally(pe, h_psum)

            def project(i, ks):
                t, hf = divmod(i, 2)
                for k in ks:
                    lhsT = mix_gdn[:, k] if k < HG else mix_swa[:, k - HG]
                    last = mm(bank[H_BANK[i]][:], lhsT[:, t * P:(t + 1) * P],
                              wout[:, k, hf * 512:(hf + 1) * 512], start=k == HG, stop=k == HG - 1)
                return last

            def open_mixture(t, halves):
                pe.wait_ge(ld_moe, 32)
                pe.wait_ge(gT_ready, t + 1)
                for hf in halves:
                    mm(bank[2 * t + hf][:], gT[:, t * P:(t + 1) * P], bdn[:, hf * 512:(hf + 1) * 512],
                       start=True, stop=False, skip_group_check=True)

            def keep_warm(n):
                for _ in range(n):
                    mm(bank[3][:], ident[:], cv[:, 2], start=True, stop=True)

            ht, lp = Tally(pe, hT_psum), Tally(pe, lg_psum)
            for kind, a, s in ORDER:
                if kind in "yz":
                    halved = ("y", a, None) in ORDER
                    if kind == "y":
                        unit(a, range(KT // 2))
                    else:
                        unit(a, range(KT // 2 if halved else 0, KT))
                    if (kind, a) == ("z", 7):
                        pe.wait_ge(l2_done, 4)
                    continue
                if kind == "B":
                    if a == 0:
                        pe.wait_ge(o_ready, 6)
                    pe.wait_ge(gates_ready, a + 1)
                    Tally(pe, gT_psum).mark(tp(bank[7][0:N_EXP, a * P:(a + 1) * P], gates[a], ident[:]))
                    continue
                if kind == "C":
                    open_mixture(a, (0, 1))
                    pe.wait_ge(gdn_dve, DVE_DONE[1, 13])
                    keep_warm(3)
                    continue
                if kind in "snARG":
                    continue
                if kind == "f":
                    pe.wait_ge(swa_normed, a + 1)
                    dst = ring_bank(f"f{a}")
                    for c in range(4):
                        ins = tp(dst[:, c * P:(c + 1) * P], zswa[:, a, c * P:(c + 1) * P], ident[:])
                    qt.mark(ins)
                    continue
                if kind == "W":
                    if a == 0:
                        pe.wait_ge(ld_wout, 16)
                        pe.wait_ge(o_ready, 2)
                        pe.wait_ge(gdn_dve, DVE_DONE[0, 13])
                    if a == 2:
                        pe.wait_ge(o_ready, 6)
                        pe.wait_ge(s_max, 6)
                    ins = project(a, range(HG, KT))
                    if a == 3:
                        Tally(pe, w_used).mark(ins)
                    continue
                if kind == "X":
                    pe.wait_ge(gdn_dve, DVE_DONE[a // 2, 13])
                    hp.mark(project(a, range(HG)))
                    continue
                if kind == "L":
                    for q in range(2):
                        pe.wait_ge(hn_ready, 2 * a + q + 1)
                        for k in range(4):
                            c = (4 * q + k) * P
                            ins = tp(bank[2 * a + q][:, k * P:(k + 1) * P], hn[:, a, c:c + P], ident[:])
                        ht.mark(ins)
                    pe.wait_ge(ld_wr, 16)
                    for k in range(KT):
                        if k % 4 == 0:
                            pe.wait_ge(hnT_ready, 2 * a + 1 + (k == 4))
                        ins = mm(bank[2 * a][:, 0:N_EXP], hnT[:, k, a * P:(a + 1) * P], wr[:, k, :],
                                 start=k == 0, stop=k == KT - 1)
                    lp.mark(ins)
                    continue
                if kind == "gdn" and s not in PE_STAGES:
                    continue
                if kind == "gdn":
                    t, m = a, MAT[a]
                    X, Y, Z = bank[2 * t], bank[2 * t + 1], bank[4]
                    at = GDN_SEQ.index((t, s))
                    before = [q for q in GDN_SEQ[:at] if q[0] == t]
                    if before:
                        pe.wait_ge(gdn_dve, DVE_DONE[before[-1]])
                        if ACT_DONE[before[-1]]:
                            pe.wait_ge(gdn_act, ACT_DONE[before[-1]])
                    if s == "K":
                        pe.wait_ge(gdn_dve, DVE_DONE[0, 12])
                    take_shared((kind, t, s))

                    def product(dst, lhsT, rhs, start=True, stop=True):
                        for h in range(HG):
                            c = slice(h * P, (h + 1) * P)
                            last = mm(dst[:, c], lhsT(h) if callable(lhsT) else lhsT[:, c],
                                      rhs(h) if callable(rhs) else rhs[:, c], start=start, stop=stop)
                        return last

                    def flip(dst, src):
                        for h in range(HG):
                            c = slice(h * P, (h + 1) * P)
                            last = tp(dst[:, c], src(h) if callable(src) else src[:, c], ident[:])
                        return last

                    kt, qt_, vt = (lambda h, f=f: f(t, h) for f in (kT, qT, vT))
                    if s == 1:
                        product(X, kt, kt)
                        ins = product(Y, kt, qt_)
                    elif s == 2:
                        flip(X, m["N"])
                        pe.wait_ge(silu_ready, 6)
                        ins = flip(Z, vt)
                    elif s == 3:
                        product(X, m["D"], m["N"])
                        ins = product(Y, m["N"], m["D"])
                    elif s == 4:
                        product(X, m["F"], m["E"])
                        product(Y, m["E"], m["F"])
                        ins = product(Z, m["E"], m["G"])
                    elif s == 5:
                        product(X, m["D"], m["N"])
                        ins = product(Z, m["N"], m["G"])
                    elif s == 6:
                        ins = product(X, m["E"], m["G"])
                    elif s == 7:
                        product(X, m["G"], m["L"])
                        ins = product(Y, m["L"], m["G"])
                    elif s == "K":
                        ins = product(Y, kt, MAT[0]["F"])
                    elif s == 8:
                        product(X, m["D"], m["N"])
                        product(Y, m["N"], m["D"])
                        ins = product(Z, m["G"], m["H"])
                    elif s == 9:
                        product(X, m["E"], m["F"])
                        ins = product(Z, m["D"], m["V"])
                    elif s == 10:
                        if t == 0:
                            flip(Y, kt)
                        ins = product(X, m["F"], m["V"])
                    elif s == 11:
                        ins = product(Y, m["N"], m["V"])
                    elif s == 12:
                        product(X, m["A"], m["V"])
                        if t == 0:
                            ins = product(Y, m["I"], m["V"])
                        else:
                            ins = product(Y, qt_, MAT[0]["F"])
                    elif s == 13:
                        ins = flip(X, m["D"])
                    gdn.mark(ins)
                    continue
                g = a
                if kind == "S":
                    pe.wait_ge(z_evac, len(RING))
                    if g >= 1:
                        pe.wait_ge(s_max, g)
                    for i in range(2 if g >= 2 else 4):
                        r = i % 2
                        pair, qt0, n = (g - 2, 1, S) if g >= 2 else (2 * g + i // 2, 0, P)
                        c0 = 0 if g >= 2 else (i // 2) * P
                        ins = mm(swa_s[r][:, c0:c0 + n], qkT[DH * r:DH * (r + 1), 0, pair, qt0 * P:(qt0 + 1) * P],
                                 qkT[DH * r:DH * (r + 1), 1, pair, 0:n], start=True, stop=True)
                    sp_.mark(ins)
                elif kind == "T":
                    pe.wait_ge(p_ready, g + 1)
                    take_shared((kind, g, None))
                    for c in range(4):
                        ins = tp(bank[7][:, c * P:(c + 1) * P], sc[:, g % 2, c * P:(c + 1) * P], ident[:])
                    pp.mark(ins)
                else:
                    pe.wait_ge(pt_ready, g + 1)
                    take_shared((kind, g, None))
                    if g >= 2:
                        for r in range(2):
                            h = 2 * (g - 2) + r
                            for j in range(2):
                                ins = mm(bank[7][DH * r:DH * (r + 1), 0:P], zswa[:, 4 + j, h * DH:(h + 1) * DH],
                                         pt[:, g % 2, (2 * r + j) * P:(2 * r + j + 1) * P],
                                         start=j == 0, stop=j == 1)
                    else:
                        for i in range(4):
                            h, r = 4 * g + i, i % 2
                            ins = mm(bank[7][DH * r:DH * (r + 1), (i // 2) * P:(i // 2 + 1) * P],
                                     zswa[:, 4, h * DH:(h + 1) * DH], pt[:, g % 2, i * P:(i + 1) * P],
                                     start=True, stop=True)
                    op.mark(ins)

            keep_warm(2)
            pe.wait_ge(mask_ready, T)
            mm(bank[4][:, 0:32], ustr[:], mask[0], start=True, stop=True)
            mm(bank[4][:, 32:64], ustr[:], mask[1], start=True, stop=False)
            mm(bank[4][:, 32:64], ones[:], mask[0], start=False, stop=True)
            for t in range(T):
                ins = mm(bank[5][0:N_EXP, 0:1], mask[t], ones[:, 0:1], start=t == 0, stop=t == T - 1)
            Tally(pe, cnt_psum).mark(ins)
            keep_warm(1)

            def gather():
                for t in range(T):
                    for hf in range(2):
                        last = mm(bank[6][SLOTS * hf:SLOTS * (hf + 1), :], SEL[:, t, :],
                                  hn[:, t, hf * 512:(hf + 1) * 512], start=t == 0, stop=t == T - 1)
                last.then_inc(xg_psum, 1)

            def gather_flip():
                for c in range(4):
                    last = tp(bank[6][:, c * P:(c + 1) * P], xg[:, c * P:(c + 1) * P], ident[:])
                last.then_inc(xgT_psum, 1)

            pe.wait_ge(gates_ready, T)
            Tally(pe, gT_psum).mark(tp(bank[7][0:N_EXP, P:2 * P], gates[1], ident[:]))
            pe.wait_ge(nb_ready, 1)
            mm(bank[5][0:N_EXP, 1:2], ucum[0:N_EXP, 0:N_EXP], more, start=True, stop=True)
            mm(bank[5][0:N_EXP, 2:3], ustr[0:N_EXP, 0:N_EXP], more, start=True, stop=True)
            Tally(pe, end_psum).mark(mm(bank[5][0:1, 4:5], ones[0:N_EXP, 0:1], more, start=True, stop=True))
            pe.wait_ge(rm_ready, 1)
            for t in range(T):
                ins = tp(bank[4][0:N_EXP, (t + 1) * P:(t + 2) * P], rm[t], ident[:])
            Tally(pe, rt_psum).mark(ins)
            pe.wait_ge(S_ready, 1)
            gather()
            pe.wait_ge(rt_ready, 3)
            pe.wait_ge(gT_ready, T)
            mm(bank[4][0:1, 0:MAXB], col[0:N_EXP, 8:9], oh, start=True, stop=True)
            for t in range(T):
                c = slice(t * MAXB, (t + 1) * MAXB)
                mm(bank[7][:, c], rmT[:, t * P:(t + 1) * P], oh, start=True, stop=False)
                mm(bank[7][:, c], ones[0:N_EXP, :], ohr, start=False, stop=True)
                ins = mm(bank[7][:, 128 + t * MAXB:128 + (t + 1) * MAXB], gT[:, t * P:(t + 1) * P], oh,
                         start=True, stop=True)
            Tally(pe, tab_psum).mark(ins)
            pe.wait_ge(xg_ready, 1)
            gather_flip()
            open_mixture(1, (0, 1))

            def combine(final=False):
                for t in range(T):
                    for hf in range(2):
                        last = mm(bank[2 * t + hf][:], SGT[SLOTS * hf:SLOTS * (hf + 1), t * P:(t + 1) * P],
                                  yb[SLOTS * hf:SLOTS * (hf + 1), :], start=False, stop=False,
                                  skip_group_check=True)
                        if final:
                            last.then_inc(acc_done, 1)

            n_blocks = pe.value_load(nbl[0:1, MAXB:MAXB + 1], min_val=N_EXP, max_val=NB_MAX)

            def gate_up(b, odd):
                pe.wait_ge(xgT_ready, b + 1)
                pe.wait_ge(oh_ready, b + 1)
                order = [(bank[4], 0, 0), (bank[4], 1, 512), (bank[5], 0, 1024), (bank[5], 1, 1536)]
                for dst, hf, c0 in order:
                    mm(dst[SLOTS * hf:SLOTS * (hf + 1), :], oh_cur, bgu[:, c0:c0 + 512], start=True, stop=False)
                for k in range(KT):
                    pe.wait_ge(ld_slot[k], 16 * (b + 1))
                    c = (k % 4) * P + (k // 4) * SLOTS
                    for dst, hf, c0 in order:
                        last = mm(dst[SLOTS * hf:SLOTS * (hf + 1), :], xgT[:, c:c + SLOTS],
                                  store[:, slot_at(k, odd) + c0:slot_at(k, odd) + c0 + 512], start=False, stop=k == KT - 1)
                    last.then_inc(wgu_used, 1)

            def rest(b):
                pe.wait_ge(SG_ready, b + 1)
                for t in range(T):
                    last = tp(bank[7][:, t * P:(t + 1) * P], SG[:, t, :], ident[:])
                last.then_inc(SGT_psum, 1)
                pe.wait_ge(S_ready, b + 2)
                gather()
                pe.wait_ge(act_ready, b + 1)
                for c in range(4):
                    last = tp(bank[4][:, c * P:(c + 1) * P], up[:, c * P:(c + 1) * P], ident[:])
                last.then_inc(actT_psum, 1)
                pe.wait_ge(xg_ready, b + 2)
                gather_flip()
                pe.wait_ge(actT_ready, b + 1)
                pe.wait_ge(SGT_ready, b + 1)
                for f in range(KT):
                    if f % 2 == 0:
                        pe.wait_ge(ld_slot[8 + f // 2], 16 * (b + 1))
                    w = store[:, slot_at(8) + f * D:slot_at(8) + (f + 1) * D]
                    c = (f % 4) * P + (f // 4) * SLOTS
                    for hf in range(2):
                        last = mm(bank[7][SLOTS * hf:SLOTS * (hf + 1), :], actT[:, c:c + SLOTS],
                                  w[:, hf * 512:(hf + 1) * 512], start=f == 0, stop=f == KT - 1)
                    if f % 2:
                        last.then_inc(wdn_used, 1)

            pe.wait_ge(zeroed, 2)

            def expert_block(b, odd):
                gate_up(b, odd)
                pe.wait_ge(y_ready, b + 1)
                combine()
                rest(b)

            with pe.Fori(0, n_blocks >> 1) as pair:
                expert_block(2 * pair, 0)
                expert_block(2 * pair + 1, 1)
            with pe.If(n_blocks & 1):
                expert_block(n_blocks - 1, 0)
            pe.wait_ge(y_ready, n_blocks + 1)
            combine(final=True)


_INS = ["x", "norm1_w", "w_in", "conv_w", "a_log", "dt_bias", "gdn_norm_w", "q_norm_w", "k_norm_w", "rel_bias",
        "w_out", "norm2_w", "w_router", "b_router", "w_gate_up", "b_gate_up", "w_down", "b_down"]


def kernel(**inputs):
    import numpy as _np
    import concourse.bacc as _bacc
    from concourse import mybir as _mybir
    from concourse.bass_utils import run_bass_kernel_spmd as _run

    nc = _bacc.Bacc("TRN2", target_bir_lowering=False, num_devices=1)
    arrays, args = {}, []
    for name in _INS + ["dist_table"]:
        a = distance_table(inputs["x"].shape[1]) if name == "dist_table" else inputs[name]
        a = _np.ascontiguousarray(a)
        arrays[f"in_{name}_dram"] = a
        args.append(nc.dram_tensor(f"in_{name}_dram", a.shape, _mybir.dt.from_np(a.dtype), kind="ExternalInput").ap())
    shape = inputs["x"].shape
    args.append(nc.dram_tensor("out_dram", shape, _mybir.dt.float32, kind="ExternalOutput").ap())
    hybrid_layer(nc, *args)
    r = _run(nc, [arrays], core_ids=[0])
    return r.results[0]["out_dram"]
```
